# Optimizing a Trainium2 kernel written in Bass

```python
import jax
import jax.numpy as jnp
from jax import lax
import numpy as np

D_MODEL = 1024
BATCH = 1
SEQ = 512
DEPTH = 2

CTX_LEN = 256
GRID_W = 64
D_MIX = D_MODEL
ML_HEADS = 4
ML_DV = D_MIX // (2 * ML_HEADS)
ML_DK = ML_DV // 2
ML_CHUNK = 64
CONV_W = 5
NA_HEADS = 8
NA_DH = (D_MIX - ML_HEADS * ML_DV) // NA_HEADS
NA_WIN_H = 8
NA_WIN_W = 16
NA_QB = 16
NA_BAND_W = 2 * NA_WIN_W
ROPE_BASE = 10000.0
PEER_HEADS = 8
PEER_NKEYS = 128
PEER_EXPERTS = PEER_NKEYS * PEER_NKEYS
PEER_TOPK = 16
PEER_DKEY = 256
PEER_TB = 128
N_MOD = 6
ML_QK_W = 2 * ML_HEADS * ML_DK
ML_V_W = ML_HEADS * ML_DV
ML_G_W = 4 * ML_HEADS
NA_W = NA_HEADS * NA_DH
D_IN = ML_QK_W + 2 * ML_V_W + ML_G_W + 3 * NA_W
DEEPNORM_ALPHA = (2.0 * DEPTH) ** 0.25
DEEPNORM_BETA = (8.0 * DEPTH) ** -0.25
LN_EPS = 1e-5

kernel_name = 'hybrid_mlstm_natten_peer_dit'

def _layer_norm(x, w, b):
    xf = x.astype(jnp.float32)
    mu = xf.mean(-1, keepdims=True)
    var = jnp.square(xf - mu).mean(-1, keepdims=True)
    return ((xf - mu) * lax.rsqrt(var + LN_EPS) * w + b).astype(x.dtype)

def _modulation(cond, w, b):
    return jnp.split(jax.nn.silu(cond) @ w + b, N_MOD, axis=-1)

def _heads(t, h):
    return t.reshape(t.shape[0], t.shape[1], h, -1).transpose(0, 2, 1, 3)

def _merge_heads(t):
    return t.transpose(0, 2, 1, 3).reshape(t.shape[0], t.shape[2], -1)

def _split_in(p):
    sizes = (ML_QK_W, ML_V_W, ML_V_W, ML_G_W, NA_W, NA_W, NA_W)
    offs = [0]
    for s in sizes:
        offs.append(offs[-1] + s)
    return [p[..., a:b] for a, b in zip(offs[:-1], offs[1:])]

def _centred_dwconv(x, w):
    return lax.conv_general_dilated(
        x, w[:, None, :].astype(x.dtype), window_strides=(1,),
        padding=[(CONV_W // 2, CONV_W // 2)],
        dimension_numbers=('NWC', 'WIO', 'NWC'), feature_group_count=x.shape[-1])

def _axial_rope(t):
    T, d = t.shape[2], t.shape[-1]
    pos = jnp.arange(T)
    n_freq = d // 4
    inv = ROPE_BASE ** (-jnp.arange(n_freq, dtype=jnp.float32) / n_freq)
    ang = jnp.concatenate([(pos // GRID_W)[:, None] * inv, (pos % GRID_W)[:, None] * inv], -1)
    cos, sin = jnp.cos(ang), jnp.sin(ang)
    t1, t2 = t[..., : d // 2], t[..., d // 2:]
    return jnp.concatenate([t1 * cos - t2 * sin, t1 * sin + t2 * cos], -1).astype(t.dtype)

def _chunked(t):
    return t.reshape(t.shape[:2] + (t.shape[2] // ML_CHUNK, ML_CHUNK) + t.shape[3:])

def _mlstm_states(k, v, log_i, log_f, state):
    kc, vc = _chunked(k), _chunked(v)
    li, lf = _chunked(log_i), _chunked(log_f)
    b = jnp.cumsum(lf, axis=-1)
    b_last = b[..., -1]
    a = b_last[..., None] - b + li
    m_loc = a.max(-1)
    w = jnp.exp(a - m_loc[..., None])
    c_loc = jnp.einsum('bhcs,bhcsv,bhcsk->bhcvk', w, vc, kc)
    n_loc = jnp.einsum('bhcs,bhcsk->bhck', w, kc)

    def step(carry, xs):
        C, n, m = carry
        C_l, n_l, m_l, bl = xs
        m_new = jnp.maximum(bl + m, m_l)
        s_old = jnp.exp(bl + m - m_new)
        s_loc = jnp.exp(m_l - m_new)
        C_new = s_old[..., None, None] * C + s_loc[..., None, None] * C_l
        n_new = s_old[..., None] * n + s_loc[..., None] * n_l
        return (C_new, n_new, m_new), (C, n, m)

    front = lambda t: jnp.moveaxis(t, 2, 0)
    final, (c_in, n_in, m_in) = lax.scan(step, state, (front(c_loc), front(n_loc), front(m_loc), front(b_last)))
    back = lambda t: jnp.moveaxis(t, 0, 2)
    return (back(c_in), back(n_in), back(m_in)), final

def _mlstm_outputs(q, k, v, log_i, log_f, incoming):
    c_in, n_in, m_in = incoming
    qc, kc, vc = _chunked(q), _chunked(k), _chunked(v)
    li, lf = _chunked(log_i), _chunked(log_f)
    b = jnp.cumsum(lf, axis=-1)
    dmat = b[..., :, None] - b[..., None, :] + li[..., None, :]
    lower = jnp.tril(jnp.ones((ML_CHUNK, ML_CHUNK), bool))
    dmat = jnp.where(lower, dmat, -jnp.inf)
    m_inter = b + m_in[..., None]
    m_j = jnp.maximum(m_inter, dmat.max(-1))
    s = jnp.einsum('bhcjk,bhcsk->bhcjs', qc, kc) * jnp.exp(dmat - m_j[..., None])
    inter = jnp.exp(m_inter - m_j)
    num = jnp.einsum('bhcjs,bhcsv->bhcjv', s, vc) + inter[..., None] * jnp.einsum('bhcvk,bhcjk->bhcjv', c_in, qc)
    den = s.sum(-1) + inter * jnp.einsum('bhck,bhcjk->bhcj', n_in, qc)
    h = num / jnp.maximum(jnp.abs(den), jnp.exp(-m_j))[..., None]
    return h.reshape(h.shape[:2] + (-1, h.shape[-1]))

def _mlstm_bidir(qx, kx, vx, gx, qc, kc, vc, gc, need_ctx):
    B_ = qx.shape[0]
    f32 = jnp.float32
    zero = (jnp.zeros((B_, ML_HEADS, ML_DV, ML_DK), f32), jnp.zeros((B_, ML_HEADS, ML_DK), f32),
            jnp.zeros((B_, ML_HEADS), f32))
    hx, hc = [], []
    for d in range(2):
        o = (lambda t: t) if d == 0 else (lambda t: jnp.flip(t, axis=2))
        li_c, lf_c = o(gc[2 * d]), o(jax.nn.log_sigmoid(gc[2 * d + 1]))
        li_x, lf_x = o(gx[2 * d]), o(jax.nn.log_sigmoid(gx[2 * d + 1]))
        inc_c, final_c = _mlstm_states(o(kc), o(vc), li_c, lf_c, zero)
        inc_x, _ = _mlstm_states(o(kx), o(vx), li_x, lf_x, final_c)
        hx.append(o(_mlstm_outputs(o(qx), o(kx), o(vx), li_x, lf_x, inc_x)))
        if need_ctx:
            hc.append(o(_mlstm_outputs(o(qc), o(kc), o(vc), li_c, lf_c, inc_c)))
    return hx[0] + hx[1], (hc[0] + hc[1] if need_ctx else None)

def _head_norm(h, w):
    mu = h.mean(-1, keepdims=True)
    var = jnp.square(h - mu).mean(-1, keepdims=True)
    return _merge_heads((h - mu) * lax.rsqrt(var + LN_EPS)) * w

def _neighbourhood_attention(qx, kx, vx, qc, kc, vc, rpb, need_ctx):
    B_, T, _ = qx.shape
    rows = T // GRID_W
    kh = min(NA_WIN_H, rows)
    scale = NA_DH ** -0.5
    grid = lambda t: t.reshape(B_, rows, GRID_W, NA_HEADS, NA_DH).transpose(0, 3, 1, 2, 4)
    qg, kg, vg = grid(qx * scale), grid(kx), grid(vx)
    qh_c, kh_c, vh_c = _heads(qc * scale, NA_HEADS), _heads(kc, NA_HEADS), _heads(vc, NA_HEADS)
    n_cb = GRID_W // NA_QB
    q_cols = np.arange(GRID_W).reshape(n_cb, NA_QB)
    band_cols = np.clip(q_cols[:, :1] - NA_WIN_W // 2, 0, GRID_W - NA_BAND_W) + np.arange(NA_BAND_W)
    win_lo = np.clip(q_cols - NA_WIN_W // 2, 0, GRID_W - NA_WIN_W)[..., None]
    col_ok = (band_cols[:, None, :] >= win_lo) & (band_cols[:, None, :] < win_lo + NA_WIN_W)
    col_idx = np.clip(band_cols[:, None, :] - q_cols[..., None], 1 - NA_WIN_W, NA_WIN_W - 1) + NA_WIN_W - 1
    n_loc = kh * NA_BAND_W

    def row_block(r):
        r0 = jnp.clip(r - kh // 2, 0, rows - kh)
        k_band = lax.dynamic_slice_in_dim(kg, r0, kh, axis=2)[:, :, :, band_cols]
        v_band = lax.dynamic_slice_in_dim(vg, r0, kh, axis=2)[:, :, :, band_cols]
        q_blk = lax.dynamic_index_in_dim(qg, r, axis=2, keepdims=False).reshape(B_, NA_HEADS, n_cb, NA_QB, NA_DH)
        row_idx = r0 + jnp.arange(kh) - r + NA_WIN_H - 1
        bias = rpb[:, row_idx[None, None, :, None], col_idx[:, :, None, :]]
        s_loc = jnp.einsum('bhcqd,bhicjd->bhcqij', q_blk, k_band).astype(jnp.float32) + bias
        s_loc = jnp.where(col_ok[:, :, None, :], s_loc, -jnp.inf)
        s_ctx = jnp.einsum('bhcqd,bhnd->bhcqn', q_blk, kh_c).astype(jnp.float32)
        p = jax.nn.softmax(jnp.concatenate([s_loc.reshape(s_loc.shape[:4] + (n_loc,)), s_ctx], -1), axis=-1)
        p = p.astype(vx.dtype)
        out = (jnp.einsum('bhcqij,bhicjd->bhcqd', p[..., :n_loc].reshape(s_loc.shape), v_band)
               + jnp.einsum('bhcqn,bhnd->bhcqd', p[..., n_loc:], vh_c))
        return out.reshape(B_, NA_HEADS, GRID_W, NA_DH)

    out = lax.map(row_block, jnp.arange(rows))
    yx = out.transpose(1, 0, 3, 2, 4).reshape(B_, T, NA_W)
    yc = None
    if need_ctx:
        pc = jax.nn.softmax(jnp.einsum('bhnd,bhmd->bhnm', qh_c, kh_c).astype(jnp.float32), axis=-1)
        yc = _merge_heads(jnp.einsum('bhnm,bhmd->bhnd', pc.astype(vc.dtype), vh_c))
    return yx, yc

def _hybrid_mixer(ux, uc, w_in, b_gate, conv_w, ml_norm_w, rpb, w_out, need_ctx):
    f32 = jnp.float32
    px, pc = ux @ w_in, uc @ w_in

    def prep(p, rope):
        qk, v, o, g, nq, nk, nv = _split_in(p)
        qk = jax.nn.silu(_centred_dwconv(qk, conv_w)).astype(f32)
        q = _heads(qk[..., : ML_QK_W // 2], ML_HEADS)
        k = _heads(qk[..., ML_QK_W // 2:], ML_HEADS) * ML_DK ** -0.5
        if rope:
            q, k = _axial_rope(q), _axial_rope(k)
        gates = (g.astype(f32) + b_gate).reshape(g.shape[:2] + (4, ML_HEADS)).transpose(2, 0, 3, 1)
        return q, k, _heads(v.astype(f32), ML_HEADS), o, gates, nq, nk, nv

    qx, kx, vx, ox, gx, nqx, nkx, nvx = prep(px, True)
    qc, kc, vc, oc, gc, nqc, nkc, nvc = prep(pc, False)
    hx, hc = _mlstm_bidir(qx, kx, vx, gx, qc, kc, vc, gc, need_ctx)
    ml_x = (_head_norm(hx, ml_norm_w) * jax.nn.sigmoid(ox.astype(f32))).astype(ux.dtype)
    na_x, na_c = _neighbourhood_attention(nqx, nkx, nvx, nqc, nkc, nvc, rpb, need_ctx)
    yx = jnp.concatenate([ml_x, na_x], -1) @ w_out
    yc = None
    if need_ctx:
        ml_c = (_head_norm(hc, ml_norm_w) * jax.nn.sigmoid(oc.astype(f32))).astype(uc.dtype)
        yc = jnp.concatenate([ml_c, na_c], -1) @ w_out
    return yx, yc

def _peer(u, wq, sub_keys, up, down):
    B_, T, D = u.shape

    def block(ub):
        tb = ub.shape[0]
        q = (ub @ wq).reshape(tb, PEER_HEADS, 2, PEER_DKEY // 2)
        s1 = jnp.einsum('thd,hnd->thn', q[:, :, 0], sub_keys[:, 0])
        s2 = jnp.einsum('thd,hnd->thn', q[:, :, 1], sub_keys[:, 1])
        t1, i1 = lax.top_k(s1, PEER_TOPK)
        t2, i2 = lax.top_k(s2, PEER_TOPK)
        cand = (t1[..., :, None] + t2[..., None, :]).reshape(tb, PEER_HEADS, PEER_TOPK * PEER_TOPK)
        cidx = (i1[..., :, None] * PEER_NKEYS + i2[..., None, :]).reshape(tb, PEER_HEADS, PEER_TOPK * PEER_TOPK)
        top, pos = lax.top_k(cand, PEER_TOPK)
        eidx = jnp.take_along_axis(cidx, pos, -1).reshape(tb, PEER_HEADS * PEER_TOPK)
        g = jax.nn.softmax(top.astype(jnp.float32), axis=-1).reshape(tb, -1).astype(ub.dtype)
        act = jax.nn.gelu(jnp.einsum('td,tkd->tk', ub, up[eidx]))
        return jnp.einsum('tk,tkd->td', g * act, down[eidx])

    y = lax.map(block, u.reshape(B_ * T // PEER_TB, PEER_TB, D))
    return y.reshape(B_, T, D)

def setup_inputs(seed: int = 0) -> dict:
    key = jax.random.key(seed)
    ks = jax.random.split(key, 20)
    f32 = jnp.float32

    def nrm(k, shape, scale):
        return scale * jax.random.normal(k, shape, f32)

    L = DEPTH
    gate_base = jnp.repeat(jnp.array([0.0, 3.0, 0.0, 3.0], f32), ML_HEADS)
    return {
        'x': nrm(ks[0], (BATCH, SEQ, D_MODEL), 1.0),
        'c': nrm(ks[1], (BATCH, D_MODEL), 1.0),
        'ctx': nrm(ks[2], (BATCH, CTX_LEN, D_MODEL), 1.0),
        'c_ctx': nrm(ks[3], (D_MODEL,), 1.0),
        'ada_w': nrm(ks[4], (L, D_MODEL, N_MOD * D_MODEL), D_MODEL ** -0.5),
        'ada_b': nrm(ks[5], (L, N_MOD * D_MODEL), 0.02),
        'w_in': nrm(ks[6], (L, D_MODEL, D_IN), D_MODEL ** -0.5),
        'b_gate': gate_base + nrm(ks[7], (L, ML_G_W), 0.1),
        'conv_w': nrm(ks[8], (L, CONV_W, ML_QK_W), CONV_W ** -0.5),
        'ml_norm_w': 1.0 + nrm(ks[9], (L, ML_V_W), 0.1),
        'na_rpb': nrm(ks[10], (L, NA_HEADS, 2 * NA_WIN_H - 1, 2 * NA_WIN_W - 1), 0.1),
        'w_out': nrm(ks[11], (L, D_MIX, D_MODEL), DEEPNORM_BETA * D_MIX ** -0.5),
        'ln1_w': 1.0 + nrm(ks[12], (L, D_MODEL), 0.1),
        'ln1_b': nrm(ks[13], (L, D_MODEL), 0.02),
        'peer_wq': nrm(ks[14], (L, D_MODEL, PEER_HEADS * PEER_DKEY), D_MODEL ** -0.5),
        'peer_keys': nrm(ks[15], (L, PEER_HEADS, 2, PEER_NKEYS, PEER_DKEY // 2), (PEER_DKEY // 2) ** -0.5),
        'peer_up': nrm(ks[16], (L, PEER_EXPERTS, D_MODEL), D_MODEL ** -0.5),
        'peer_down': nrm(ks[17], (L, PEER_EXPERTS, D_MODEL), DEEPNORM_BETA),
        'ln2_w': 1.0 + nrm(ks[18], (L, D_MODEL), 0.1),
        'ln2_b': nrm(ks[19], (L, D_MODEL), 0.02),
    }

def reference(x, c, ctx, c_ctx, ada_w, ada_b, w_in, b_gate, conv_w, ml_norm_w, na_rpb, w_out,
              ln1_w, ln1_b, peer_wq, peer_keys, peer_up, peer_down, ln2_w, ln2_b):
    for l in range(DEPTH):
        need_ctx = l < DEPTH - 1
        sh1, sc1, g1, sh2, sc2, g2 = _modulation(c[:, None, :], ada_w[l], ada_b[l])
        csh1, csc1, cg1, csh2, csc2, cg2 = _modulation(c_ctx[None, None, :], ada_w[l], ada_b[l])
        ux = x * (1.0 + sc1) + sh1
        uc = ctx * (1.0 + csc1) + csh1
        yx, yc = _hybrid_mixer(ux, uc, w_in[l], b_gate[l], conv_w[l], ml_norm_w[l], na_rpb[l], w_out[l], need_ctx)
        x = _layer_norm(DEEPNORM_ALPHA * x + g1 * yx, ln1_w[l], ln1_b[l])
        fx = _peer(x * (1.0 + sc2) + sh2, peer_wq[l], peer_keys[l], peer_up[l], peer_down[l])
        x = _layer_norm(DEEPNORM_ALPHA * x + g2 * fx, ln2_w[l], ln2_b[l])
        if need_ctx:
            ctx = _layer_norm(DEEPNORM_ALPHA * ctx + cg1 * yc, ln1_w[l], ln1_b[l])
            fc = _peer(ctx * (1.0 + csc2) + csh2, peer_wq[l], peer_keys[l], peer_up[l], peer_down[l])
            ctx = _layer_norm(DEEPNORM_ALPHA * ctx + cg2 * fc, ln2_w[l], ln2_b[l])
    return x


_drawn_inputs = setup_inputs


def setup_inputs(seed=0):
    import zlib

    import numpy as np

    out = dict(_drawn_inputs(seed))
    spreads = {}
    factors = {'na_rpb': 4.967}
    for name, (base, spread) in spreads.items():
        noise = np.random.default_rng([zlib.crc32(name.encode()), seed]).standard_normal(out[name].shape)
        drawn = base * np.exp(spread * noise) if base else spread * noise
        out[name] = jnp.asarray(drawn.astype(out[name].dtype))
    for name, factor in factors.items():
        out[name] = (out[name] * factor).astype(out[name].dtype)
    return out
```

```python
from contextlib import ExitStack

import numpy as np
import concourse.bass as bass
from concourse import mybir

F32 = mybir.dt.float32
U32 = mybir.dt.uint32
ALU = mybir.AluOpType
ACT = mybir.ActivationFunctionType
AX = mybir.AxisListType

P = 128
D = 1024
KD = D // P
L = 2
CTX, SEQ = 256, 512
NT, NCT = (CTX + SEQ) // P, CTX // P
T = CTX + SEQ
GRID_W = 64
ROWS = SEQ // GRID_W
MLH, DV, DK = 4, 128, 64
NAH, DH = 8, 64
QB, BAND, WIN = 16, 32, 16
NBAND = GRID_W // QB
BAND_LO = [min(max(b * QB - WIN // 2, 0), GRID_W - BAND) for b in range(NBAND)]
LOC = ROWS * BAND
N_MOD = 6
SH1, SC1, G1, SH2, SC2, G2 = range(N_MOD)
D_IN = 3088
COL_ML, COL_V, COL_O, COL_G, COL_NQ, COL_NK, COL_NV = 0, 512, 1024, 1536, 1552, 2064, 2576
PH, NKEY, TOPK = 8, 128, 16
NEXP = NKEY * NKEY
ALPHA = (2.0 * L) ** 0.25
EPS = 1e-5
LOWEST = -3.0e38
MASKED = -1.0e30
RING = 8

C_ID, C_ROT, C_TRI, C_IOTA, C_MASK, C_COS, C_SIN, C_END = 0, 128, 256, 512, 528, 1552, 2064, 2576


def shape_constants():
    c = np.zeros((P, C_END), np.float32)
    p = np.arange(P)
    c[:, C_ID:C_ID + P] = np.eye(P)
    for m in range(P):
        if m % DK < DK // 2:
            c[m + DK // 2, C_ROT + m] = -1.0
        else:
            c[m - DK // 2, C_ROT + m] = 1.0
    c[:, C_TRI:C_TRI + P] = p[:, None] <= p[None, :]
    c[:, C_TRI + P:C_TRI + 2 * P] = p[:, None] >= p[None, :]
    c[:, C_IOTA:C_IOTA + TOPK] = np.arange(TOPK)
    for b in range(NBAND):
        q = b * QB + p % QB
        lo = np.clip(q - WIN // 2, 0, GRID_W - WIN)
        k = BAND_LO[b] + np.arange(BAND)
        ok = (k[None] >= lo[:, None]) & (k[None] < lo[:, None] + WIN)
        c[:, C_MASK + b * LOC:C_MASK + (b + 1) * LOC] = np.tile(np.where(ok, 0.0, MASKED), (1, ROWS))
    pos, nf = np.arange(SEQ), DK // 4
    inv = np.float32(10000.0) ** (-np.arange(nf, dtype=np.float32) / nf)
    ang = np.concatenate([(pos // GRID_W)[:, None] * inv, (pos % GRID_W)[:, None] * inv], -1).astype(np.float32)
    c[:, C_COS:C_COS + SEQ] = np.cos(ang).T[p % (DK // 2)]
    c[:, C_SIN:C_SIN + SEQ] = np.sin(ang).T[p % (DK // 2)]
    return c


class Chain:

    def __init__(self, eng, sem, token=None):
        self.eng, self.sem, self.token, self.n = eng, sem, token, 0

    def link(self, ins):
        self.n += 1
        ins.then_inc(self.sem, 1)
        self.eng.wait_ge(self.sem, self.n)
        return ins

    def restart(self):
        self.eng.sem_inc(self.token, 1)
        self.eng.sem_clear(self.sem)
        self.n = 0


def proj_jobs(l):
    q_ctx = l < L - 1
    jobs = []
    for k in range(KD):
        jobs += [("T", k, "x", "v"), ("T", k, "c", "a")]
    for g in range(2):
        jobs += [("G", g, "x", "a"), ("G", g, "c", "a")]

    def ml(c):
        out = [("M", c, "x", "a")]
        if q_ctx or c >= 2:
            out.append(("M", c, "c", "a"))
        return out
    jobs += ml(0) + ml(1) + [("X", 0, "x", "v")] + ml(2) + [("R", 0, "x", "v")] + ml(3) + [("R", 1, "x", "v")]
    for kind in "QK":
        for c in range(4):
            jobs.append((kind, c, "x", "va"[c % 2]))
            if q_ctx or kind == "K":
                jobs.append((kind, c, "c", "av"[c % 2]))
            if kind == "Q" and c < 2:
                jobs.append(("R", 2 + c, "x", "v"))
    for t in range(NT):
        jobs.append(("V", t, "x", "va"[t % 2]))
    for t in range(0 if q_ctx else NCT, NT):
        jobs.append(("O", t, "x", "a"))
    for n in range(2 * NBAND + NCT):
        jobs.append(("B", n, "x", "v"))
    return jobs


def f_start(i, t0):
    return max(i, t0)


OFF_F = [sum(6 - m for m in range(i)) * P for i in range(6)]
OFF_B = [0, 5 * P, 11 * P, 12 * P, 14 * P, 17 * P]
N_BLK = 21 * P


def at_f(i, j):
    return OFF_F[i] + (j - i) * P


def at_b(i, j):
    if i < NCT:
        return OFF_B[i] + ((j - NCT) * P if j >= NCT else 4 * P + j * P)
    return OFF_B[i] + (j - NCT) * P


def b_sources(j):
    return list(range(j, NCT)) if j < NCT else [0, 1] + list(range(j, NT))


def b_len(i, t0):
    if i < NCT:
        return SEQ + ((i + 1) * P if t0 == 0 else 0)
    return (i - 1) * P


def segments(l):
    return [(0, 0, NCT), (1, NCT, NT)] if l < L - 1 else [(1, NCT, NT)]


def units_before(l, sg):
    every = [(a, b) for a in range(L) for b in range(len(segments(a)))]
    return PH * sum(segments(a)[b][2] - segments(a)[b][1] for a, b in every[:every.index((l, sg))])


def attention_jobs(l):
    return [(b, h) for b in range(NBAND + (NCT if l < L - 1 else 0)) for h in range(NAH)]


def last_job(jobs, kind):
    return max(n for n, j in enumerate(jobs) if j[0] == kind) + 1


def chunk_end(jobs, c):
    kind, i = "MQK"[c // 4], c % 4
    return max(n for n, j in enumerate(jobs) if j[:2] == (kind, i)) + 1


def ordinals(jobs):
    count, out = {"v": 0, "a": 0}, []
    for j in jobs:
        count[j[3]] += 1
        out.append(count[j[3]])
    return out


def build(nc, xin, cT, consts, ada_w, ada_b, w_in, wg, bg, convw, ml_norm_w, bias, w_out, ln1, wq, keysT,
          updown, ln2, mod_d, negm_d, out):
    with ExitStack() as ctx:
        def sb(name, shape, dt=F32):
            return ctx.enter_context(nc.sbuf_tensor(name, shape, dt))

        X = sb("X", [P, NT, D])
        CN = sb("CN", [P, C_END])
        modcol = sb("modcol", [P, L, N_MOD * KD, 2])
        sT = sb("sT", [P, KD, 2])
        epsc = sb("epsc", [P, 1])
        ARENA_W = 43800
        arena = sb("arena", [P, ARENA_W])
        ident = CN[:, C_ID:C_ID + P]
        rot = CN[:, C_ROT:C_ROT + P]
        iota = CN[:, C_IOTA:C_IOTA + TOPK]

        class Region:

            def __init__(self, at=0):
                self.at = at

            def __call__(self, *shape):
                n = int(np.prod(shape))
                v = arena[:, self.at:self.at + n]
                self.at += n
                assert self.at <= ARENA_W, self.at
                if len(shape) == 2:
                    return v.rearrange("p (a b) -> p a b", a=shape[0])
                if len(shape) == 3:
                    return v.rearrange("p (a b c) -> p a b c", a=shape[0], b=shape[1])
                return v

        r = Region()
        adaw = r(3, KD, 512)
        adab = r(L * N_MOD * D)
        modrow = r(L * N_MOD * D)
        r = Region()
        mlqk = r(4, T)
        nq = r(4, T)
        nk = r(4, T)
        vband_at = r.at
        vband = r(2 * NBAND + NCT, 512)
        vml_at = r.at
        vml = r(NT, MLH, DV + 1)
        sigo_at = r.at
        sigo = r(NT, 512)
        gcol = r(4 * NT * 8)
        mixer_top = r.at
        r = Region(mixer_top)
        uT = r(KD, T)
        ubT = r(2, KD, P)
        wch = r(3, KD, P)
        wtok_at = r.at
        wtok = r(2, KD, 512)
        wgs = r(KD, 16)
        convs = r(4, 5)
        bgs = r(2)
        r = Region(sigo_at)
        raw = r(2, 776)
        ysil = r(2, 512)
        assert r.at <= sigo_at + NT * 512
        r = Region(vml_at)
        cvs = r(2, 776)
        rt = r(2, 512)
        assert r.at <= vml_at + NT * MLH * (DV + 1)
        r = Region(wtok_at + KD * 512)
        li, lf, lnl, cum = [r(T)[0:8, :] for _ in range(4)]
        r = Region(vband_at)
        gF, gB, eF, eB, nMf, nMb = [r(T)[0:8, :] for _ in range(6)]
        r = Region(mixer_top)
        mixT = r(KD, T)
        H = r(NT, 512)
        stat = r(NT * MLH, 2)
        rstd = r(NT * MLH)
        bns = r(4, 6)
        den = r(2, 2)
        rden = r(2, 2)
        nwrow = r(512)
        heads_top = r.at
        negm = r(2, 2, T)
        WD = r(2, N_BLK)
        biasb = r(2, 4, LOC)
        prob = r(2, 512)
        probT = r(2, 512)
        nmax = r(2)
        rsum = r(2)
        rinv = r(2)
        r = Region()
        wo = r(KD, D)
        g1r = r(2, D)
        ln1r = r(2, D)
        tmp = r(2, D)
        lns = r(2, 2, 6)
        mv = r(2)
        sd = r(2)
        r = Region()
        qT = r(2 * PH, T)
        peer_top = r.at
        puT = r(KD, T)
        wqs = r(3, KD, P)
        r = Region(peer_top)
        ring = r(RING, 2 * D)
        keys = r(2 * PH, NKEY)
        u = r(D)
        sc2r, sh2r, g2r = r(D), r(D), r(D)
        ln2r = r(2, D)
        junk = r(D)
        prod = r(2, D)
        diag = r(2, P)
        qs = r(2, P)
        zero = r(P)
        idx16 = r(TOPK).bitcast(U32)
        sc = r(2, NKEY)
        tv = r(2, TOPK)
        ti = r(2, TOPK).bitcast(U32)
        cand = r(256)
        cand2 = r(256)
        tt = r(TOPK)
        pos = r(TOPK).bitcast(U32)
        hilo = r(2, TOPK).bitcast(U32)
        oh = r(256)
        e1 = r(2, TOPK)
        eidx_all = r((NT + 1) * PH * TOPK).bitcast(U32)
        gate_all = r((NT + 1) * PH * TOPK)
        gsum = r(PH)
        dots = r(TOPK)
        acts = r(TOPK)
        lns2 = r(2, 6)
        mv2 = r(2)
        sd2 = r(2)

        ps = [ctx.enter_context(nc.psum_tensor(f"ps{i}", [P, 512], F32)) for i in range(8)]

        sems = {}

        def sem(name):
            if name not in sems:
                sems[name] = ctx.enter_context(nc.semaphore(name))
            return sems[name]

        barrier = sem("stage_barrier")
        bar_n = {}

        def meet(e, who):
            bar_n[who] = bar_n.get(who, 0) + 1
            e.drain()
            e.sem_inc(barrier, 1)
            e.wait_ge(barrier, 5 * bar_n[who])
            e.sem_inc(sem("stage_passed"), 1)

        def reset(e, who, scope, ch=None):
            if who == "dve":
                for name, x in sems.items():
                    if name.startswith(scope):
                        ins = e.sem_clear(x)
                ch.link(ins)
            meet(e, who)

        block = ctx.enter_context(nc.Block())
        cond_of = [0] * NCT + [1] * (NT - NCT)
        mod_v = modrow.rearrange("p (l n) -> p l n", l=L)

        @block.sync
        def _(e):
            e.dma_start(sT[:], cT).then_inc(sem("c_loaded"), 16)
            e.dma_start(adab[0:2, :], ada_b.rearrange("(o l) n -> o (l n)", o=1).to_broadcast([2, L * N_MOD * D])).then_inc(sem("adab_loaded"), 16)
            for n in range(24):
                if n >= 3:
                    e.wait_ge(sem("mod_mm"), n - 2)
                e.dma_start(adaw[:, n % 3], ada_w[n // 12].rearrange("(k p) n -> p k n", p=P)[:, :, (n % 12) * 512:(n % 12 + 1) * 512]).then_inc(sem(f"adaw_loaded{n % 3}"), 16)
                if n == 2:
                    e.dma_start(CN[:], consts).then_inc(sem("const_loaded"), 16)
                    e.dma_start(X[:], xin.rearrange("(t p) d -> p t d", p=P)).then_inc(sem("x_loaded"), 16)
            e.wait_ge(sem("mod_row"), 24)
            for l in range(L):
                e.dma_start(mod_d[l], mod_v[0:2, l, :]).then_inc(sem("mod_stored"), 16)
            e.wait_ge(sem("mod_stored"), 16 * L)
            e.wait_ge(sem("x_loaded"), 16)
            e.wait_ge(sem("const_loaded"), 16)
            meet(e, "sp")
            for l in range(L):
                jobs = proj_jobs(l)
                e.dma_start(wgs[:], wg[l]).then_inc(sem("L.small_loaded"), 16)
                e.dma_start(bgs[0:8, :], bg[l]).then_inc(sem("L.small_loaded"), 16)
                e.dma_start(convs[:], convw[l]).then_inc(sem("L.small_loaded"), 16)
                wv = w_in[l].rearrange("(k p) n -> p k n", p=P)
                chunks = [COL_ML + c * P for c in range(4)] + [COL_NQ + c * P for c in range(4)] + [COL_NK + c * P for c in range(4)]

                def load_tok(n):
                    col = (COL_V, COL_O, COL_NV)[n]
                    e.dma_start(wtok[:, n % 2], wv[:, :, col:col + 512]).then_inc(sem(f"L.wtok_loaded{n % 2}"), 16)
                load_tok(0)
                for n, col in enumerate(chunks):
                    if n >= 3:
                        e.wait_ge(sem("L.proj_mm"), chunk_end(jobs, n - 3))
                    e.dma_start(wch[:, n % 3], wv[:, :, col:col + P]).then_inc(sem(f"L.wch_loaded{n % 3}"), 16)
                    if n == 3:
                        e.wait_ge(sem("L.negm_ready"), 2)
                        e.dma_start(negm_d[l, 0], nMf[0:4, :]).then_inc(sem("L.negm_stored"), 16)
                        e.dma_start(negm_d[l, 1], nMb[4:8, :]).then_inc(sem("L.negm_stored"), 16)
                e.wait_ge(sem("L.negm_stored"), 32)
                e.wait_ge(sem("L.proj_mm"), last_job(jobs, "X"))
                load_tok(1)
                e.wait_ge(sem("L.proj_mm"), last_job(jobs, "V"))
                load_tok(2)
                meet(e, "sp")
                e.dma_start(nwrow, ml_norm_w[l:l + 1, :].to_broadcast([P, 512])).then_inc(sem("L.nw_loaded"), 16)
                for h in range(MLH):
                    if h >= 2:
                        e.wait_ge(sem("L.arg_ready"), (h - 1) * NT)
                    for d in range(2):
                        e.dma_start(negm[:, h % 2, d, :], negm_d[l, d, h:h + 1, :].to_broadcast([P, T])).then_inc(sem(f"L.negm_loaded{h % 2}"), 16)
                for n in range(2 * NBAND):
                    if n >= 2:
                        e.wait_ge(sem("L.bias_used"), 4 * (n - 1))
                    e.dma_start(biasb[:, n % 2], bias[l, n // 2][:, 4 * (n % 2):4 * (n % 2) + 4, :]).then_inc(sem(f"L.bias_loaded{n % 2}"), 16)
                meet(e, "sp")
                e.dma_start(wo[:], w_out[l].rearrange("(k p) n -> p k n", p=P)).then_inc(sem("L.wo_loaded"), 16)
                for cnd in range(2):
                    e.dma_start(g1r[:, cnd], mod_d[l, cnd:cnd + 1, G1 * D:(G1 + 1) * D].to_broadcast([P, D])).then_inc(sem("L.row1_loaded"), 16)
                e.dma_start(ln1r[:].rearrange("p a b -> p (a b)"), ln1[l:l + 1, :].to_broadcast([P, 2 * D])).then_inc(sem("L.row1_loaded"), 16)
                meet(e, "sp")
                for n in range(2 * PH):
                    if n >= 3:
                        e.wait_ge(sem("L.q_mm"), (n - 2) * (2 if l < L - 1 else 1))
                    e.dma_start(wqs[:, n % 3], wq[l].rearrange("(k p) n -> p k n", p=P)[:, :, n * P:(n + 1) * P]).then_inc(sem(f"L.wq_loaded{n % 3}"), 16)
                meet(e, "sp")
                for sg, (cnd, t0, t1) in enumerate(segments(l)):
                    e.dma_start(keys[:], keysT[l]).then_inc(sem("S.row2_loaded"), 16)
                    for row, v in ((sc2r, SC2), (sh2r, SH2), (g2r, G2)):
                        e.dma_start(row, mod_d[l, cnd:cnd + 1, v * D:(v + 1) * D].to_broadcast([P, D])).then_inc(sem("S.row2_loaded"), 16)
                    e.dma_start(ln2r[:].rearrange("p a b -> p (a b)"), ln2[l:l + 1, :].to_broadcast([P, 2 * D])).then_inc(sem("S.row2_loaded"), 16)
                    meet(e, "sp")
                    reset(e, "sp", "S.")
                reset(e, "sp", "L.")
            e.dma_start(out[0].rearrange("(t p) d -> p t d", p=P), X[:, NCT:NT, :]).then_inc(sem("out_stored"), 16)
            e.wait_ge(sem("out_stored"), 16)

        @block.tensor
        def _(e):
            e.wait_ge(sem("silu_c"), 1)
            for n in range(24):
                e.wait_ge(sem(f"adaw_loaded{n % 3}"), 16 * (n // 3 + 1))
                if n >= 4:
                    e.wait_ge(sem("mod_row"), n - 3)
                for k in range(KD):
                    mm = e.matmul(ps[n % 4][0:2, :], sT[:, k, :], adaw[:, n % 3, k, :], start=(k == 0), stop=(k == KD - 1))
                mm.then_inc(sem("mod_mm"), 1)
            e.wait_ge(sem("mod_row"), 24)
            e.wait_ge(sem("const_loaded"), 16)
            for l in range(L):
                for c in range(N_MOD * KD):
                    mm = e.transpose(ps[4 + l][:, 2 * c:2 * c + 2], mod_v[0:2, l, c * P:(c + 1) * P], ident[0:2, 0:2])
                mm.then_inc(sem("modcol_t"), 1)
            e.wait_ge(sem("x_loaded"), 16)
            meet(e, "pe")
            for l in range(L):
                q_ctx = l < L - 1
                t0 = 0 if q_ctx else NCT
                jobs = proj_jobs(l)
                count = {"v": 0, "a": 0}
                freed = []
                n_t = {"v": sum(j[0] == "T" and j[3] == "v" for j in jobs), "a": sum(j[0] == "T" and j[3] == "a" for j in jobs)}
                chunk_no = -1
                for n, (kind, i, part, ev) in enumerate(jobs):
                    if n >= 8:
                        w, val = freed[n - 8]
                        e.wait_ge(sem(f"L.proj_evac_{w}"), val)
                    count[ev] += 1
                    freed.append((ev, count[ev]))
                    bank = ps[n % 8]
                    cols = slice(CTX, T) if part == "x" else slice(0, CTX)
                    width = SEQ if part == "x" else CTX
                    if kind == "T":
                        tiles = range(NCT, NT) if part == "x" else range(NCT)
                        for a, t in enumerate(tiles):
                            mm = e.transpose(bank[:, a * P:(a + 1) * P], X[:, t, i * P:(i + 1) * P], ident)
                    elif kind == "G":
                        if i == 0 and part == "x":
                            e.wait_ge(sem("L.proj_evac_v"), n_t["v"])
                            e.wait_ge(sem("L.proj_evac_a"), n_t["a"])
                            e.wait_ge(sem("L.small_loaded"), 48)
                        for k in range(KD):
                            mm = e.matmul(bank[0:8, 0:width], wgs[:, k, 8 * i:8 * i + 8], uT[:, k, cols], start=(k == 0), stop=(k == KD - 1))
                    elif kind in "MQK":
                        c = i + {"M": 0, "Q": 4, "K": 8}[kind]
                        e.wait_ge(sem(f"L.wch_loaded{c % 3}"), 16 * (c // 3 + 1))
                        for k in range(KD):
                            mm = e.matmul(bank[:, 0:width], wch[:, c % 3, k, :], uT[:, k, cols], start=(k == 0), stop=(k == KD - 1))
                    elif kind == "R":
                        e.wait_ge(sem("L.silu_done"), i + 1)
                        mm = e.matmul(bank[:], rot, ysil[:, i % 2, :], start=True, stop=True)
                    elif kind == "X":
                        e.wait_ge(sem("L.gates_done"), 1)
                        for a, g in enumerate((gF, gB, eF, eB)):
                            for t in range(NT):
                                o = (a * NT + t) * 8
                                mm = e.transpose(bank[:, o:o + 8], g[:, t * P:(t + 1) * P], ident[0:8, 0:8])
                    elif kind in "VO":
                        s = "VO".index(kind)
                        if i == (0 if kind == "V" else t0):
                            e.wait_ge(sem(f"L.wtok_loaded{s}"), 16)
                        for k in range(KD):
                            mm = e.matmul(bank[:], uT[:, k, i * P:(i + 1) * P], wtok[:, s, k, :], start=(k == 0), stop=(k == KD - 1))
                    else:
                        if i == 0:
                            e.wait_ge(sem("L.wtok_loaded0"), 32)
                        if i < 2 * NBAND:
                            e.wait_ge(sem("L.band_ready"), i + 1)
                        for k in range(KD):
                            lhs = ubT[:, i % 2, k, :] if i < 2 * NBAND else uT[:, k, (i - 2 * NBAND) * P:(i - 2 * NBAND + 1) * P]
                            mm = e.matmul(bank[:], lhs, wtok[:, 0, k, :], start=(k == 0), stop=(k == KD - 1))
                    mm.then_inc(sem("L.proj_mm"), 1)
                meet(e, "pe")
                for h in range(MLH):
                    o = (h % 2) * DK
                    for i in range(NT):
                        m = h * NT + i
                        if m >= 2:
                            e.wait_ge(sem("L.w_ready"), m - 1)
                        kk = mlqk[o:o + DK, 2 + h // 2, i * P:(i + 1) * P]
                        mm = e.matmul(ps[m % 2][:], kk, mlqk[o:o + DK, h // 2, CTX:T], start=True, stop=True)
                        if i < NCT and q_ctx:
                            mm = e.matmul(ps[2 + m % 2][:, 0:CTX], kk, mlqk[o:o + DK, h // 2, 0:CTX], start=True, stop=True)
                        mm.then_inc(sem("L.s_ready"), 1)
                    e.wait_ge(sem("L.w_ready"), (h + 1) * NT)
                    for j in range(t0, NT):
                        m = h * (NT - t0) + j - t0
                        if m >= 2:
                            e.wait_ge(sem("L.h_done"), m - 1)
                        bank = ps[4 + m % 2]
                        for d, src, at in ((0, list(range(j + 1)), at_f), (1, b_sources(j), at_b)):
                            for i in src:
                                mm = e.matmul(bank[:, d * (DV + 1):(d + 1) * (DV + 1)], WD[:, d, at(i, j):at(i, j) + P],
                                              vml[:, i, h, :], start=(i == src[0]), stop=(i == src[-1]))
                        mm.then_inc(sem("L.num_ready"), 1)
                for t in range(t0, NT):
                    e.wait_ge(sem("L.mlout"), t - t0 + 1)
                    if t >= t0 + 2:
                        e.wait_ge(sem("L.mlT_evac"), t - t0 - 1)
                    for h in range(MLH):
                        mm = e.transpose(ps[6 + t % 2][:, h * P:(h + 1) * P], H[:, t, h * P:(h + 1) * P], ident)
                    mm.then_inc(sem("L.mlT"), 1)
                att = attention_jobs(l)

                def scores(n):
                    b, h = att[n]
                    if n == 0:
                        e.wait_ge(sem("L.w_ready"), MLH * NT)
                    if n >= 2:
                        e.wait_ge(sem("L.p_exp"), n - 1)
                    o, c = (h % 2) * DH, h // 2
                    q = nq[o:o + DH, c, CTX + b * P:CTX + (b + 1) * P] if b < NBAND else nq[o:o + DH, c, (b - NBAND) * P:(b - NBAND + 1) * P]
                    if b < NBAND:
                        kb = nk[o:o + DH, c, CTX:T].rearrange("p (r w) -> p r w", w=GRID_W)[:, :, BAND_LO[b]:BAND_LO[b] + BAND]
                        e.matmul(ps[n % 2][:, 0:LOC], q, kb, start=True, stop=True)
                    e.matmul(ps[n % 2][:, LOC:512], q, nk[o:o + DH, c, 0:CTX], start=True, stop=True).then_inc(sem("L.s_att"), 1)

                def turn(n):
                    e.wait_ge(sem("L.p_ready"), n + 1)
                    if n >= 2:
                        e.wait_ge(sem("L.pT_ready"), n - 1)
                    for a in range(0 if att[n][0] < NBAND else 2, 4):
                        mm = e.transpose(ps[2 + n % 2][:, a * P:(a + 1) * P], prob[:, n % 2, a * P:(a + 1) * P], ident)
                    mm.then_inc(sem("L.pT_mm"), 1)

                def values(n):
                    b, h = att[n]
                    e.wait_ge(sem("L.pT_ready"), n + 1)
                    if n == 0:
                        e.wait_ge(sem("L.h_done"), MLH * (NT - t0))
                    if n >= 2:
                        e.wait_ge(sem("L.o_att"), n - 1)
                    first = 0 if b < NBAND else 2
                    for a in range(first, 4):
                        vt = 2 * b + a if a < 2 else 2 * NBAND + a - 2
                        mm = e.matmul(ps[4 + n % 2][:, 0:P], vband[:, vt, (h // 2) * P:(h // 2 + 1) * P],
                                      probT[:, n % 2, a * P:(a + 1) * P], start=(a == first), stop=(a == 3))
                    mm.then_inc(sem("L.o_mm"), 1)
                for n in range(len(att) + 2):
                    if n < len(att):
                        scores(n)
                    if 1 <= n <= len(att):
                        turn(n - 1)
                    if n >= 2:
                        values(n - 2)
                meet(e, "pe")
                e.wait_ge(sem("L.wo_loaded"), 16)
                for t in range(t0, NT):
                    m = t - t0
                    if m >= 4:
                        e.wait_ge(sem("L.y_read"), m - 3)
                    for hf in range(2):
                        for k in range(KD):
                            mm = e.matmul(ps[2 * (m % 4) + hf][:], mixT[:, k, t * P:(t + 1) * P], wo[:, k, hf * 512:(hf + 1) * 512],
                                          start=(k == 0), stop=(k == KD - 1))
                    mm.then_inc(sem("L.y_ready"), 1)
                meet(e, "pe")
                n = 0
                for k in range(KD):
                    for part in range(0 if q_ctx else 1, 2):
                        if n >= 8:
                            e.wait_ge(sem("L.pu_evac"), n - 7)
                        for a, t in enumerate(range(NCT) if part == 0 else range(NCT, NT)):
                            mm = e.transpose(ps[n % 8][:, a * P:(a + 1) * P], X[:, t, k * P:(k + 1) * P], ident)
                        mm.then_inc(sem("L.pu_mm"), 1)
                        n += 1
                e.wait_ge(sem("L.pu_evac"), n)
                m = 0
                for c in range(2 * PH):
                    e.wait_ge(sem(f"L.wq_loaded{c % 3}"), 16 * (c // 3 + 1))
                    for part in range(0 if q_ctx else 1, 2):
                        if m >= 8:
                            e.wait_ge(sem("L.q_evac"), m - 7)
                        cols, width = (slice(0, CTX), CTX) if part == 0 else (slice(CTX, T), SEQ)
                        for k in range(KD):
                            mm = e.matmul(ps[m % 8][:, 0:width], wqs[:, c % 3, k, :], puT[:, k, cols], start=(k == 0), stop=(k == KD - 1))
                        mm.then_inc(sem("L.q_mm"), 1)
                        m += 1
                meet(e, "pe")
                for sg, (cnd, ta, tb) in enumerate(segments(l)):
                    nt = tb - ta
                    keys_flat = keys[:].rearrange("p a b -> p (a b)")

                    def key_scores(unit, h):
                        e.wait_ge(sem("S.qs_ready"), unit + 1)
                        e.sem_inc(sem("S.pe_token"), 1)
                        e.wait_ge(sem("S.route_read"), unit + 1)
                        for hf in range(2):
                            mm = e.matmul(ps[2][:, hf * NKEY:(hf + 1) * NKEY], qs[:, hf, :], keys_flat[:, bass.ds((2 * h + hf) * NKEY, NKEY)], start=True, stop=True)
                        mm.then_inc(sem("S.key_mm"), 1)

                    def weigh(n, k):
                        e.wait_ge(sem("S.diag_ready"), n + (k + 1))
                        for hf in range(2):
                            mm = e.matmul(ps[hf][:], diag[:, k % 2, :], ring[:, k % RING, D + hf * 512:D + (hf + 1) * 512],
                                          start=False, stop=False, skip_group_check=True)
                        mm.then_inc(sem("S.slot_done"), 1)

                    def tile(t, route):
                        e.wait_ge(sem("S.acc_free"), t + 1)
                        for hf in range(2):
                            e.matmul(ps[hf][:], zero, CN[:, C_COS:C_COS + 512], start=True, stop=False, skip_group_check=True)
                        with e.Fori(0, PH) as h:
                            if route:
                                key_scores(t * PH + h + PH, h)
                            for k in range(TOPK):
                                weigh(t * (PH * TOPK) + h * TOPK, k)
                        for hf in range(2):
                            mm = e.matmul(ps[hf][:], zero, CN[:, C_COS:C_COS + 512], start=False, stop=True, skip_group_check=True)
                        mm.then_inc(sem("S.acc_ready"), 1)

                    e.wait_ge(sem("S.row2_loaded"), 80)
                    e.wait_ge(sem("S.zero_set"), 2)
                    with e.Fori(0, PH) as h:
                        key_scores(h, h)
                    with e.Fori(0, nt - 1) as t:
                        tile(t, True)
                    tile(nt - 1, False)
                    meet(e, "pe")
                    reset(e, "pe", "S.")
                reset(e, "pe", "L.")

        @block.scalar
        def _(e):
            ch = Chain(e, sem("act_chain"))
            e.wait_ge(sem("c_loaded"), 16)
            e.activation(sT[:], sT[:], ACT.Silu).then_inc(sem("silu_c"), 1)
            meet(e, "act")
            for l in range(L):
                q_ctx = l < L - 1
                t0 = 0 if q_ctx else NCT
                jobs = proj_jobs(l)
                n_conv = [0]

                def silu(c):
                    e.wait_ge(sem("L.conv_done"), c + 1)
                    if c >= 2:
                        e.wait_ge(sem("L.rope_done"), c - 1)
                    if q_ctx or c >= 2:
                        e.activation(mlqk[:, c, 0:CTX], cvs[:, c % 2, 0:CTX], ACT.Silu).then_inc(sem("L.silu_ctx"), 1)
                    e.activation(ysil[:, c % 2, :], cvs[:, c % 2, 260:772], ACT.Silu).then_inc(sem("L.silu_done"), 1)

                done = 0
                for n, (kind, i, part, ev) in enumerate(jobs):
                    if ev != "a":
                        continue
                    bank = ps[n % 8]
                    width = SEQ if part == "x" else CTX
                    tc = slice(CTX, T) if part == "x" else slice(0, CTX)
                    if kind == "M" and part == "x" and i >= 2:
                        e.wait_ge(sem("L.conv_done"), i - 1)
                    if kind in "VO":
                        e.wait_ge(sem("L.rope_done"), 4)
                    e.wait_ge(sem("L.proj_mm"), n + 1)
                    if kind == "T":
                        cnd = 1 if part == "x" else 0
                        ins = e.activation(uT[:, i, tc], bank[:, 0:width], ACT.Identity, scale=modcol[:, l, SC1 * KD + i, cnd:cnd + 1],
                                           bias=modcol[:, l, SH1 * KD + i, cnd:cnd + 1])
                    elif kind == "G":
                        if i == 0 and part == "x":
                            e.wait_ge(sem("L.small_loaded"), 48)
                        ins = e.activation((li, lf)[i][:, tc], bank[0:8, 0:width], ACT.Identity, bias=bgs[0:8, i:i + 1])
                    elif kind == "M":
                        at = 262 if part == "x" else 2
                        ins = e.activation(raw[:, i % 2, at:at + width], bank[:, 0:width], ACT.Copy)
                    elif kind == "Q":
                        if part == "x":
                            ins = e.activation(nq[:, i, CTX:T].rearrange("p (b r c) -> p r b c", b=NBAND, r=ROWS),
                                               bank[:, :].rearrange("p (r b c) -> p r b c", r=ROWS, b=NBAND), ACT.Copy, scale=DH ** -0.5)
                        else:
                            ins = e.activation(nq[:, i, 0:CTX], bank[:, 0:CTX], ACT.Copy, scale=DH ** -0.5)
                    elif kind == "K":
                        ins = e.activation(nk[:, i, tc], bank[:, 0:width], ACT.Copy)
                    elif kind == "V":
                        ins = e.activation(vml[:, i, :, 0:DV], bank[:, :].rearrange("p (h d) -> p h d", h=MLH), ACT.Copy)
                    elif kind == "O":
                        ins = e.activation(sigo[:, i, :], bank[:], ACT.Sigmoid)
                    ins.then_inc(sem("L.proj_evac_a"), 1)
                    done += 1
                    if kind == "G" and i == 1 and part == "c":
                        e.wait_ge(sem("L.proj_evac_a"), done)
                        ch.link(e.activation(lnl, lf, ACT.Abs))
                        ch.link(e.activation(lnl, lnl, ACT.Exp, scale=-1.0))
                        e.activation(lnl, lnl, ACT.Ln, bias=1.0).then_inc(sem("L.ln_done"), 1)
                        e.wait_ge(sem("L.negm_ready"), 2)
                        ch.link(e.activation(eF, eF, ACT.Exp, scale=-1.0))
                        e.activation(eB, eB, ACT.Exp, scale=-1.0).then_inc(sem("L.gates_done"), 1)
                    if kind == "M" and i >= 1 and (part == "c" or (not q_ctx and i < 2)):
                        silu(i - 1)
                        if i == 3:
                            silu(3)
                meet(e, "act")
                for h in range(MLH):
                    for i in range(NT):
                        m = h * NT + i
                        e.wait_ge(sem("L.arg_ready"), m + 1)
                        fa, fn = at_f(i, f_start(i, t0)), (NT - f_start(i, t0)) * P
                        ch.link(e.activation(WD[:, 0, fa:fa + fn], WD[:, 0, fa:fa + fn], ACT.Exp))
                        ba, bn = OFF_B[i], b_len(i, t0)
                        e.activation(WD[:, 1, ba:ba + bn], WD[:, 1, ba:ba + bn], ACT.Exp).then_inc(sem("L.decay_ready"), 1)
                e.wait_ge(sem("L.h_done"), MLH * (NT - t0))
                e.wait_ge(sem("eps_set"), 1)
                e.activation(rstd[:, t0 * MLH:], stat[:, t0 * MLH:, 1], ACT.Sqrt, bias=epsc[:, 0:1]).then_inc(sem("L.hsd"), 1)
                for t in range(t0, NT):
                    e.wait_ge(sem("L.mlT"), t - t0 + 1)
                    e.activation(mixT[:, 0:MLH, t * P:(t + 1) * P], ps[6 + t % 2][:, :].rearrange("p (h t) -> p h t", h=MLH), ACT.Copy).then_inc(sem("L.mlT_evac"), 1)
                att = attention_jobs(l)
                for n in range(len(att) + 1):
                    if n < len(att):
                        b, h = att[n]
                        a0 = 0 if b < NBAND else LOC
                        e.wait_ge(sem("L.nmax_ready"), n + 1)
                        if n >= 2:
                            e.wait_ge(sem("L.pT_mm"), n - 1)
                        e.activation(prob[:, n % 2, a0:512], ps[n % 2][:, a0:512], ACT.Exp, bias=nmax[:, n % 2:n % 2 + 1],
                                     accum_out=rsum[:, n % 2:n % 2 + 1]).then_inc(sem("L.p_exp"), 1)
                    if n >= 1:
                        m = n - 1
                        a0 = 0 if att[m][0] < NBAND else LOC
                        e.wait_ge(sem("L.pT_mm"), m + 1)
                        if m >= 2:
                            e.wait_ge(sem("L.o_mm"), m - 1)
                        e.activation(probT[:, m % 2, a0:512], ps[2 + m % 2][:, a0:512], ACT.Copy).then_inc(sem("L.pT_ready"), 1)
                meet(e, "act")
                for t in range(t0, NT):
                    e.wait_ge(sem("L.var1"), t - t0 + 1)
                    e.activation(sd[:, 0:1], mv[:, 1:2], ACT.Sqrt, bias=epsc[:, 0:1]).then_inc(sem("L.sd1"), 1)
                meet(e, "act")
                n = 0
                for k in range(KD):
                    for part in range(0 if q_ctx else 1, 2):
                        tc, width = (slice(0, CTX), CTX) if part == 0 else (slice(CTX, T), SEQ)
                        e.wait_ge(sem("L.pu_mm"), n + 1)
                        e.activation(puT[:, k, tc], ps[n % 8][:, 0:width], ACT.Identity, scale=modcol[:, l, SC2 * KD + k, part:part + 1],
                                     bias=modcol[:, l, SH2 * KD + k, part:part + 1]).then_inc(sem("L.pu_evac"), 1)
                        n += 1
                m = 0
                for c in range(2 * PH):
                    for part in range(0 if q_ctx else 1, 2):
                        tc, width = (slice(0, CTX), CTX) if part == 0 else (slice(CTX, T), SEQ)
                        e.wait_ge(sem("L.q_mm"), m + 1)
                        e.activation(qT[:, c, tc], ps[m % 8][:, 0:width], ACT.Copy).then_inc(sem("L.q_evac"), 1)
                        m += 1
                meet(e, "act")
                for sg, (cnd, ta, tb) in enumerate(segments(l)):
                    nt = tb - ta

                    def stage_queries(unit, h, t):
                        e.wait_ge(sem("S.key_mm"), unit + 1)
                        e.sem_inc(sem("S.act_token"), 1)
                        e.activation(qs[:], qT[:, bass.ds(2 * h, 2), bass.ds(t * P, P)], ACT.Copy).then_inc(sem("S.qs_ready"), 1)

                    def gate_exp(t):
                        e.wait_ge(sem("S.route_done"), t * PH + PH)
                        e.sem_inc(sem("S.act_token"), 1)
                        e.activation(gate_all[:, bass.ds(t * PH * TOPK, PH * TOPK)], gate_all[:, bass.ds(t * PH * TOPK, PH * TOPK)], ACT.Exp).then_inc(sem("S.gexp"), 1)

                    def tile(t, route):
                        with e.Fori(0, PH) as h:
                            if route:
                                stage_queries(t * PH + h + PH, h, t + (ta + 1))
                            for k in range(TOPK):
                                e.wait_ge(sem("S.dot_done"), t * (PH * TOPK) + h * TOPK + (k + 1))
                                e.activation(acts[:, k:k + 1], dots[:, k:k + 1], ACT.Gelu_apprx_tanh).then_inc(sem("S.act_done"), 1)
                        if route:
                            gate_exp(t + 1)
                        e.wait_ge(sem("S.var2"), t + 1)
                        e.activation(sd2[:, 0:1], mv2[:, 1:2], ACT.Sqrt, bias=epsc[:, 0:1]).then_inc(sem("S.sd2"), 1)

                    e.sem_inc(sem("S.key_mm"), 1)
                    with e.Fori(0, PH) as h:
                        stage_queries(h, h, ta)
                    gate_exp(0)
                    with e.Fori(0, nt - 1) as t:
                        tile(t, True)
                    tile(nt - 1, False)
                    meet(e, "act")
                    reset(e, "act", "S.")
                reset(e, "act", "L.")

        @block.gpsimd
        def _(e):
            e.memset(epsc[:], EPS).then_inc(sem("eps_set"), 1)
            meet(e, "pool")
            for l in range(L):
                q_ctx = l < L - 1
                jobs = proj_jobs(l)
                n_t = {w: sum(j[0] == "T" and j[3] == w for j in jobs) for w in "va"}
                first_b = [n for n, j in enumerate(jobs) if j[0] == "B"][0]
                e.wait_ge(sem("L.proj_evac_v"), n_t["v"])
                e.wait_ge(sem("L.proj_evac_a"), n_t["a"])
                for n in range(2 * NBAND):
                    b, a = n // 2, n % 2
                    if n >= 2:
                        e.wait_ge(sem("L.proj_mm"), first_b + n - 1)
                    lat = uT[:, :, CTX:T].rearrange("p k (r w) -> p k r w", w=GRID_W)
                    e.tensor_copy(ubT[:, n % 2].rearrange("p k (r w) -> p k r w", r=4),
                                  lat[:, :, 4 * a:4 * a + 4, BAND_LO[b]:BAND_LO[b] + BAND]).then_inc(sem("L.band_ready"), 1)
                meet(e, "pool")
                for n in range(2 * NBAND):
                    e.wait_ge(sem(f"L.bias_loaded{n % 2}"), 16 * (n // 2 + 1))
                    for q in range(4):
                        ins = e.tensor_tensor(biasb[:, n % 2, q, :], biasb[:, n % 2, q, :], CN[:, C_MASK + (n // 2) * LOC:C_MASK + (n // 2 + 1) * LOC], ALU.add)
                    ins.then_inc(sem("L.bias_ready"), 1)
                meet(e, "pool")
                meet(e, "pool")
                meet(e, "pool")
                for sg, (cnd, ta, tb) in enumerate(segments(l)):
                    nt = tb - ta
                    e.sem_inc(sem("S.slot_done"), RING)
                    with e.Fori(0, nt * PH) as un:
                        for k in range(TOPK):
                            if k % RING == 0:
                                e.wait_ge(sem("S.idx_ready"), un * 2 + (k // RING + 1))
                                e.sem_inc(sem("S.pool_token"), 1)
                            e.wait_ge(sem("S.slot_done"), un * TOPK + (k + 1))
                            e.sem_inc(sem("S.pool_token"), 1)
                            e.indirect_dma_start(ring[:, k % RING, :], None, updown,
                                                 bass.IndirectOffsetOnAxis(ap=idx16[:, k:k + 1], axis=0)).then_inc(sem(f"rows{k % RING}"), 16)
                    meet(e, "pool")
                    reset(e, "pool", "S.")
                reset(e, "pool", "L.")

        @block.vector
        def _(e):
            ch = Chain(e, sem("dve_chain"))
            lc = Chain(e, sem("dve_loop_chain"), sem("dve_restarts"))
            e.wait_ge(sem("adab_loaded"), 16)
            for n in range(24):
                e.wait_ge(sem("mod_mm"), n + 1)
                one = 1.0 if (n % 12) // 2 in (SC1, SC2) else 0.0
                e.scalar_tensor_tensor(out=modrow[0:2, n * 512:(n + 1) * 512], in0=ps[n % 4][0:2, :], scalar=one,
                                       in1=adab[0:2, n * 512:(n + 1) * 512], op0=ALU.add, op1=ALU.add).then_inc(sem("mod_row"), 1)
            e.wait_ge(sem("modcol_t"), L)
            for l in range(L):
                e.tensor_copy(modcol[:, l].rearrange("p a b -> p (a b)"), ps[4 + l][:, 0:2 * N_MOD * KD])
            meet(e, "dve")
            for l in range(L):
                q_ctx = l < L - 1
                t0 = 0 if q_ctx else NCT
                jobs = proj_jobs(l)
                for a in range(2):
                    for c0, c1 in ((0, 2), (258, 262), (774, 776)):
                        ins = e.memset(raw[:, a, c0:c1], 0.0)
                ch.link(ins)
                evac_no = ordinals(jobs)

                def conv(c):
                    lo = 0 if (q_ctx or c >= 2) else 260
                    for part in "xc":
                        if ("M", c, part, "a") in jobs:
                            e.wait_ge(sem("L.proj_evac_a"), evac_no[jobs.index(("M", c, part, "a"))])
                    if c >= 2:
                        e.wait_ge(sem("L.silu_done"), c - 1)
                    cvb = cvs[:, c % 2, lo:772]
                    ch.link(e.tensor_scalar(cvb, raw[:, c % 2, lo:772], convs[:, c, 0:1], None, ALU.mult))
                    for w in range(1, 5):
                        ins = e.scalar_tensor_tensor(out=cvb, in0=raw[:, c % 2, lo + w:772 + w], scalar=convs[:, c, w:w + 1], in1=cvb, op0=ALU.mult, op1=ALU.add)
                        if w < 4:
                            ch.link(ins)
                    ins.then_inc(sem("L.conv_done"), 1)

                def gates():
                    e.wait_ge(sem("L.ln_done"), 1)
                    ch.link(e.scalar_tensor_tensor(out=lf, in0=lf, scalar=0.0, in1=lnl, op0=ALU.min, op1=ALU.subtract))
                    ch.link(e.memset(lnl, 1.0))
                    for g, F, nM, back in ((gF, eF, nMf, False), (gB, eB, nMb, True)):
                        parts = [(0, CTX), (CTX, T)] if back else [(0, T)]
                        for what, src, dst in (("sum", lf, F), ("max", g, cum)):
                            if what == "max":
                                ch.link(e.tensor_tensor(g, li, F, ALU.subtract))
                            start = 0.0
                            for a, b in parts:
                                v = [x[:, a:b][:, ::-1] if back else x[:, a:b] for x in (lnl if what == "sum" else src, src, dst)]
                                ops = (ALU.mult, ALU.add) if what == "sum" else (ALU.max, ALU.max)
                                ch.link(e.tensor_tensor_scan(v[2], v[0], v[1], start, *ops))
                                start = dst[:, a:a + 1] if back else None
                        ch.link(e.tensor_tensor(F, F, cum, ALU.add))
                        e.tensor_scalar(nM, cum, -1.0, None, ALU.mult).then_inc(sem("L.negm_ready"), 1)
                        e.wait_ge(sem("L.negm_ready"), 2 if back else 1)

                for n, (kind, i, part, ev) in enumerate(jobs):
                    if kind == "M" and part == "x" and i >= 1:
                        conv(i - 1)
                    if kind == "M" and part == "x" and i == 0:
                        gates()
                    if kind == "Q" and i == 0 and part == "x":
                        conv(3)
                    if ev != "v":
                        continue
                    bank = ps[n % 8]
                    width = SEQ if part == "x" else CTX
                    tc = slice(CTX, T) if part == "x" else slice(0, CTX)
                    if kind in "VB":
                        e.wait_ge(sem("L.rope_done"), 4)
                    e.wait_ge(sem("L.proj_mm"), n + 1)
                    if kind == "T":
                        ins = e.tensor_scalar(uT[:, i, tc], bank[:, 0:width], modcol[:, l, SC1 * KD + i, 1:2], modcol[:, l, SH1 * KD + i, 1:2], ALU.mult, ALU.add)
                    elif kind == "X":
                        ins = e.tensor_copy(gcol, bank[:, 0:4 * NT * 8])
                    elif kind == "R":
                        e.wait_ge(sem("L.silu_done"), i + 1)
                        e.tensor_tensor(rt[:, 0, :], ysil[:, i % 2, :], CN[:, C_COS:C_COS + SEQ], ALU.mult)
                        ch.link(e.tensor_tensor(rt[:, 1, :], bank[:], CN[:, C_SIN:C_SIN + SEQ], ALU.mult))
                        ch.link(e.tensor_tensor(mlqk[:, i, CTX:T], rt[:, 0, :], rt[:, 1, :], ALU.add))
                        e.sem_inc(sem("L.rope_done"), 1)
                        e.sem_inc(sem("L.proj_evac_v"), 1)
                        continue
                    elif kind == "Q":
                        if part == "x":
                            ins = e.tensor_scalar(nq[:, i, CTX:T].rearrange("p (b r c) -> p r b c", b=NBAND, r=ROWS),
                                                  bank[:, :].rearrange("p (r b c) -> p r b c", r=ROWS, b=NBAND), DH ** -0.5, None, ALU.mult)
                        else:
                            ins = e.tensor_scalar(nq[:, i, 0:CTX], bank[:, 0:CTX], DH ** -0.5, None, ALU.mult)
                    elif kind == "K":
                        ins = e.tensor_copy(nk[:, i, tc], bank[:, 0:width])
                    elif kind == "V":
                        ins = e.tensor_copy(vml[:, i, :, 0:DV], bank[:, :].rearrange("p (h d) -> p h d", h=MLH))
                    else:
                        ins = e.tensor_copy(vband[:, i, :], bank[:])
                    ins.then_inc(sem("L.proj_evac_v"), 1)
                e.memset(vml[:, :, :, DV:DV + 1].rearrange("p a b c -> p (a b) c"), 1.0)
                meet(e, "dve")
                def args(h, i):
                    fs = f_start(i, t0)
                    fa, fn = at_f(i, fs), (NT - fs) * P
                    nm = negm[:, h % 2]
                    e.tensor_scalar(WD[:, 0, fa:fa + fn], nm[:, 0, fs * P:T], gc[:, 0, i, h:h + 1], 0.0, ALU.add, ALU.min)
                    ba = OFF_B[i]
                    gb = gc[:, 1, i, 4 + h:5 + h]
                    if i < NCT:
                        ins = e.tensor_scalar(WD[:, 1, ba:ba + SEQ], nm[:, 1, CTX:T], gb, 0.0, ALU.add, ALU.min)
                        if q_ctx:
                            n = (i + 1) * P
                            ins = e.tensor_scalar(WD[:, 1, ba + SEQ:ba + SEQ + n], nm[:, 1, 0:n], gb, 0.0, ALU.add, ALU.min)
                    else:
                        n = (i - 1) * P
                        ins = e.tensor_scalar(WD[:, 1, ba:ba + n], nm[:, 1, CTX:CTX + n], gb, 0.0, ALU.add, ALU.min)
                    ins.then_inc(sem("L.arg_ready"), 1)

                def apply(h, i):
                    m = h * NT + i
                    e.wait_ge(sem("L.decay_ready"), m + 1)
                    e.wait_ge(sem("L.s_ready"), m + 1)
                    if i >= t0:
                        e.tensor_tensor(WD[:, 0, at_f(i, i):at_f(i, i) + P], WD[:, 0, at_f(i, i):at_f(i, i) + P], CN[:, C_TRI:C_TRI + P], ALU.mult)
                        ch.link(e.tensor_tensor(WD[:, 1, at_b(i, i):at_b(i, i) + P], WD[:, 1, at_b(i, i):at_b(i, i) + P], CN[:, C_TRI + P:C_TRI + 2 * P], ALU.mult))
                    SX, SC = ps[m % 2], ps[2 + m % 2]
                    work = []
                    xs = max(i, NCT)
                    work.append((0, at_f(i, xs), SX, (xs - NCT) * P, (NT - xs) * P))
                    work.append((1, OFF_B[i], SX, 0, SEQ if i < NCT else (i - 1) * P))
                    if i < NCT and q_ctx:
                        work.append((0, at_f(i, i), SC, i * P, (NCT - i) * P))
                        work.append((1, OFF_B[i] + SEQ, SC, 0, (i + 1) * P))
                    for d, wa, S, sa, n in work:
                        ins = e.scalar_tensor_tensor(out=WD[:, d, wa:wa + n], in0=S[:, sa:sa + n], scalar=DK ** -0.5, in1=WD[:, d, wa:wa + n], op0=ALU.mult, op1=ALU.mult)
                    ins.then_inc(sem("L.w_ready"), 1)

                gc = gcol.rearrange("p (a t r) -> p a t r", a=4, t=NT)
                for h in range(MLH):
                    e.wait_ge(sem(f"L.negm_loaded{h % 2}"), 32 * (h // 2 + 1))
                    if h >= 1:
                        e.wait_ge(sem("L.num_ready"), h * (NT - t0))
                    args(h, 0)
                    for i in range(NT):
                        if i + 1 < NT:
                            args(h, i + 1)
                        apply(h, i)
                    for j in range(t0, NT):
                        m = h * (NT - t0) + j - t0
                        bank = ps[4 + m % 2]
                        e.wait_ge(sem("L.num_ready"), m + 1)
                        o = (2 * NT + j) * 8 + h
                        dn = bank[:, DV:2 * DV + 2:DV + 1]
                        ch.link(e.scalar_tensor_tensor(out=den[:, 1, :], in0=dn, scalar=-1.0, in1=gcol[:, o:o + NT * 8 + 5:NT * 8 + 4], op0=ALU.mult, op1=ALU.max))
                        ch.link(e.tensor_tensor(den[:, 0, :], dn, den[:, 1, :], ALU.max))
                        ch.link(e.reciprocal(rden[:, 0, :], den[:, 0, :]))
                        Hj = H[:, j, h * DV:(h + 1) * DV]
                        ch.link(e.tensor_scalar(Hj, bank[:, 0:DV], rden[:, 0, 0:1], None, ALU.mult))
                        ch.link(e.scalar_tensor_tensor(out=Hj, in0=bank[:, DV + 1:2 * DV + 1], scalar=rden[:, 0, 1:2], in1=Hj, op0=ALU.mult, op1=ALU.add))
                        ch.link(e.bn_stats(bns[:, 0, :], Hj))
                        e.bn_aggr(stat[:, j * MLH + h, :], bns[:, 0, :]).then_inc(sem("L.h_done"), 1)
                e.wait_ge(sem("L.hsd"), 1)
                e.wait_ge(sem("L.nw_loaded"), 16)
                ch.link(e.reciprocal(rstd[:, t0 * MLH:], rstd[:, t0 * MLH:]))
                for t in range(t0, NT):
                    for h in range(MLH):
                        n = t * MLH + h
                        ins = e.tensor_scalar(H[:, t, h * DV:(h + 1) * DV], H[:, t, h * DV:(h + 1) * DV], stat[:, n, 0:1], rstd[:, n:n + 1], ALU.subtract, ALU.mult)
                    ch.link(ins)
                    ch.link(e.tensor_tensor(H[:, t, :], H[:, t, :], nwrow, ALU.mult))
                    e.tensor_tensor(H[:, t, :], H[:, t, :], sigo[:, t, :], ALU.mult).then_inc(sem("L.mlout"), 1)
                att = attention_jobs(l)
                for n in range(len(att) + 2):
                    if n < len(att):
                        b, h = att[n]
                        a0 = 0 if b < NBAND else LOC
                        e.wait_ge(sem("L.s_att"), n + 1)
                        if n >= 2:
                            e.wait_ge(sem("L.p_exp"), n - 1)
                        if b < NBAND:
                            half = 2 * b + h // 4
                            e.wait_ge(sem("L.bias_ready"), half + 1)
                            e.tensor_tensor(ps[n % 2][:, 0:LOC], ps[n % 2][:, 0:LOC], biasb[:, half % 2, h % 4, :], ALU.add).then_inc(sem("L.bias_used"), 1)
                            e.wait_ge(sem("L.bias_used"), n + 1)
                        e.tensor_reduce(nmax[:, n % 2:n % 2 + 1], ps[n % 2][:, a0:512], AX.X, ALU.max, negate=True).then_inc(sem("L.nmax_ready"), 1)
                    if 1 <= n <= len(att):
                        m = n - 1
                        a0 = 0 if att[m][0] < NBAND else LOC
                        e.wait_ge(sem("L.p_exp"), m + 1)
                        ch.link(e.reciprocal(rinv[:, m % 2:m % 2 + 1], rsum[:, m % 2:m % 2 + 1]))
                        e.tensor_scalar(prob[:, m % 2, a0:512], prob[:, m % 2, a0:512], rinv[:, m % 2:m % 2 + 1], None, ALU.mult).then_inc(sem("L.p_ready"), 1)
                    if n >= 2:
                        m = n - 2
                        b, h = att[m]
                        o = (h % 2) * DH
                        e.wait_ge(sem("L.o_mm"), m + 1)
                        src = ps[4 + m % 2][o:o + DH, 0:P]
                        if b < NBAND:
                            dst = mixT[o:o + DH, 4 + h // 2, CTX:T].rearrange("p (r w) -> p r w", w=GRID_W)[:, :, b * QB:(b + 1) * QB]
                            src = src.rearrange("p (r c) -> p r c", r=ROWS)
                        else:
                            dst = mixT[o:o + DH, 4 + h // 2, (b - NBAND) * P:(b - NBAND + 1) * P]
                        e.tensor_copy(dst, src).then_inc(sem("L.o_att"), 1)
                meet(e, "dve")

                e.wait_ge(sem("L.row1_loaded"), 48)
                for t in range(t0, NT):
                    m = t - t0
                    w = tmp[:, m % 2, :]
                    e.wait_ge(sem("L.y_ready"), m + 1)
                    for hf in range(2):
                        c = slice(hf * 512, (hf + 1) * 512)
                        ins = e.tensor_tensor(w[:, c], ps[2 * (m % 4) + hf][:], g1r[:, cond_of[t], c], ALU.mult)
                    ins.then_inc(sem("L.y_read"), 1)
                    e.wait_ge(sem("L.y_read"), m + 1)
                    ch.link(e.scalar_tensor_tensor(out=w, in0=X[:, t, :], scalar=ALPHA, in1=w, op0=ALU.mult, op1=ALU.add))
                    e.bn_stats(lns[:, 0, 0, :], w[:, 0:512])
                    ch.link(e.bn_stats(lns[:, 0, 1, :], w[:, 512:D]))
                    e.bn_aggr(mv, lns[:, 0].rearrange("p a b -> p (a b)")).then_inc(sem("L.var1"), 1)
                    e.wait_ge(sem("L.var1"), m + 1)
                    e.wait_ge(sem("L.sd1"), m + 1)
                    ch.link(e.reciprocal(sd[:, 1:2], sd[:, 0:1]))
                    ch.link(e.tensor_scalar(w, w, mv[:, 0:1], sd[:, 1:2], ALU.subtract, ALU.mult))
                    ch.link(e.tensor_tensor(w, w, ln1r[:, 0, :], ALU.mult))
                    ch.link(e.tensor_tensor(X[:, t, :], w, ln1r[:, 1, :], ALU.add))
                meet(e, "dve")
                meet(e, "dve")

                for sg, (cnd, ta, tb) in enumerate(segments(l)):
                    nt = tb - ta
                    UN = TOPK

                    def route(un):
                        e.wait_ge(sem("S.key_mm"), un + 2)
                        e.sem_inc(sem("S.dve_token"), 1)
                        S = [ps[2][:, hf * NKEY:(hf + 1) * NKEY] for hf in range(2)]
                        e.max(tv[:, 0, 0:8], S[0])
                        yield
                        lc.link(e.max(tv[:, 1, 0:8], S[1]))
                        yield
                        for hf in range(2):
                            e.max_index(ti[:, hf, 0:8], tv[:, hf, 0:8], S[hf])
                            yield
                        e.match_replace(sc[:, 0, :], tv[:, 0, 0:8], S[0], LOWEST)
                        yield
                        e.match_replace(sc[:, 1, :], tv[:, 1, 0:8], S[1], LOWEST).then_inc(sem("S.route_read"), 1)
                        e.wait_ge(sem("S.route_read"), un + 2)
                        e.sem_inc(sem("S.dve_token"), 1)
                        yield
                        e.max(tv[:, 0, 8:16], sc[:, 0, :])
                        yield
                        lc.link(e.max(tv[:, 1, 8:16], sc[:, 1, :]))
                        yield
                        for hf in range(2):
                            e.max_index(ti[:, hf, 8:16], tv[:, hf, 8:16], sc[:, hf, :])
                            yield
                        lc.link(e.tensor_tensor(cand.rearrange("p (a b) -> p a b", a=TOPK), tv[:, 0, :].unsqueeze(2).to_broadcast([P, TOPK, TOPK]),
                                                tv[:, 1, :].unsqueeze(1).to_broadcast([P, TOPK, TOPK]), ALU.add))
                        yield
                        lc.link(e.max(tt[:, 0:8], cand))
                        yield
                        e.max_index(pos[:, 0:8], tt[:, 0:8], cand)
                        yield
                        lc.link(e.match_replace(cand2, tt[:, 0:8], cand, LOWEST))
                        yield
                        lc.link(e.max(tt[:, 8:16], cand2))
                        yield
                        lc.link(e.max_index(pos[:, 8:16], tt[:, 8:16], cand2))
                        yield
                        e.tensor_scalar(hilo[:, 0, :], pos, 4, None, ALU.logical_shift_right)
                        lc.link(e.tensor_scalar(hilo[:, 1, :], pos, 15, None, ALU.bitwise_and))
                        yield
                        for hf in range(2):
                            o3 = oh.rearrange("p (k a) -> p k a", k=TOPK)
                            lc.link(e.tensor_tensor(o3, hilo[:, hf, :].unsqueeze(2).to_broadcast([P, TOPK, TOPK]),
                                                    iota.unsqueeze(1).to_broadcast([P, TOPK, TOPK]), ALU.is_equal))
                            yield
                            lc.link(e.tensor_tensor(o3, o3, ti[:, hf, :].unsqueeze(1).to_broadcast([P, TOPK, TOPK]), ALU.mult))
                            yield
                            lc.link(e.tensor_reduce(e1[:, hf, :], o3, AX.X, ALU.add))
                            yield
                        lc.link(e.tensor_scalar(e1[:, 0, :], e1[:, 0, :], float(NKEY), float(l * NEXP), ALU.mult, ALU.add))
                        yield
                        e.tensor_tensor(eidx_all[:, bass.ds(un * UN, UN)], e1[:, 0, :], e1[:, 1, :], ALU.add)
                        e.tensor_scalar(gate_all[:, bass.ds(un * UN, UN)], tt, tt[:, 0:1], None, ALU.subtract).then_inc(sem("S.route_done"), 1)
                        e.wait_ge(sem("S.route_done"), un + 1)
                        yield

                    def stage_index(un, half):
                        e.tensor_copy(idx16[:, 8 * half:8 * half + 8], eidx_all[:, bass.ds(un * UN + 8 * half, 8)]).then_inc(sem("S.idx_ready"), 1)

                    def gate_norm(t):
                        e.wait_ge(sem("S.gexp"), t + 1)
                        g = gate_all[:, bass.ds(t * PH * TOPK, PH * TOPK)].rearrange("p (h k) -> p h k", h=PH)
                        lc.restart()
                        lc.link(e.tensor_reduce(gsum, g, AX.X, ALU.add))
                        lc.link(e.reciprocal(gsum, gsum))
                        lc.link(e.tensor_tensor(g, g, gsum.unsqueeze(2).to_broadcast([P, PH, TOPK]), ALU.mult))

                    def make_diag(un, k):
                        e.wait_ge(sem("S.act_done"), un * UN + (k + 1))
                        e.wait_ge(sem("S.slot_done"), un * UN + (k - 1 + RING))
                        e.tensor_scalar(diag[:, k % 2, :], ident, acts[:, k:k + 1], gate_all[:, bass.ds(un * UN + k, 1)], ALU.mult, ALU.mult).then_inc(sem("S.diag_ready"), 1)

                    def unit(t, h, steps):
                        un = t * PH + h
                        lc.restart()
                        for k in range(TOPK):
                            e.wait_ge(sem(f"rows{k % RING}"), un * 32 + (32 * units_before(l, sg) + 16 * (k // RING + 1)))
                            e.tensor_tensor_reduce(prod[:, k % 2, :], ring[:, k % RING, 0:D], u, 1.0, 0.0, ALU.mult, ALU.add, dots[:, k:k + 1]).then_inc(sem("S.dot_done"), 1)
                            if k >= 1:
                                make_diag(un, k - 1)
                            if k % RING == RING - 1:
                                stage_index(un + 1, k // RING)
                            for _ in range(2):
                                next(steps, None)
                        for _ in steps:
                            pass
                        make_diag(un, TOPK - 1)

                    def tile(t, more):
                        xt = X[:, bass.ds(t + ta, 1), :]
                        lc.restart()
                        lc.link(e.tensor_tensor(u, xt.rearrange("p a d -> p (a d)"), sc2r, ALU.mult))
                        lc.link(e.tensor_tensor(u, u, sh2r, ALU.add))
                        with e.Fori(0, PH) as h:
                            unit(t, h, route(t * PH + h + PH) if more else iter(()))
                        if more:
                            gate_norm(t + 1)
                        e.wait_ge(sem("S.acc_ready"), t + 1)
                        lc.restart()
                        for hf in range(2):
                            c = slice(hf * 512, (hf + 1) * 512)
                            ins = e.tensor_tensor(junk[:, c], ps[hf][:], g2r[:, c], ALU.mult)
                        ins.then_inc(sem("S.acc_free"), 1)
                        e.wait_ge(sem("S.acc_free"), t + 2)
                        lc.link(e.scalar_tensor_tensor(out=junk, in0=xt.rearrange("p a d -> p (a d)"), scalar=ALPHA, in1=junk, op0=ALU.mult, op1=ALU.add))
                        e.bn_stats(lns2[:, 0, :], junk[:, 0:512])
                        lc.link(e.bn_stats(lns2[:, 1, :], junk[:, 512:D]))
                        e.bn_aggr(mv2, lns2.rearrange("p a b -> p (a b)")).then_inc(sem("S.var2"), 1)
                        e.wait_ge(sem("S.sd2"), t + 1)
                        lc.link(e.reciprocal(sd2[:, 1:2], sd2[:, 0:1]))
                        lc.link(e.tensor_scalar(junk, junk, mv2[:, 0:1], sd2[:, 1:2], ALU.subtract, ALU.mult))
                        lc.link(e.tensor_tensor(junk, junk, ln2r[:, 0, :], ALU.mult))
                        lc.link(e.tensor_tensor(xt.rearrange("p a d -> p (a d)"), junk, ln2r[:, 1, :], ALU.add))

                    e.memset(zero, 0.0).then_inc(sem("S.zero_set"), 1)
                    e.memset(eidx_all[:, nt * PH * UN:nt * PH * UN + UN], 0).then_inc(sem("S.zero_set"), 1)
                    e.sem_inc(sem("S.route_read"), 1)
                    e.sem_inc(sem("S.acc_free"), 1)
                    with e.Fori(0, PH) as h:
                        lc.restart()
                        for _ in route(h):
                            pass
                    gate_norm(0)
                    stage_index(0, 0)
                    stage_index(0, 1)
                    e.wait_ge(sem("S.row2_loaded"), 80)
                    with e.Fori(0, nt - 1) as t:
                        tile(t, True)
                    tile(nt - 1, False)
                    meet(e, "dve")
                    reset(e, "dve", "S.", ch)
                reset(e, "dve", "L.", ch)


def kernel(**inputs):
    import numpy as _np
    import concourse.bacc as _bacc
    from concourse import mybir as _mybir
    from concourse.bass_utils import run_bass_kernel_spmd as _run

    nc = _bacc.Bacc("TRN2", target_bir_lowering=False, num_devices=1)
    arrays = {}

    def inp(name, a):
        a = _np.ascontiguousarray(a)
        arrays[f"in_{name}"] = a
        return nc.dram_tensor(f"in_{name}", a.shape, _mybir.dt.from_np(a.dtype), kind="ExternalInput").ap()

    i = {k: _np.asarray(v) for k, v in inputs.items()}
    li_cols = [0, 1, 2, 3, 8, 9, 10, 11]
    lf_cols = [4, 5, 6, 7, 12, 13, 14, 15]
    gates = i["w_in"][:, :, COL_G:COL_G + 16][:, :, li_cols + lf_cols]
    q = _np.arange(P)
    k = _np.arange(LOC)
    row = k[None] // BAND - q[:, None] // QB + ROWS - 1
    spread = []
    for b in range(NBAND):
        col = BAND_LO[b] + k[None] % BAND - (b * QB + q[:, None] % QB)
        col = _np.clip(col, 1 - WIN, WIN - 1) + WIN - 1
        spread.append(i["na_rpb"][:, :, row, col].transpose(0, 2, 1, 3))
    args = [
        inp("x", _np.concatenate([i["ctx"][0], i["x"][0]], 0)),
        inp("c", _np.stack([i["c_ctx"], i["c"][0]]).reshape(2, KD, P).transpose(2, 1, 0)),
        inp("consts", shape_constants()),
        inp("ada_w", i["ada_w"]), inp("ada_b", i["ada_b"]), inp("w_in", i["w_in"]),
        inp("wg", gates.reshape(L, KD, P, 16).transpose(0, 2, 1, 3)),
        inp("bg", _np.stack([i["b_gate"][:, li_cols], i["b_gate"][:, lf_cols]], -1)),
        inp("conv_w", i["conv_w"].reshape(L, 5, 4, P).transpose(0, 3, 2, 1)),
        inp("ml_norm_w", i["ml_norm_w"]),
        inp("bias", _np.stack(spread, 1)),
        inp("w_out", i["w_out"]),
        inp("ln1", _np.concatenate([i["ln1_w"], i["ln1_b"]], -1)),
        inp("wq", i["peer_wq"]),
        inp("keys", i["peer_keys"].reshape(L, 2 * PH, NKEY, P).transpose(0, 3, 1, 2)),
        inp("updown", _np.concatenate([i["peer_up"].reshape(L * NEXP, D), i["peer_down"].reshape(L * NEXP, D)], -1)),
        inp("ln2", _np.concatenate([i["ln2_w"], i["ln2_b"]], -1)),
        nc.dram_tensor("mod_rows", (L, 2, N_MOD * D), _mybir.dt.float32).ap(),
        nc.dram_tensor("negm_rows", (L, 2, MLH, T), _mybir.dt.float32).ap(),
        nc.dram_tensor("out_0", (1, SEQ, D), _mybir.dt.float32, kind="ExternalOutput").ap(),
    ]
    build(nc, *args)
    r = _run(nc, [arrays], core_ids=[0])
    return r.results[0]["out_0"]
```

```python
from contextlib import ExitStack

import numpy as np
import concourse.bass as bass
from concourse import mybir

F32 = mybir.dt.float32
U32 = mybir.dt.uint32
BF16 = mybir.dt.bfloat16
ALU = mybir.AluOpType
ACT = mybir.ActivationFunctionType
AX = mybir.AxisListType

P = 128
D = 1024
KD = D // P
L = 2
CTX, SEQ = 256, 512
NT, NCT = (CTX + SEQ) // P, CTX // P
T = CTX + SEQ
GRID_W = 64
ROWS = SEQ // GRID_W
MLH, DV, DK = 4, 128, 64
NAH, DH = 8, 64
QB, BAND, WIN = 16, 32, 16
NBAND = GRID_W // QB
BAND_LO = [min(max(b * QB - WIN // 2, 0), GRID_W - BAND) for b in range(NBAND)]
LOC = ROWS * BAND
N_MOD = 6
SH1, SC1, G1, SH2, SC2, G2 = range(N_MOD)
D_IN = 3088
COL_ML, COL_V, COL_O, COL_G, COL_NQ, COL_NK, COL_NV = 0, 512, 1024, 1536, 1552, 2064, 2576
PH, NKEY, TOPK = 8, 128, 16
NEXP = NKEY * NKEY
ALPHA = (2.0 * L) ** 0.25
EPS = 1e-5
LOWEST = -3.0e38
MASKED = -1.0e30
RING = 8
EXP_AT, NORM_AT = 11, 14
LEAD = 2

C_ID, C_ROT, C_TRI, C_IOTA, C_KEEP, C_MASK, C_COS, C_SIN, C_END = 0, 128, 256, 512, 528, 528, 1552, 2064, 2576


def shape_constants():
    c = np.zeros((P, C_END), np.float32)
    p = np.arange(P)
    c[:, C_ID:C_ID + P] = np.eye(P)
    for m in range(P):
        if m % DK < DK // 2:
            c[m + DK // 2, C_ROT + m] = -1.0
        else:
            c[m - DK // 2, C_ROT + m] = 1.0
    c[:, C_TRI:C_TRI + P] = p[:, None] <= p[None, :]
    c[:, C_TRI + P:C_TRI + 2 * P] = p[:, None] >= p[None, :]
    c[:, C_IOTA:C_IOTA + TOPK] = np.arange(TOPK)
    for b in range(NBAND):
        q = b * QB + p % QB
        lo = np.clip(q - WIN // 2, 0, GRID_W - WIN)
        k = BAND_LO[b] + np.arange(BAND)
        ok = (k[None] >= lo[:, None]) & (k[None] < lo[:, None] + WIN)
        c[:, C_MASK + b * LOC:C_MASK + (b + 1) * LOC] = np.tile(np.where(ok, 0.0, MASKED), (1, ROWS))
    pos, nf = np.arange(SEQ), DK // 4
    inv = np.float32(10000.0) ** (-np.arange(nf, dtype=np.float32) / nf)
    ang = np.concatenate([(pos // GRID_W)[:, None] * inv, (pos % GRID_W)[:, None] * inv], -1).astype(np.float32)
    c[:, C_COS:C_COS + SEQ] = np.cos(ang).T[p % (DK // 2)]
    c[:, C_SIN:C_SIN + SEQ] = np.sin(ang).T[p % (DK // 2)]
    return c


class Chain:

    def __init__(self, eng, sem, token=None):
        self.eng, self.sem, self.token, self.n = eng, sem, token, 0

    def link(self, ins):
        self.n += 1
        ins.then_inc(self.sem, 1)
        self.eng.wait_ge(self.sem, self.n)
        return ins

    def restart(self):
        self.eng.sem_inc(self.token, 1)
        self.eng.sem_clear(self.sem)
        self.n = 0


def proj_jobs(l):
    q_ctx = l < L - 1
    jobs = []
    for k in range(KD):
        jobs += [("T", k, "x", "v"), ("T", k, "c", "a")]
    for g in range(2):
        jobs += [("G", g, "x", "a"), ("G", g, "c", "a")]

    def ml(c):
        out = [("M", c, "x", "a")]
        if q_ctx or c >= 2:
            out.append(("M", c, "c", "a"))
        return out
    jobs += ml(0) + ml(1) + [("X", 0, "x", "v")] + ml(2) + [("R", 0, "x", "v")] + ml(3) + [("R", 1, "x", "v")]
    for kind in "QK":
        for c in range(4):
            jobs.append((kind, c, "x", "va"[c % 2]))
            if q_ctx or kind == "K":
                jobs.append((kind, c, "c", "av"[c % 2]))
            if kind == "Q" and c < 2:
                jobs.append(("R", 2 + c, "x", "v"))
    for t in range(NT):
        jobs.append(("V", t, "x", "va"[t % 2]))
    for t in range(0 if q_ctx else NCT, NT):
        jobs.append(("O", t, "x", "a"))
    for n in range(2 * NBAND + NCT):
        jobs.append(("B", n, "x", "v"))
    return jobs


def f_start(i, t0):
    return max(i, t0)


OFF_F = [sum(6 - m for m in range(i)) * P for i in range(6)]
OFF_B = [0, 5 * P, 11 * P, 12 * P, 14 * P, 17 * P]
N_BLK = 21 * P


def at_f(i, j):
    return OFF_F[i] + (j - i) * P


def at_b(i, j):
    if i < NCT:
        return OFF_B[i] + ((j - NCT) * P if j >= NCT else 4 * P + j * P)
    return OFF_B[i] + (j - NCT) * P


def b_sources(j):
    return list(range(j, NCT)) if j < NCT else [0, 1] + list(range(j, NT))


def b_len(i, t0):
    if i < NCT:
        return SEQ + ((i + 1) * P if t0 == 0 else 0)
    return (i - 1) * P


def tile_spans(l):
    return [(0, 1), (1, 2), (2, NT - 1), (NT - 1, NT)] if l < L - 1 else [(0, NT - NCT - 1), (NT - NCT - 1, NT - NCT)]


def attention_jobs(l):
    return [(b, h) for b in range(NBAND + (NCT if l < L - 1 else 0)) for h in range(NAH)]


def last_job(jobs, kind):
    return max(n for n, j in enumerate(jobs) if j[0] == kind) + 1


def chunk_end(jobs, c):
    kind, i = "MQK"[c // 4], c % 4
    return max(n for n, j in enumerate(jobs) if j[:2] == (kind, i)) + 1


def ordinals(jobs):
    count, out = {"v": 0, "a": 0}, []
    for j in jobs:
        count[j[3]] += 1
        out.append(count[j[3]])
    return out


def build(nc, xin, cT, consts, ada_w, ada_b, w_in, wg, bg, convw, ml_norm_w, bias, w_out, ln1, wqT, keysT,
          updown, ln2, mod_d, negm_d, out):
    with ExitStack() as ctx:
        def sb(name, shape, dt=F32):
            return ctx.enter_context(nc.sbuf_tensor(name, shape, dt))

        X = sb("X", [P, NT, D])
        CN = sb("CN", [P, C_KEEP])
        modcol = sb("modcol", [P, L, N_MOD * KD, 2])
        sT = sb("sT", [P, KD, 2])
        epsc = sb("epsc", [P, 1])
        ARENA_W = 45900
        arena = sb("arena", [P, ARENA_W])
        ident = CN[:, C_ID:C_ID + P]
        rot = CN[:, C_ROT:C_ROT + P]
        iota = CN[:, C_IOTA:C_IOTA + TOPK]

        class Region:

            def __init__(self, at=0):
                self.at = at

            def __call__(self, *shape):
                n = int(np.prod(shape))
                v = arena[:, self.at:self.at + n]
                self.at += n
                assert self.at <= ARENA_W, self.at
                if len(shape) == 2:
                    return v.rearrange("p (a b) -> p a b", a=shape[0])
                if len(shape) == 3:
                    return v.rearrange("p (a b c) -> p a b c", a=shape[0], b=shape[1])
                return v

        r = Region()
        adaw = r(3, KD, 512)
        adab = r(L * N_MOD * D)
        modrow = r(L * N_MOD * D)
        r = Region()
        mlqk = r(4, T)
        nq = r(4, T)
        nk = r(4, T)
        vband_at = r.at
        vband = r(2 * NBAND + NCT, 512)
        vml_at = r.at
        vml = r(NT, MLH, DV + 1)
        sigo_at = r.at
        sigo = r(NT, 512)
        gcol = r(4 * NT * 8)
        mixer_top = r.at
        r = Region(mixer_top)
        uT = r(KD, T)
        ubT = r(2, KD, P)
        wch = r(3, KD, P)
        wtok_at = r.at
        wtok = r(2, KD, 512)
        wgs = r(KD, 16)
        convs = r(4, 5)
        bgs = r(2)
        cosr = r(SEQ)
        sinr = r(SEQ)
        r = Region(sigo_at)
        raw = r(2, 776)
        ysil = r(2, 512)
        assert r.at <= sigo_at + NT * 512
        r = Region(vml_at)
        cvs = r(2, 776)
        rt = r(2, 512)
        assert r.at <= vml_at + NT * MLH * (DV + 1)
        r = Region(wtok_at + KD * 512)
        li, lf, lnl, cum = [r(T)[0:8, :] for _ in range(4)]
        r = Region(vband_at)
        gF, gB, eF, eB, nMf, nMb = [r(T)[0:8, :] for _ in range(6)]
        r = Region(mixer_top)
        mixT = r(KD, T)
        H = r(NT, 512)
        stat = r(NT * MLH, 2)
        rstd = r(NT * MLH)
        bns = r(4, 6)
        den = r(2, 2)
        rden = r(2, 2)
        nwrow = r(512)
        heads_top = r.at
        negm = r(2, 2, T)
        WD = r(2, N_BLK)
        biasb = r(2, 4, LOC)
        prob = r(2, 512)
        probT = r(2, 512)
        nmax = r(2)
        rsum = r(2)
        rinv = r(2)
        masks = r(NBAND, LOC)
        r = Region()
        wo = r(KD, D)
        g1r = r(2, D)
        ln1r = r(2, D)
        tmp = r(2, D)
        lns = r(2, 2, 6)
        mv = r(2)
        sd = r(2)
        r = Region()
        wk = r(KD, 2 * PH * NKEY)
        wk_flat = wk.rearrange("p k n -> p (k n)")
        wq_at = r.at
        ring = r(RING, 2 * D)
        keys_at = r.at
        u = r(D)
        u_next = r(D)
        uTs = r(KD, P)
        sc2r, sh2r, g2r = r(D), r(D), r(D)
        ln2r = r(2, D)
        junk = r(D)
        prod = junk.bitcast(BF16).rearrange("p (a d) -> p a d", a=2)
        diag = r(2, P)
        zero = r(P)
        idx16 = r(TOPK).bitcast(U32)
        sc = r(2, NKEY)
        cand2 = sc.rearrange("p a b -> p (a b)")
        tv = r(2, TOPK)
        ti = r(2, TOPK).bitcast(U32)
        cand = r(256)
        oh = cand
        tt = r(TOPK)
        pos = r(TOPK).bitcast(U32)
        hilo = r(2, TOPK).bitcast(U32)
        e1 = r(2, TOPK)
        eidx_all = r((NT + 1) * PH * TOPK).bitcast(U32)
        gate_all = r((NT + 1) * PH * TOPK)
        gsum = r(PH)
        dots = r(TOPK)
        acts = r(TOPK)
        lns2 = r(2, 6)
        mv2 = r(2)
        sd2 = r(2)
        wqs = Region(wq_at)(2 * PH, D)
        keys = Region(keys_at)(2 * PH, NKEY)

        ps = [ctx.enter_context(nc.psum_tensor(f"ps{i}", [P, 512], F32)) for i in range(8)]

        sems = {}

        def sem(name):
            if name not in sems:
                sems[name] = ctx.enter_context(nc.semaphore(name))
            return sems[name]

        barrier = sem("stage_barrier")
        bar_n = {}

        def meet(e, who):
            bar_n[who] = bar_n.get(who, 0) + 1
            e.drain()
            e.sem_inc(barrier, 1)
            e.wait_ge(barrier, 5 * bar_n[who])
            e.sem_inc(sem("stage_passed"), 1)

        def reset(e, who, scope, ch=None):
            if who == "dve":
                for name, x in sems.items():
                    if name.startswith(scope):
                        ins = e.sem_clear(x)
                ch.link(ins)
            meet(e, who)

        block = ctx.enter_context(nc.Block())
        cond_of = [0] * NCT + [1] * (NT - NCT)
        mod_v = modrow.rearrange("p (l n) -> p l n", l=L)

        @block.sync
        def _(e):
            e.dma_start(sT[:], cT).then_inc(sem("c_loaded"), 16)
            e.dma_start(adab[0:2, :], ada_b.rearrange("(o l) n -> o (l n)", o=1).to_broadcast([2, L * N_MOD * D])).then_inc(sem("adab_loaded"), 16)
            for n in range(24):
                if n >= 3:
                    e.wait_ge(sem("mod_mm"), n - 2)
                e.dma_start(adaw[:, n % 3], ada_w[n // 12].rearrange("(k p) n -> p k n", p=P)[:, :, (n % 12) * 512:(n % 12 + 1) * 512]).then_inc(sem(f"adaw_loaded{n % 3}"), 16)
                if n == 2:
                    e.dma_start(CN[:], consts[:, 0:C_KEEP]).then_inc(sem("const_loaded"), 16)
                    e.dma_start(X[:], xin.rearrange("(t p) d -> p t d", p=P)).then_inc(sem("x_loaded"), 16)
            e.wait_ge(sem("mod_row"), 24)
            for l in range(L):
                e.dma_start(mod_d[l], mod_v[0:2, l, :]).then_inc(sem("mod_stored"), 16)
            e.wait_ge(sem("mod_stored"), 16 * L)
            e.wait_ge(sem("x_loaded"), 16)
            e.wait_ge(sem("const_loaded"), 16)
            meet(e, "sp")
            for l in range(L):
                jobs = proj_jobs(l)
                e.dma_start(wgs[:], wg[l]).then_inc(sem("L.small_loaded"), 16)
                e.dma_start(bgs[0:8, :], bg[l]).then_inc(sem("L.small_loaded"), 16)
                e.dma_start(convs[:], convw[l]).then_inc(sem("L.small_loaded"), 16)
                e.dma_start(cosr, consts[:, C_COS:C_COS + SEQ]).then_inc(sem("L.rotary_loaded"), 16)
                e.dma_start(sinr, consts[:, C_SIN:C_SIN + SEQ]).then_inc(sem("L.rotary_loaded"), 16)
                wv = w_in[l].rearrange("(k p) n -> p k n", p=P)
                chunks = [COL_ML + c * P for c in range(4)] + [COL_NQ + c * P for c in range(4)] + [COL_NK + c * P for c in range(4)]

                def load_tok(n):
                    col = (COL_V, COL_O, COL_NV)[n]
                    e.dma_start(wtok[:, n % 2], wv[:, :, col:col + 512]).then_inc(sem(f"L.wtok_loaded{n % 2}"), 16)
                load_tok(0)
                for n, col in enumerate(chunks):
                    if n >= 3:
                        e.wait_ge(sem("L.proj_mm"), chunk_end(jobs, n - 3))
                    e.dma_start(wch[:, n % 3], wv[:, :, col:col + P]).then_inc(sem(f"L.wch_loaded{n % 3}"), 16)
                    if n == 3:
                        e.wait_ge(sem("L.negm_ready"), 2)
                        e.dma_start(negm_d[l, 0], nMf[0:4, :]).then_inc(sem("L.negm_stored"), 16)
                        e.dma_start(negm_d[l, 1], nMb[4:8, :]).then_inc(sem("L.negm_stored"), 16)
                e.wait_ge(sem("L.negm_stored"), 32)
                e.wait_ge(sem("L.proj_mm"), last_job(jobs, "X"))
                load_tok(1)
                e.wait_ge(sem("L.proj_mm"), last_job(jobs, "V"))
                load_tok(2)
                meet(e, "sp")
                e.dma_start(nwrow, ml_norm_w[l:l + 1, :].to_broadcast([P, 512])).then_inc(sem("L.nw_loaded"), 16)
                for h in range(MLH):
                    if h >= 2:
                        e.wait_ge(sem("L.arg_ready"), (h - 1) * NT)
                    for d in range(2):
                        e.dma_start(negm[:, h % 2, d, :], negm_d[l, d, h:h + 1, :].to_broadcast([P, T])).then_inc(sem(f"L.negm_loaded{h % 2}"), 16)
                e.dma_start(masks.rearrange("p a b -> p (a b)"), consts[:, C_MASK:C_MASK + NBAND * LOC]).then_inc(sem("L.masks_loaded"), 16)
                for n in range(2 * NBAND):
                    if n >= 2:
                        e.wait_ge(sem("L.bias_used"), 4 * (n - 1))
                    e.dma_start(biasb[:, n % 2], bias[l, n // 2][:, 4 * (n % 2):4 * (n % 2) + 4, :]).then_inc(sem(f"L.bias_loaded{n % 2}"), 16)
                meet(e, "sp")
                e.dma_start(wo[:], w_out[l].rearrange("(k p) n -> p k n", p=P)).then_inc(sem("L.wo_loaded"), 16)
                for cnd in range(2):
                    e.dma_start(g1r[:, cnd], mod_d[l, cnd:cnd + 1, G1 * D:(G1 + 1) * D].to_broadcast([P, D])).then_inc(sem("L.row1_loaded"), 16)
                e.dma_start(ln1r[:].rearrange("p a b -> p (a b)"), ln1[l:l + 1, :].to_broadcast([P, 2 * D])).then_inc(sem("L.row1_loaded"), 16)
                meet(e, "sp")
                e.dma_start(keys[:], keysT[l]).then_inc(sem("L.keys_loaded"), 16)
                for g in range(4):
                    e.dma_start(wqs[:, 4 * g:4 * g + 4, :], wqT[l, g * 4 * P:(g + 1) * 4 * P, :].rearrange("(c p) d -> p c d", p=P)).then_inc(sem(f"L.wq_loaded{g}"), 16)
                cnd = 0 if l < L - 1 else 1

                def mod_row(dst, cnd, v, name):
                    e.dma_start(dst, mod_d[l, cnd:cnd + 1, v * D:(v + 1) * D].to_broadcast([P, D])).then_inc(sem(name), 16)
                mod_row(sc2r, cnd, SC2, "L.row2_loaded")
                mod_row(sh2r, cnd, SH2, "L.row2_loaded")
                mod_row(g2r, cnd, G2, "L.row2_loaded")
                e.dma_start(ln2r[:].rearrange("p a b -> p (a b)"), ln2[l:l + 1, :].to_broadcast([P, 2 * D])).then_inc(sem("L.row2_loaded"), 16)
                meet(e, "sp")
                if l < L - 1:
                    e.wait_ge(sem("L.u_ready"), NCT)
                    mod_row(sc2r, 1, SC2, "L.u_rows_changed")
                    mod_row(sh2r, 1, SH2, "L.u_rows_changed")
                    e.wait_ge(sem("L.acc_free"), NCT + 1)
                    mod_row(g2r, 1, G2, "L.g_row_changed")
                meet(e, "sp")
                reset(e, "sp", "L.")
            e.dma_start(out[0].rearrange("(t p) d -> p t d", p=P), X[:, NCT:NT, :]).then_inc(sem("out_stored"), 16)
            e.wait_ge(sem("out_stored"), 16)

        @block.tensor
        def _(e):
            e.wait_ge(sem("silu_c"), 1)
            for n in range(24):
                e.wait_ge(sem(f"adaw_loaded{n % 3}"), 16 * (n // 3 + 1))
                if n >= 4:
                    e.wait_ge(sem("mod_row"), n - 3)
                for k in range(KD):
                    mm = e.matmul(ps[n % 4][0:2, :], sT[:, k, :], adaw[:, n % 3, k, :], start=(k == 0), stop=(k == KD - 1))
                mm.then_inc(sem("mod_mm"), 1)
            e.wait_ge(sem("mod_row"), 24)
            e.wait_ge(sem("const_loaded"), 16)
            for l in range(L):
                for c in range(N_MOD * KD):
                    mm = e.transpose(ps[4 + l][:, 2 * c:2 * c + 2], mod_v[0:2, l, c * P:(c + 1) * P], ident[0:2, 0:2])
                mm.then_inc(sem("modcol_t"), 1)
            e.wait_ge(sem("x_loaded"), 16)
            meet(e, "pe")
            for l in range(L):
                q_ctx = l < L - 1
                t0 = 0 if q_ctx else NCT
                jobs = proj_jobs(l)
                count = {"v": 0, "a": 0}
                freed = []
                n_t = {"v": sum(j[0] == "T" and j[3] == "v" for j in jobs), "a": sum(j[0] == "T" and j[3] == "a" for j in jobs)}
                chunk_no = -1
                for n, (kind, i, part, ev) in enumerate(jobs):
                    if n >= 8:
                        w, val = freed[n - 8]
                        e.wait_ge(sem(f"L.proj_evac_{w}"), val)
                    count[ev] += 1
                    freed.append((ev, count[ev]))
                    bank = ps[n % 8]
                    cols = slice(CTX, T) if part == "x" else slice(0, CTX)
                    width = SEQ if part == "x" else CTX
                    if kind == "T":
                        tiles = range(NCT, NT) if part == "x" else range(NCT)
                        for a, t in enumerate(tiles):
                            mm = e.transpose(bank[:, a * P:(a + 1) * P], X[:, t, i * P:(i + 1) * P], ident)
                    elif kind == "G":
                        if i == 0 and part == "x":
                            e.wait_ge(sem("L.proj_evac_v"), n_t["v"])
                            e.wait_ge(sem("L.proj_evac_a"), n_t["a"])
                            e.wait_ge(sem("L.small_loaded"), 48)
                        for k in range(KD):
                            mm = e.matmul(bank[0:8, 0:width], wgs[:, k, 8 * i:8 * i + 8], uT[:, k, cols], start=(k == 0), stop=(k == KD - 1))
                    elif kind in "MQK":
                        c = i + {"M": 0, "Q": 4, "K": 8}[kind]
                        e.wait_ge(sem(f"L.wch_loaded{c % 3}"), 16 * (c // 3 + 1))
                        for k in range(KD):
                            mm = e.matmul(bank[:, 0:width], wch[:, c % 3, k, :], uT[:, k, cols], start=(k == 0), stop=(k == KD - 1))
                    elif kind == "R":
                        e.wait_ge(sem("L.silu_done"), i + 1)
                        mm = e.matmul(bank[:], rot, ysil[:, i % 2, :], start=True, stop=True)
                    elif kind == "X":
                        e.wait_ge(sem("L.gates_done"), 1)
                        for a, g in enumerate((gF, gB, eF, eB)):
                            for t in range(NT):
                                o = (a * NT + t) * 8
                                mm = e.transpose(bank[:, o:o + 8], g[:, t * P:(t + 1) * P], ident[0:8, 0:8])
                    elif kind in "VO":
                        s = "VO".index(kind)
                        if i == (0 if kind == "V" else t0):
                            e.wait_ge(sem(f"L.wtok_loaded{s}"), 16)
                        for k in range(KD):
                            mm = e.matmul(bank[:], uT[:, k, i * P:(i + 1) * P], wtok[:, s, k, :], start=(k == 0), stop=(k == KD - 1))
                    else:
                        if i == 0:
                            e.wait_ge(sem("L.wtok_loaded0"), 32)
                        if i < 2 * NBAND:
                            e.wait_ge(sem("L.band_ready"), i + 1)
                        for k in range(KD):
                            lhs = ubT[:, i % 2, k, :] if i < 2 * NBAND else uT[:, k, (i - 2 * NBAND) * P:(i - 2 * NBAND + 1) * P]
                            mm = e.matmul(bank[:], lhs, wtok[:, 0, k, :], start=(k == 0), stop=(k == KD - 1))
                    mm.then_inc(sem("L.proj_mm"), 1)
                meet(e, "pe")
                for h in range(MLH):
                    o = (h % 2) * DK
                    for i in range(NT):
                        m = h * NT + i
                        if m >= 2:
                            e.wait_ge(sem("L.w_ready"), m - 1)
                        kk = mlqk[o:o + DK, 2 + h // 2, i * P:(i + 1) * P]
                        mm = e.matmul(ps[m % 2][:], kk, mlqk[o:o + DK, h // 2, CTX:T], start=True, stop=True)
                        if i < NCT and q_ctx:
                            mm = e.matmul(ps[2 + m % 2][:, 0:CTX], kk, mlqk[o:o + DK, h // 2, 0:CTX], start=True, stop=True)
                        mm.then_inc(sem("L.s_ready"), 1)
                    e.wait_ge(sem("L.w_ready"), (h + 1) * NT)
                    for j in range(t0, NT):
                        m = h * (NT - t0) + j - t0
                        if m >= 2:
                            e.wait_ge(sem("L.h_done"), m - 1)
                        bank = ps[4 + m % 2]
                        for d, src, at in ((0, list(range(j + 1)), at_f), (1, b_sources(j), at_b)):
                            for i in src:
                                mm = e.matmul(bank[:, d * (DV + 1):(d + 1) * (DV + 1)], WD[:, d, at(i, j):at(i, j) + P],
                                              vml[:, i, h, :], start=(i == src[0]), stop=(i == src[-1]))
                        mm.then_inc(sem("L.num_ready"), 1)
                for t in range(t0, NT):
                    e.wait_ge(sem("L.mlout"), t - t0 + 1)
                    if t >= t0 + 2:
                        e.wait_ge(sem("L.mlT_evac"), t - t0 - 1)
                    for h in range(MLH):
                        mm = e.transpose(ps[6 + t % 2][:, h * P:(h + 1) * P], H[:, t, h * P:(h + 1) * P], ident)
                    mm.then_inc(sem("L.mlT"), 1)
                att = attention_jobs(l)

                def scores(n):
                    b, h = att[n]
                    if n == 0:
                        e.wait_ge(sem("L.w_ready"), MLH * NT)
                    if n >= 2:
                        e.wait_ge(sem("L.p_exp"), n - 1)
                    o, c = (h % 2) * DH, h // 2
                    q = nq[o:o + DH, c, CTX + b * P:CTX + (b + 1) * P] if b < NBAND else nq[o:o + DH, c, (b - NBAND) * P:(b - NBAND + 1) * P]
                    if b < NBAND:
                        kb = nk[o:o + DH, c, CTX:T].rearrange("p (r w) -> p r w", w=GRID_W)[:, :, BAND_LO[b]:BAND_LO[b] + BAND]
                        e.matmul(ps[n % 2][:, 0:LOC], q, kb, start=True, stop=True)
                    e.matmul(ps[n % 2][:, LOC:512], q, nk[o:o + DH, c, 0:CTX], start=True, stop=True).then_inc(sem("L.s_att"), 1)

                def turn(n):
                    e.wait_ge(sem("L.p_ready"), n + 1)
                    if n >= 2:
                        e.wait_ge(sem("L.pT_ready"), n - 1)
                    for a in range(0 if att[n][0] < NBAND else 2, 4):
                        mm = e.transpose(ps[2 + n % 2][:, a * P:(a + 1) * P], prob[:, n % 2, a * P:(a + 1) * P], ident)
                    mm.then_inc(sem("L.pT_mm"), 1)

                def values(n):
                    b, h = att[n]
                    e.wait_ge(sem("L.pT_ready"), n + 1)
                    if n == 0:
                        e.wait_ge(sem("L.h_done"), MLH * (NT - t0))
                    if n >= 2:
                        e.wait_ge(sem("L.o_att"), n - 1)
                    first = 0 if b < NBAND else 2
                    for a in range(first, 4):
                        vt = 2 * b + a if a < 2 else 2 * NBAND + a - 2
                        mm = e.matmul(ps[4 + n % 2][:, 0:P], vband[:, vt, (h // 2) * P:(h // 2 + 1) * P],
                                      probT[:, n % 2, a * P:(a + 1) * P], start=(a == first), stop=(a == 3))
                    mm.then_inc(sem("L.o_mm"), 1)
                for n in range(len(att) + 2):
                    if n < len(att):
                        scores(n)
                    if 1 <= n <= len(att):
                        turn(n - 1)
                    if n >= 2:
                        values(n - 2)
                meet(e, "pe")
                e.wait_ge(sem("L.wo_loaded"), 16)
                for t in range(t0, NT):
                    m = t - t0
                    if m >= 4:
                        e.wait_ge(sem("L.y_read"), m - 3)
                    for hf in range(2):
                        for k in range(KD):
                            mm = e.matmul(ps[2 * (m % 4) + hf][:], mixT[:, k, t * P:(t + 1) * P], wo[:, k, hf * 512:(hf + 1) * 512],
                                          start=(k == 0), stop=(k == KD - 1))
                    mm.then_inc(sem("L.y_ready"), 1)
                meet(e, "pe")
                e.wait_ge(sem("L.keys_loaded"), 16)
                for n in range(4 * PH):
                    c, j = n // 2, n % 2
                    if n % 8 == 0:
                        e.wait_ge(sem(f"L.wq_loaded{c // 4}"), 16)
                    if n >= 8:
                        e.wait_ge(sem(f"L.wk_evac_{'av'[j]}"), (n - 8) // 2 + 1)
                    for k in range(4):
                        mm = e.matmul(ps[n % 8][:, k * P:(k + 1) * P], wqs[:, c, (4 * j + k) * P:(4 * j + k + 1) * P], keys[:, c, :], start=True, stop=True)
                    mm.then_inc(sem("L.wk_mm"), 1)
                meet(e, "pe")
                nt = NT - t0

                def turn_u(t):
                    e.wait_ge(sem("L.u_ready"), t + 1)
                    for k in range(KD):
                        mm = e.transpose(ps[4 + k // 4][:, (k % 4) * P:(k % 4 + 1) * P], u_next[:, k * P:(k + 1) * P], ident)
                    mm.then_inc(sem("L.uT_mm"), 1)

                def key_scores(unit, h, lead):
                    if lead < 2 or unit >= 1:
                        e.wait_ge(sem("L.route_read"), unit + 2 - lead)
                    bank = ps[2 + (unit % 2 if lead == 2 else 0)]
                    for k in range(KD):
                        mm = e.matmul(bank[:, 0:2 * NKEY], uTs[:, k, :], wk_flat[:, bass.ds(h * (2 * NKEY) + k * (2 * PH * NKEY), 2 * NKEY)],
                                      start=(k == 0), stop=(k == KD - 1))
                    mm.then_inc(sem("L.key_mm"), 1)

                def weigh(n, k):
                    e.wait_ge(sem("L.diag_ready"), n + (k + 1))
                    for hf in range(2):
                        mm = e.matmul(ps[hf][:], diag[:, k % 2, :], ring[:, k % RING, D + hf * 512:D + (hf + 1) * 512],
                                      start=False, stop=False, skip_group_check=True)
                    mm.then_inc(sem("L.slot_done"), 1)

                def tile(t, more):
                    e.wait_ge(sem("L.acc_free"), t + 1)
                    for hf in range(2):
                        e.matmul(ps[hf][:], zero, ln2r[:, 0, 0:512], start=True, stop=False, skip_group_check=True)
                    if more:
                        turn_u(t + 1)
                    with e.Fori(0, PH - LEAD) as h:
                        key_scores(t * PH + h + LEAD, h + LEAD, 1)
                        for k in range(TOPK):
                            weigh(t * (PH * TOPK) + h * TOPK, k)
                    if more:
                        e.wait_ge(sem("L.uT_ready"), t + 2)
                        e.sem_inc(sem("pe_token"), 1)
                    with e.Fori(0, LEAD) as h:
                        if more:
                            key_scores(t * PH + h + PH, h, 1)
                        for k in range(TOPK):
                            weigh(t * (PH * TOPK) + h * TOPK + (PH - LEAD) * TOPK, k)
                    for hf in range(2):
                        mm = e.matmul(ps[hf][:], zero, ln2r[:, 0, 0:512], start=False, stop=True, skip_group_check=True)
                    mm.then_inc(sem("L.acc_ready"), 1)

                e.wait_ge(sem("L.row2_loaded"), 64)
                e.wait_ge(sem("L.zero_set"), 2)
                turn_u(0)
                e.wait_ge(sem("L.uT_ready"), 1)
                for h in range(LEAD):
                    key_scores(h, h, 2)
                for ta, tb in tile_spans(l):
                    if tb - ta > 1:
                        with e.Fori(ta, tb) as t:
                            tile(t, True)
                    else:
                        tile(ta, tb < nt)
                meet(e, "pe")
                reset(e, "pe", "L.")

        @block.scalar
        def _(e):
            ch = Chain(e, sem("act_chain"))
            e.wait_ge(sem("c_loaded"), 16)
            e.activation(sT[:], sT[:], ACT.Silu).then_inc(sem("silu_c"), 1)
            meet(e, "act")
            for l in range(L):
                q_ctx = l < L - 1
                t0 = 0 if q_ctx else NCT
                jobs = proj_jobs(l)
                n_conv = [0]

                def silu(c):
                    e.wait_ge(sem("L.conv_done"), c + 1)
                    if c >= 2:
                        e.wait_ge(sem("L.rope_done"), c - 1)
                    if q_ctx or c >= 2:
                        e.activation(mlqk[:, c, 0:CTX], cvs[:, c % 2, 0:CTX], ACT.Silu).then_inc(sem("L.silu_ctx"), 1)
                    e.activation(ysil[:, c % 2, :], cvs[:, c % 2, 260:772], ACT.Silu).then_inc(sem("L.silu_done"), 1)

                done = 0
                for n, (kind, i, part, ev) in enumerate(jobs):
                    if ev != "a":
                        continue
                    bank = ps[n % 8]
                    width = SEQ if part == "x" else CTX
                    tc = slice(CTX, T) if part == "x" else slice(0, CTX)
                    if kind == "M" and part == "x" and i >= 2:
                        e.wait_ge(sem("L.conv_done"), i - 1)
                    if kind in "VO":
                        e.wait_ge(sem("L.rope_done"), 4)
                    e.wait_ge(sem("L.proj_mm"), n + 1)
                    if kind == "T":
                        cnd = 1 if part == "x" else 0
                        ins = e.activation(uT[:, i, tc], bank[:, 0:width], ACT.Identity, scale=modcol[:, l, SC1 * KD + i, cnd:cnd + 1],
                                           bias=modcol[:, l, SH1 * KD + i, cnd:cnd + 1])
                    elif kind == "G":
                        if i == 0 and part == "x":
                            e.wait_ge(sem("L.small_loaded"), 48)
                        ins = e.activation((li, lf)[i][:, tc], bank[0:8, 0:width], ACT.Identity, bias=bgs[0:8, i:i + 1])
                    elif kind == "M":
                        at = 262 if part == "x" else 2
                        ins = e.activation(raw[:, i % 2, at:at + width], bank[:, 0:width], ACT.Copy)
                    elif kind == "Q":
                        if part == "x":
                            ins = e.activation(nq[:, i, CTX:T].rearrange("p (b r c) -> p r b c", b=NBAND, r=ROWS),
                                               bank[:, :].rearrange("p (r b c) -> p r b c", r=ROWS, b=NBAND), ACT.Copy, scale=DH ** -0.5)
                        else:
                            ins = e.activation(nq[:, i, 0:CTX], bank[:, 0:CTX], ACT.Copy, scale=DH ** -0.5)
                    elif kind == "K":
                        ins = e.activation(nk[:, i, tc], bank[:, 0:width], ACT.Copy)
                    elif kind == "V":
                        ins = e.activation(vml[:, i, :, 0:DV], bank[:, :].rearrange("p (h d) -> p h d", h=MLH), ACT.Copy)
                    elif kind == "O":
                        ins = e.activation(sigo[:, i, :], bank[:], ACT.Sigmoid)
                    ins.then_inc(sem("L.proj_evac_a"), 1)
                    done += 1
                    if kind == "G" and i == 1 and part == "c":
                        e.wait_ge(sem("L.proj_evac_a"), done)
                        ch.link(e.activation(lnl, lf, ACT.Abs))
                        ch.link(e.activation(lnl, lnl, ACT.Exp, scale=-1.0))
                        e.activation(lnl, lnl, ACT.Ln, bias=1.0).then_inc(sem("L.ln_done"), 1)
                        e.wait_ge(sem("L.negm_ready"), 2)
                        ch.link(e.activation(eF, eF, ACT.Exp, scale=-1.0))
                        e.activation(eB, eB, ACT.Exp, scale=-1.0).then_inc(sem("L.gates_done"), 1)
                    if kind == "M" and i >= 1 and (part == "c" or (not q_ctx and i < 2)):
                        silu(i - 1)
                        if i == 3:
                            silu(3)
                meet(e, "act")
                for h in range(MLH):
                    for i in range(NT):
                        m = h * NT + i
                        e.wait_ge(sem("L.arg_ready"), m + 1)
                        fa, fn = at_f(i, f_start(i, t0)), (NT - f_start(i, t0)) * P
                        ch.link(e.activation(WD[:, 0, fa:fa + fn], WD[:, 0, fa:fa + fn], ACT.Exp))
                        ba, bn = OFF_B[i], b_len(i, t0)
                        e.activation(WD[:, 1, ba:ba + bn], WD[:, 1, ba:ba + bn], ACT.Exp).then_inc(sem("L.decay_ready"), 1)
                e.wait_ge(sem("L.h_done"), MLH * (NT - t0))
                e.wait_ge(sem("eps_set"), 1)
                e.activation(rstd[:, t0 * MLH:], stat[:, t0 * MLH:, 1], ACT.Sqrt, bias=epsc[:, 0:1]).then_inc(sem("L.hsd"), 1)
                for t in range(t0, NT):
                    e.wait_ge(sem("L.mlT"), t - t0 + 1)
                    e.activation(mixT[:, 0:MLH, t * P:(t + 1) * P], ps[6 + t % 2][:, :].rearrange("p (h t) -> p h t", h=MLH), ACT.Copy).then_inc(sem("L.mlT_evac"), 1)
                att = attention_jobs(l)
                for n in range(len(att) + 1):
                    if n < len(att):
                        b, h = att[n]
                        a0 = 0 if b < NBAND else LOC
                        e.wait_ge(sem("L.nmax_ready"), n + 1)
                        if n >= 2:
                            e.wait_ge(sem("L.pT_mm"), n - 1)
                        e.activation(prob[:, n % 2, a0:512], ps[n % 2][:, a0:512], ACT.Exp, bias=nmax[:, n % 2:n % 2 + 1],
                                     accum_out=rsum[:, n % 2:n % 2 + 1]).then_inc(sem("L.p_exp"), 1)
                    if n >= 1:
                        m = n - 1
                        a0 = 0 if att[m][0] < NBAND else LOC
                        e.wait_ge(sem("L.pT_mm"), m + 1)
                        if m >= 2:
                            e.wait_ge(sem("L.o_mm"), m - 1)
                        e.activation(probT[:, m % 2, a0:512], ps[2 + m % 2][:, a0:512], ACT.Copy).then_inc(sem("L.pT_ready"), 1)
                meet(e, "act")
                for t in range(t0, NT):
                    e.wait_ge(sem("L.var1"), t - t0 + 1)
                    e.activation(sd[:, 0:1], mv[:, 1:2], ACT.Sqrt, bias=epsc[:, 0:1]).then_inc(sem("L.sd1"), 1)
                meet(e, "act")
                for n in range(0, 4 * PH, 2):
                    c = n // 2
                    e.wait_ge(sem("L.wk_mm"), n + 1)
                    e.activation(wk[:, 0:4, c * NKEY:(c + 1) * NKEY], ps[n % 8][:, :].rearrange("p (k n) -> p k n", k=4), ACT.Copy).then_inc(sem("L.wk_evac_a"), 1)
                meet(e, "act")
                nt = NT - t0

                def keep_uT(t):
                    e.wait_ge(sem("L.uT_mm"), t + 1)
                    e.sem_inc(sem("act_token"), 1)
                    e.wait_ge(sem("L.key_mm"), t * PH)
                    e.sem_inc(sem("act_token"), 1)
                    for j in range(2):
                        ins = e.activation(uTs[:, 4 * j:4 * j + 4, :], ps[4 + j][:, :].rearrange("p (k n) -> p k n", k=4), ACT.Copy)
                    ins.then_inc(sem("L.uT_ready"), 1)

                def gate_exp(un):
                    e.wait_ge(sem("L.route_done"), un + 1)
                    e.sem_inc(sem("act_token"), 1)
                    e.activation(gate_all[:, bass.ds(un * TOPK, TOPK)], gate_all[:, bass.ds(un * TOPK, TOPK)], ACT.Exp).then_inc(sem("L.gexp"), 1)

                def unit(un, route):
                    for k in range(TOPK):
                        e.wait_ge(sem("L.dot_done"), un * TOPK + (k + 1))
                        e.activation(acts[:, k:k + 1], dots[:, k:k + 1], ACT.Gelu_apprx_tanh).then_inc(sem("L.act_done"), 1)
                        if k == EXP_AT and route:
                            gate_exp(un + LEAD)

                def tile(t, more):
                    with e.Fori(0, PH - LEAD) as h:
                        unit(t * PH + h, True)
                    if more:
                        keep_uT(t + 1)
                    with e.Fori(0, LEAD) as h:
                        unit(t * PH + h + (PH - LEAD), more)
                    e.wait_ge(sem("L.var2"), t + 1)
                    e.activation(sd2[:, 0:1], mv2[:, 1:2], ACT.Sqrt, bias=epsc[:, 0:1]).then_inc(sem("L.sd2"), 1)

                e.wait_ge(sem("L.uT_mm"), 1)
                for j in range(2):
                    ins = e.activation(uTs[:, 4 * j:4 * j + 4, :], ps[4 + j][:, :].rearrange("p (k n) -> p k n", k=4), ACT.Copy)
                ins.then_inc(sem("L.uT_ready"), 1)
                for h in range(LEAD):
                    gate_exp(h)
                for ta, tb in tile_spans(l):
                    if tb - ta > 1:
                        with e.Fori(ta, tb) as t:
                            tile(t, True)
                    else:
                        tile(ta, tb < nt)
                meet(e, "act")
                reset(e, "act", "L.")

        @block.gpsimd
        def _(e):
            e.memset(epsc[:], EPS).then_inc(sem("eps_set"), 1)
            meet(e, "pool")
            for l in range(L):
                q_ctx = l < L - 1
                jobs = proj_jobs(l)
                n_t = {w: sum(j[0] == "T" and j[3] == w for j in jobs) for w in "va"}
                first_b = [n for n, j in enumerate(jobs) if j[0] == "B"][0]
                e.wait_ge(sem("L.proj_evac_v"), n_t["v"])
                e.wait_ge(sem("L.proj_evac_a"), n_t["a"])
                for n in range(2 * NBAND):
                    b, a = n // 2, n % 2
                    if n >= 2:
                        e.wait_ge(sem("L.proj_mm"), first_b + n - 1)
                    lat = uT[:, :, CTX:T].rearrange("p k (r w) -> p k r w", w=GRID_W)
                    e.tensor_copy(ubT[:, n % 2].rearrange("p k (r w) -> p k r w", r=4),
                                  lat[:, :, 4 * a:4 * a + 4, BAND_LO[b]:BAND_LO[b] + BAND]).then_inc(sem("L.band_ready"), 1)
                meet(e, "pool")
                e.wait_ge(sem("L.masks_loaded"), 16)
                for n in range(2 * NBAND):
                    e.wait_ge(sem(f"L.bias_loaded{n % 2}"), 16 * (n // 2 + 1))
                    for q in range(4):
                        ins = e.tensor_tensor(biasb[:, n % 2, q, :], biasb[:, n % 2, q, :], masks[:, n // 2, :], ALU.add)
                    ins.then_inc(sem("L.bias_ready"), 1)
                meet(e, "pool")
                meet(e, "pool")
                meet(e, "pool")
                nt = NT - (0 if q_ctx else NCT)
                e.sem_inc(sem("L.slot_done"), RING)
                with e.Fori(0, nt * PH) as un:
                    for k in range(TOPK):
                        if k % RING == 0:
                            e.wait_ge(sem("L.idx_ready"), un * 2 + (k // RING + 1))
                            e.sem_inc(sem("pool_token"), 1)
                        e.wait_ge(sem("L.slot_done"), un * TOPK + (k + 1))
                        e.sem_inc(sem("pool_token"), 1)
                        e.indirect_dma_start(ring[:, k % RING, :], None, updown,
                                             bass.IndirectOffsetOnAxis(ap=idx16[:, k:k + 1], axis=0)).then_inc(sem(f"rows{k % RING}"), 16)
                meet(e, "pool")
                reset(e, "pool", "L.")

        @block.vector
        def _(e):
            ch = Chain(e, sem("dve_chain"))
            lc = Chain(e, sem("dve_loop_chain"), sem("dve_restarts"))
            e.wait_ge(sem("adab_loaded"), 16)
            for n in range(24):
                e.wait_ge(sem("mod_mm"), n + 1)
                one = 1.0 if (n % 12) // 2 in (SC1, SC2) else 0.0
                e.scalar_tensor_tensor(out=modrow[0:2, n * 512:(n + 1) * 512], in0=ps[n % 4][0:2, :], scalar=one,
                                       in1=adab[0:2, n * 512:(n + 1) * 512], op0=ALU.add, op1=ALU.add).then_inc(sem("mod_row"), 1)
            e.wait_ge(sem("modcol_t"), L)
            for l in range(L):
                e.tensor_copy(modcol[:, l].rearrange("p a b -> p (a b)"), ps[4 + l][:, 0:2 * N_MOD * KD])
            meet(e, "dve")
            for l in range(L):
                q_ctx = l < L - 1
                t0 = 0 if q_ctx else NCT
                jobs = proj_jobs(l)
                for a in range(2):
                    for c0, c1 in ((0, 2), (258, 262), (774, 776)):
                        ins = e.memset(raw[:, a, c0:c1], 0.0)
                ch.link(ins)
                evac_no = ordinals(jobs)

                def conv(c):
                    lo = 0 if (q_ctx or c >= 2) else 260
                    for part in "xc":
                        if ("M", c, part, "a") in jobs:
                            e.wait_ge(sem("L.proj_evac_a"), evac_no[jobs.index(("M", c, part, "a"))])
                    if c >= 2:
                        e.wait_ge(sem("L.silu_done"), c - 1)
                    cvb = cvs[:, c % 2, lo:772]
                    ch.link(e.tensor_scalar(cvb, raw[:, c % 2, lo:772], convs[:, c, 0:1], None, ALU.mult))
                    for w in range(1, 5):
                        ins = e.scalar_tensor_tensor(out=cvb, in0=raw[:, c % 2, lo + w:772 + w], scalar=convs[:, c, w:w + 1], in1=cvb, op0=ALU.mult, op1=ALU.add)
                        if w < 4:
                            ch.link(ins)
                    ins.then_inc(sem("L.conv_done"), 1)

                def gates():
                    e.wait_ge(sem("L.ln_done"), 1)
                    ch.link(e.scalar_tensor_tensor(out=lf, in0=lf, scalar=0.0, in1=lnl, op0=ALU.min, op1=ALU.subtract))
                    ch.link(e.memset(lnl, 1.0))
                    for g, F, nM, back in ((gF, eF, nMf, False), (gB, eB, nMb, True)):
                        parts = [(0, CTX), (CTX, T)] if back else [(0, T)]
                        for what, src, dst in (("sum", lf, F), ("max", g, cum)):
                            if what == "max":
                                ch.link(e.tensor_tensor(g, li, F, ALU.subtract))
                            start = 0.0
                            for a, b in parts:
                                v = [x[:, a:b][:, ::-1] if back else x[:, a:b] for x in (lnl if what == "sum" else src, src, dst)]
                                ops = (ALU.mult, ALU.add) if what == "sum" else (ALU.max, ALU.max)
                                ch.link(e.tensor_tensor_scan(v[2], v[0], v[1], start, *ops))
                                start = dst[:, a:a + 1] if back else None
                        ch.link(e.tensor_tensor(F, F, cum, ALU.add))
                        e.tensor_scalar(nM, cum, -1.0, None, ALU.mult).then_inc(sem("L.negm_ready"), 1)
                        e.wait_ge(sem("L.negm_ready"), 2 if back else 1)

                for n, (kind, i, part, ev) in enumerate(jobs):
                    if kind == "M" and part == "x" and i >= 1:
                        conv(i - 1)
                    if kind == "M" and part == "x" and i == 0:
                        gates()
                    if kind == "Q" and i == 0 and part == "x":
                        conv(3)
                    if ev != "v":
                        continue
                    bank = ps[n % 8]
                    width = SEQ if part == "x" else CTX
                    tc = slice(CTX, T) if part == "x" else slice(0, CTX)
                    if kind in "VB":
                        e.wait_ge(sem("L.rope_done"), 4)
                    e.wait_ge(sem("L.proj_mm"), n + 1)
                    if kind == "T":
                        ins = e.tensor_scalar(uT[:, i, tc], bank[:, 0:width], modcol[:, l, SC1 * KD + i, 1:2], modcol[:, l, SH1 * KD + i, 1:2], ALU.mult, ALU.add)
                    elif kind == "X":
                        ins = e.tensor_copy(gcol, bank[:, 0:4 * NT * 8])
                    elif kind == "R":
                        e.wait_ge(sem("L.silu_done"), i + 1)
                        if i == 0:
                            e.wait_ge(sem("L.rotary_loaded"), 32)
                        e.tensor_tensor(rt[:, 0, :], ysil[:, i % 2, :], cosr, ALU.mult)
                        ch.link(e.tensor_tensor(rt[:, 1, :], bank[:], sinr, ALU.mult))
                        ch.link(e.tensor_tensor(mlqk[:, i, CTX:T], rt[:, 0, :], rt[:, 1, :], ALU.add))
                        e.sem_inc(sem("L.rope_done"), 1)
                        e.sem_inc(sem("L.proj_evac_v"), 1)
                        continue
                    elif kind == "Q":
                        if part == "x":
                            ins = e.tensor_scalar(nq[:, i, CTX:T].rearrange("p (b r c) -> p r b c", b=NBAND, r=ROWS),
                                                  bank[:, :].rearrange("p (r b c) -> p r b c", r=ROWS, b=NBAND), DH ** -0.5, None, ALU.mult)
                        else:
                            ins = e.tensor_scalar(nq[:, i, 0:CTX], bank[:, 0:CTX], DH ** -0.5, None, ALU.mult)
                    elif kind == "K":
                        ins = e.tensor_copy(nk[:, i, tc], bank[:, 0:width])
                    elif kind == "V":
                        ins = e.tensor_copy(vml[:, i, :, 0:DV], bank[:, :].rearrange("p (h d) -> p h d", h=MLH))
                    else:
                        ins = e.tensor_copy(vband[:, i, :], bank[:])
                    ins.then_inc(sem("L.proj_evac_v"), 1)
                e.memset(vml[:, :, :, DV:DV + 1].rearrange("p a b c -> p (a b) c"), 1.0)
                meet(e, "dve")
                def args(h, i):
                    fs = f_start(i, t0)
                    fa, fn = at_f(i, fs), (NT - fs) * P
                    nm = negm[:, h % 2]
                    e.tensor_scalar(WD[:, 0, fa:fa + fn], nm[:, 0, fs * P:T], gc[:, 0, i, h:h + 1], 0.0, ALU.add, ALU.min)
                    ba = OFF_B[i]
                    gb = gc[:, 1, i, 4 + h:5 + h]
                    if i < NCT:
                        ins = e.tensor_scalar(WD[:, 1, ba:ba + SEQ], nm[:, 1, CTX:T], gb, 0.0, ALU.add, ALU.min)
                        if q_ctx:
                            n = (i + 1) * P
                            ins = e.tensor_scalar(WD[:, 1, ba + SEQ:ba + SEQ + n], nm[:, 1, 0:n], gb, 0.0, ALU.add, ALU.min)
                    else:
                        n = (i - 1) * P
                        ins = e.tensor_scalar(WD[:, 1, ba:ba + n], nm[:, 1, CTX:CTX + n], gb, 0.0, ALU.add, ALU.min)
                    ins.then_inc(sem("L.arg_ready"), 1)

                def apply(h, i):
                    m = h * NT + i
                    e.wait_ge(sem("L.decay_ready"), m + 1)
                    e.wait_ge(sem("L.s_ready"), m + 1)
                    if i >= t0:
                        e.tensor_tensor(WD[:, 0, at_f(i, i):at_f(i, i) + P], WD[:, 0, at_f(i, i):at_f(i, i) + P], CN[:, C_TRI:C_TRI + P], ALU.mult)
                        ch.link(e.tensor_tensor(WD[:, 1, at_b(i, i):at_b(i, i) + P], WD[:, 1, at_b(i, i):at_b(i, i) + P], CN[:, C_TRI + P:C_TRI + 2 * P], ALU.mult))
                    SX, SC = ps[m % 2], ps[2 + m % 2]
                    work = []
                    xs = max(i, NCT)
                    work.append((0, at_f(i, xs), SX, (xs - NCT) * P, (NT - xs) * P))
                    work.append((1, OFF_B[i], SX, 0, SEQ if i < NCT else (i - 1) * P))
                    if i < NCT and q_ctx:
                        work.append((0, at_f(i, i), SC, i * P, (NCT - i) * P))
                        work.append((1, OFF_B[i] + SEQ, SC, 0, (i + 1) * P))
                    for d, wa, S, sa, n in work:
                        ins = e.scalar_tensor_tensor(out=WD[:, d, wa:wa + n], in0=S[:, sa:sa + n], scalar=DK ** -0.5, in1=WD[:, d, wa:wa + n], op0=ALU.mult, op1=ALU.mult)
                    ins.then_inc(sem("L.w_ready"), 1)

                gc = gcol.rearrange("p (a t r) -> p a t r", a=4, t=NT)
                for h in range(MLH):
                    e.wait_ge(sem(f"L.negm_loaded{h % 2}"), 32 * (h // 2 + 1))
                    if h >= 1:
                        e.wait_ge(sem("L.num_ready"), h * (NT - t0))
                    args(h, 0)
                    for i in range(NT):
                        if i + 1 < NT:
                            args(h, i + 1)
                        apply(h, i)
                    for j in range(t0, NT):
                        m = h * (NT - t0) + j - t0
                        bank = ps[4 + m % 2]
                        e.wait_ge(sem("L.num_ready"), m + 1)
                        o = (2 * NT + j) * 8 + h
                        dn = bank[:, DV:2 * DV + 2:DV + 1]
                        ch.link(e.scalar_tensor_tensor(out=den[:, 1, :], in0=dn, scalar=-1.0, in1=gcol[:, o:o + NT * 8 + 5:NT * 8 + 4], op0=ALU.mult, op1=ALU.max))
                        ch.link(e.tensor_tensor(den[:, 0, :], dn, den[:, 1, :], ALU.max))
                        ch.link(e.reciprocal(rden[:, 0, :], den[:, 0, :]))
                        Hj = H[:, j, h * DV:(h + 1) * DV]
                        ch.link(e.tensor_scalar(Hj, bank[:, 0:DV], rden[:, 0, 0:1], None, ALU.mult))
                        ch.link(e.scalar_tensor_tensor(out=Hj, in0=bank[:, DV + 1:2 * DV + 1], scalar=rden[:, 0, 1:2], in1=Hj, op0=ALU.mult, op1=ALU.add))
                        ch.link(e.bn_stats(bns[:, 0, :], Hj))
                        e.bn_aggr(stat[:, j * MLH + h, :], bns[:, 0, :]).then_inc(sem("L.h_done"), 1)
                e.wait_ge(sem("L.hsd"), 1)
                e.wait_ge(sem("L.nw_loaded"), 16)
                ch.link(e.reciprocal(rstd[:, t0 * MLH:], rstd[:, t0 * MLH:]))
                for t in range(t0, NT):
                    for h in range(MLH):
                        n = t * MLH + h
                        ins = e.tensor_scalar(H[:, t, h * DV:(h + 1) * DV], H[:, t, h * DV:(h + 1) * DV], stat[:, n, 0:1], rstd[:, n:n + 1], ALU.subtract, ALU.mult)
                    ch.link(ins)
                    ch.link(e.tensor_tensor(H[:, t, :], H[:, t, :], nwrow, ALU.mult))
                    e.tensor_tensor(H[:, t, :], H[:, t, :], sigo[:, t, :], ALU.mult).then_inc(sem("L.mlout"), 1)
                att = attention_jobs(l)
                for n in range(len(att) + 2):
                    if n < len(att):
                        b, h = att[n]
                        a0 = 0 if b < NBAND else LOC
                        e.wait_ge(sem("L.s_att"), n + 1)
                        if n >= 2:
                            e.wait_ge(sem("L.p_exp"), n - 1)
                        if b < NBAND:
                            half = 2 * b + h // 4
                            e.wait_ge(sem("L.bias_ready"), half + 1)
                            e.tensor_tensor(ps[n % 2][:, 0:LOC], ps[n % 2][:, 0:LOC], biasb[:, half % 2, h % 4, :], ALU.add).then_inc(sem("L.bias_used"), 1)
                            e.wait_ge(sem("L.bias_used"), n + 1)
                        e.tensor_reduce(nmax[:, n % 2:n % 2 + 1], ps[n % 2][:, a0:512], AX.X, ALU.max, negate=True).then_inc(sem("L.nmax_ready"), 1)
                    if 1 <= n <= len(att):
                        m = n - 1
                        a0 = 0 if att[m][0] < NBAND else LOC
                        e.wait_ge(sem("L.p_exp"), m + 1)
                        ch.link(e.reciprocal(rinv[:, m % 2:m % 2 + 1], rsum[:, m % 2:m % 2 + 1]))
                        e.tensor_scalar(prob[:, m % 2, a0:512], prob[:, m % 2, a0:512], rinv[:, m % 2:m % 2 + 1], None, ALU.mult).then_inc(sem("L.p_ready"), 1)
                    if n >= 2:
                        m = n - 2
                        b, h = att[m]
                        o = (h % 2) * DH
                        e.wait_ge(sem("L.o_mm"), m + 1)
                        src = ps[4 + m % 2][o:o + DH, 0:P]
                        if b < NBAND:
                            dst = mixT[o:o + DH, 4 + h // 2, CTX:T].rearrange("p (r w) -> p r w", w=GRID_W)[:, :, b * QB:(b + 1) * QB]
                            src = src.rearrange("p (r c) -> p r c", r=ROWS)
                        else:
                            dst = mixT[o:o + DH, 4 + h // 2, (b - NBAND) * P:(b - NBAND + 1) * P]
                        e.tensor_copy(dst, src).then_inc(sem("L.o_att"), 1)
                meet(e, "dve")

                e.wait_ge(sem("L.row1_loaded"), 48)
                for t in range(t0, NT):
                    m = t - t0
                    w = tmp[:, m % 2, :]
                    e.wait_ge(sem("L.y_ready"), m + 1)
                    for hf in range(2):
                        c = slice(hf * 512, (hf + 1) * 512)
                        ins = e.tensor_tensor(w[:, c], ps[2 * (m % 4) + hf][:], g1r[:, cond_of[t], c], ALU.mult)
                    ins.then_inc(sem("L.y_read"), 1)
                    e.wait_ge(sem("L.y_read"), m + 1)
                    ch.link(e.scalar_tensor_tensor(out=w, in0=X[:, t, :], scalar=ALPHA, in1=w, op0=ALU.mult, op1=ALU.add))
                    e.bn_stats(lns[:, 0, 0, :], w[:, 0:512])
                    ch.link(e.bn_stats(lns[:, 0, 1, :], w[:, 512:D]))
                    e.bn_aggr(mv, lns[:, 0].rearrange("p a b -> p (a b)")).then_inc(sem("L.var1"), 1)
                    e.wait_ge(sem("L.var1"), m + 1)
                    e.wait_ge(sem("L.sd1"), m + 1)
                    ch.link(e.reciprocal(sd[:, 1:2], sd[:, 0:1]))
                    ch.link(e.tensor_scalar(w, w, mv[:, 0:1], sd[:, 1:2], ALU.subtract, ALU.mult))
                    ch.link(e.tensor_tensor(w, w, ln1r[:, 0, :], ALU.mult))
                    ch.link(e.tensor_tensor(X[:, t, :], w, ln1r[:, 1, :], ALU.add))
                meet(e, "dve")

                for n in range(1, 4 * PH, 2):
                    c = n // 2
                    e.wait_ge(sem("L.wk_mm"), n + 1)
                    e.tensor_copy(wk[:, 4:8, c * NKEY:(c + 1) * NKEY], ps[n % 8][:, :].rearrange("p (k n) -> p k n", k=4)).then_inc(sem("L.wk_evac_v"), 1)
                meet(e, "dve")

                if True:
                    nt = NT - t0
                    u_before = 0 if l == 0 else PH * NT
                    UN = TOPK

                    def route(un, bank=2):
                        e.wait_ge(sem("L.key_mm"), un + 1)
                        e.sem_inc(sem("L.dve_token"), 1)
                        S = [ps[bank][:, hf * NKEY:(hf + 1) * NKEY] for hf in range(2)]
                        e.max(tv[:, 0, 0:8], S[0])
                        yield
                        lc.link(e.max(tv[:, 1, 0:8], S[1]))
                        yield
                        for hf in range(2):
                            e.max_index(ti[:, hf, 0:8], tv[:, hf, 0:8], S[hf])
                            yield
                        e.match_replace(sc[:, 0, :], tv[:, 0, 0:8], S[0], LOWEST)
                        yield
                        e.match_replace(sc[:, 1, :], tv[:, 1, 0:8], S[1], LOWEST).then_inc(sem("L.route_read"), 1)
                        e.wait_ge(sem("L.route_read"), un + 2)
                        e.sem_inc(sem("L.dve_token"), 1)
                        yield
                        e.max(tv[:, 0, 8:16], sc[:, 0, :])
                        yield
                        lc.link(e.max(tv[:, 1, 8:16], sc[:, 1, :]))
                        yield
                        for hf in range(2):
                            e.max_index(ti[:, hf, 8:16], tv[:, hf, 8:16], sc[:, hf, :])
                            yield
                        lc.link(e.tensor_tensor(cand.rearrange("p (a b) -> p a b", a=TOPK), tv[:, 0, :].unsqueeze(2).to_broadcast([P, TOPK, TOPK]),
                                                tv[:, 1, :].unsqueeze(1).to_broadcast([P, TOPK, TOPK]), ALU.add))
                        yield
                        lc.link(e.max(tt[:, 0:8], cand))
                        yield
                        e.max_index(pos[:, 0:8], tt[:, 0:8], cand)
                        yield
                        lc.link(e.match_replace(cand2, tt[:, 0:8], cand, LOWEST))
                        yield
                        lc.link(e.max(tt[:, 8:16], cand2))
                        yield
                        lc.link(e.max_index(pos[:, 8:16], tt[:, 8:16], cand2))
                        yield
                        e.tensor_scalar(hilo[:, 0, :], pos, 4, None, ALU.logical_shift_right)
                        lc.link(e.tensor_scalar(hilo[:, 1, :], pos, 15, None, ALU.bitwise_and))
                        yield
                        for hf in range(2):
                            o3 = oh.rearrange("p (k a) -> p k a", k=TOPK)
                            lc.link(e.tensor_tensor(o3, hilo[:, hf, :].unsqueeze(2).to_broadcast([P, TOPK, TOPK]),
                                                    iota.unsqueeze(1).to_broadcast([P, TOPK, TOPK]), ALU.is_equal))
                            yield
                            lc.link(e.tensor_tensor(o3, o3, ti[:, hf, :].unsqueeze(1).to_broadcast([P, TOPK, TOPK]), ALU.mult))
                            yield
                            lc.link(e.tensor_reduce(e1[:, hf, :], o3, AX.X, ALU.add))
                            yield
                        lc.link(e.tensor_scalar(e1[:, 0, :], e1[:, 0, :], float(NKEY), float(l * NEXP), ALU.mult, ALU.add))
                        yield
                        e.tensor_tensor(eidx_all[:, bass.ds(un * UN, UN)], e1[:, 0, :], e1[:, 1, :], ALU.add)
                        e.tensor_scalar(gate_all[:, bass.ds(un * UN, UN)], tt, tt[:, 0:1], None, ALU.subtract).then_inc(sem("L.route_done"), 1)
                        e.wait_ge(sem("L.route_done"), un + 1)
                        yield

                    def stage_index(un, half):
                        e.tensor_copy(idx16[:, 8 * half:8 * half + 8], eidx_all[:, bass.ds(un * UN + 8 * half, 8)]).then_inc(sem("L.idx_ready"), 1)

                    def gate_norm(un):
                        e.wait_ge(sem("L.gexp"), un + 1)
                        e.sem_inc(sem("dve_token"), 1)
                        g = gate_all[:, bass.ds(un * TOPK, TOPK)]
                        lc.link(e.tensor_reduce(gsum[:, 0:1], g, AX.X, ALU.add))
                        lc.link(e.reciprocal(gsum[:, 1:2], gsum[:, 0:1]))
                        lc.link(e.tensor_scalar(g, g, gsum[:, 1:2], None, ALU.mult))

                    def make_diag(un, k):
                        e.wait_ge(sem("L.act_done"), un * UN + (k + 1))
                        e.wait_ge(sem("L.slot_done"), un * UN + (k - 1 + RING))
                        e.tensor_scalar(diag[:, k % 2, :], ident, acts[:, k:k + 1], gate_all[:, bass.ds(un * UN + k, 1)], ALU.mult, ALU.mult).then_inc(sem("L.diag_ready"), 1)

                    def unit(un, route_next):
                        lc.restart()
                        steps = route(un + LEAD) if route_next else iter(())
                        for k in range(TOPK):
                            e.wait_ge(sem(f"rows{k % RING}"), un * 32 + (32 * u_before + 16 * (k // RING + 1)))
                            e.tensor_tensor_reduce(prod[:, k % 2, :], ring[:, k % RING, 0:D], u, 1.0, 0.0, ALU.mult, ALU.add, dots[:, k:k + 1]).then_inc(sem("L.dot_done"), 1)
                            if k >= 1:
                                make_diag(un, k - 1)
                            if k % RING == RING - 1:
                                stage_index(un + 1, k // RING)
                            for _ in range(3):
                                next(steps, None)
                            if k == EXP_AT:
                                assert next(steps, None) is None
                            if k == NORM_AT and route_next:
                                gate_norm(un + LEAD)
                        make_diag(un, TOPK - 1)

                    def modulate(t):
                        e.wait_ge(sem("L.uT_mm"), t)
                        e.sem_inc(sem("dve_token"), 1)
                        lc.link(e.tensor_tensor(u_next, X[:, bass.ds(t + t0, 1), :].rearrange("p a d -> p (a d)"), sc2r, ALU.mult))
                        e.tensor_tensor(u_next, u_next, sh2r, ALU.add).then_inc(sem("L.u_ready"), 1)

                    def tile(t, more, static_first, late):
                        xt = X[:, bass.ds(t + t0, 1), :]
                        lc.restart()
                        lc.link(e.tensor_copy(u, u_next))
                        if more:
                            if l < L - 1 and not static_first:
                                e.wait_ge(sem("L.u_rows_changed"), 32)
                            modulate(t + 1)
                        with e.Fori(0, PH - LEAD) as h:
                            unit(t * PH + h, True)
                        with e.Fori(0, LEAD) as h:
                            unit(t * PH + h + (PH - LEAD), more)
                        if l < L - 1 and late:
                            e.wait_ge(sem("L.g_row_changed"), 16)
                        e.wait_ge(sem("L.acc_ready"), t + 1)
                        lc.restart()
                        for hf in range(2):
                            c = slice(hf * 512, (hf + 1) * 512)
                            ins = e.tensor_tensor(junk[:, c], ps[hf][:], g2r[:, c], ALU.mult)
                        ins.then_inc(sem("L.acc_free"), 1)
                        e.wait_ge(sem("L.acc_free"), t + 2)
                        lc.link(e.scalar_tensor_tensor(out=junk, in0=xt.rearrange("p a d -> p (a d)"), scalar=ALPHA, in1=junk, op0=ALU.mult, op1=ALU.add))
                        e.bn_stats(lns2[:, 0, :], junk[:, 0:512])
                        lc.link(e.bn_stats(lns2[:, 1, :], junk[:, 512:D]))
                        e.bn_aggr(mv2, lns2.rearrange("p a b -> p (a b)")).then_inc(sem("L.var2"), 1)
                        e.wait_ge(sem("L.sd2"), t + 1)
                        lc.link(e.reciprocal(sd2[:, 1:2], sd2[:, 0:1]))
                        lc.link(e.tensor_scalar(junk, junk, mv2[:, 0:1], sd2[:, 1:2], ALU.subtract, ALU.mult))
                        lc.link(e.tensor_tensor(junk, junk, ln2r[:, 0, :], ALU.mult))
                        lc.link(e.tensor_tensor(xt.rearrange("p a d -> p (a d)"), junk, ln2r[:, 1, :], ALU.add))

                    e.memset(zero, 0.0).then_inc(sem("L.zero_set"), 1)
                    e.memset(eidx_all[:, nt * PH * UN:nt * PH * UN + UN], 0).then_inc(sem("L.zero_set"), 1)
                    e.sem_inc(sem("L.route_read"), 1)
                    e.sem_inc(sem("L.acc_free"), 1)
                    e.wait_ge(sem("L.row2_loaded"), 64)
                    lc.restart()
                    lc.link(e.tensor_tensor(u_next, X[:, t0, :], sc2r, ALU.mult))
                    e.tensor_tensor(u_next, u_next, sh2r, ALU.add).then_inc(sem("L.u_ready"), 1)
                    e.wait_ge(sem("L.u_ready"), 1)
                    for h in range(LEAD):
                        lc.restart()
                        for _ in route(h, 2 + h % 2):
                            pass
                        if h == 0:
                            stage_index(0, 0)
                            stage_index(0, 1)
                    for h in range(LEAD):
                        gate_norm(h)
                    for ta, tb in tile_spans(l):
                        if tb - ta > 1:
                            with e.Fori(ta, tb) as t:
                                tile(t, True, False, ta >= NCT)
                        else:
                            tile(ta, tb < nt, ta == 0, ta >= NCT)
                    meet(e, "dve")
                    reset(e, "dve", "L.", ch)


def kernel(**inputs):
    import numpy as _np
    import concourse.bacc as _bacc
    from concourse import mybir as _mybir
    from concourse.bass_utils import run_bass_kernel_spmd as _run

    nc = _bacc.Bacc("TRN2", target_bir_lowering=False, num_devices=1)
    arrays = {}

    def inp(name, a):
        a = _np.ascontiguousarray(a)
        arrays[f"in_{name}"] = a
        return nc.dram_tensor(f"in_{name}", a.shape, _mybir.dt.from_np(a.dtype), kind="ExternalInput").ap()

    i = {k: _np.asarray(v) for k, v in inputs.items()}
    li_cols = [0, 1, 2, 3, 8, 9, 10, 11]
    lf_cols = [4, 5, 6, 7, 12, 13, 14, 15]
    gates = i["w_in"][:, :, COL_G:COL_G + 16][:, :, li_cols + lf_cols]
    q = _np.arange(P)
    k = _np.arange(LOC)
    row = k[None] // BAND - q[:, None] // QB + ROWS - 1
    spread = []
    for b in range(NBAND):
        col = BAND_LO[b] + k[None] % BAND - (b * QB + q[:, None] % QB)
        col = _np.clip(col, 1 - WIN, WIN - 1) + WIN - 1
        spread.append(i["na_rpb"][:, :, row, col].transpose(0, 2, 1, 3))
    args = [
        inp("x", _np.concatenate([i["ctx"][0], i["x"][0]], 0)),
        inp("c", _np.stack([i["c_ctx"], i["c"][0]]).reshape(2, KD, P).transpose(2, 1, 0)),
        inp("consts", shape_constants()),
        inp("ada_w", i["ada_w"]), inp("ada_b", i["ada_b"]), inp("w_in", i["w_in"]),
        inp("wg", gates.reshape(L, KD, P, 16).transpose(0, 2, 1, 3)),
        inp("bg", _np.stack([i["b_gate"][:, li_cols], i["b_gate"][:, lf_cols]], -1)),
        inp("conv_w", i["conv_w"].reshape(L, 5, 4, P).transpose(0, 3, 2, 1)),
        inp("ml_norm_w", i["ml_norm_w"]),
        inp("bias", _np.stack(spread, 1)),
        inp("w_out", i["w_out"]),
        inp("ln1", _np.concatenate([i["ln1_w"], i["ln1_b"]], -1)),
        inp("wq", i["peer_wq"].transpose(0, 2, 1)),
        inp("keys", i["peer_keys"].reshape(L, 2 * PH, NKEY, P).transpose(0, 3, 1, 2)),
        inp("updown", _np.concatenate([i["peer_up"].reshape(L * NEXP, D), i["peer_down"].reshape(L * NEXP, D)], -1)),
        inp("ln2", _np.concatenate([i["ln2_w"], i["ln2_b"]], -1)),
        nc.dram_tensor("mod_rows", (L, 2, N_MOD * D), _mybir.dt.float32).ap(),
        nc.dram_tensor("negm_rows", (L, 2, MLH, T), _mybir.dt.float32).ap(),
        nc.dram_tensor("out_0", (1, SEQ, D), _mybir.dt.float32, kind="ExternalOutput").ap(),
    ]
    build(nc, *args)
    r = _run(nc, [arrays], core_ids=[0])
    return r.results[0]["out_0"]
```

```python
from contextlib import ExitStack

import numpy as np
import concourse.bass as bass
from concourse import mybir

F32 = mybir.dt.float32
U32 = mybir.dt.uint32
BF16 = mybir.dt.bfloat16
ALU = mybir.AluOpType
ACT = mybir.ActivationFunctionType
AX = mybir.AxisListType

P = 128
D = 1024
KD = D // P
L = 2
CTX, SEQ = 256, 512
NT, NCT = (CTX + SEQ) // P, CTX // P
T = CTX + SEQ
GRID_W = 64
ROWS = SEQ // GRID_W
MLH, DV, DK = 4, 128, 64
NAH, DH = 8, 64
QB, BAND, WIN = 16, 32, 16
NBAND = GRID_W // QB
BAND_LO = [min(max(b * QB - WIN // 2, 0), GRID_W - BAND) for b in range(NBAND)]
LOC = ROWS * BAND
N_MOD = 6
SH1, SC1, G1, SH2, SC2, G2 = range(N_MOD)
D_IN = 3088
COL_ML, COL_V, COL_O, COL_G, COL_NQ, COL_NK, COL_NV = 0, 512, 1024, 1536, 1552, 2064, 2576
PH, NKEY, TOPK = 8, 128, 16
NEXP = NKEY * NKEY
ALPHA = (2.0 * L) ** 0.25
EPS = 1e-5
LOWEST = -3.0e38
MASKED = -1.0e30
RING = 8
EXP_AT, NORM_AT = 11, 14
LEAD = 2

C_ID, C_ROT, C_TRI, C_IOTA, C_KEEP, C_MASK, C_COS, C_SIN, C_END = 0, 128, 256, 512, 528, 528, 1552, 2064, 2576


def shape_constants():
    c = np.zeros((P, C_END), np.float32)
    p = np.arange(P)
    c[:, C_ID:C_ID + P] = np.eye(P)
    for m in range(P):
        if m % DK < DK // 2:
            c[m + DK // 2, C_ROT + m] = -1.0
        else:
            c[m - DK // 2, C_ROT + m] = 1.0
    c[:, C_TRI:C_TRI + P] = p[:, None] <= p[None, :]
    c[:, C_TRI + P:C_TRI + 2 * P] = p[:, None] >= p[None, :]
    c[:, C_IOTA:C_IOTA + TOPK] = np.arange(TOPK)
    for b in range(NBAND):
        q = b * QB + p % QB
        lo = np.clip(q - WIN // 2, 0, GRID_W - WIN)
        k = BAND_LO[b] + np.arange(BAND)
        ok = (k[None] >= lo[:, None]) & (k[None] < lo[:, None] + WIN)
        c[:, C_MASK + b * LOC:C_MASK + (b + 1) * LOC] = np.tile(np.where(ok, 0.0, MASKED), (1, ROWS))
    pos, nf = np.arange(SEQ), DK // 4
    inv = np.float32(10000.0) ** (-np.arange(nf, dtype=np.float32) / nf)
    ang = np.concatenate([(pos // GRID_W)[:, None] * inv, (pos % GRID_W)[:, None] * inv], -1).astype(np.float32)
    c[:, C_COS:C_COS + SEQ] = np.cos(ang).T[p % (DK // 2)]
    c[:, C_SIN:C_SIN + SEQ] = np.sin(ang).T[p % (DK // 2)]
    return c


class Chain:

    def __init__(self, eng, sem, token=None):
        self.eng, self.sem, self.token, self.n = eng, sem, token, 0

    def link(self, ins):
        self.n += 1
        ins.then_inc(self.sem, 1)
        self.eng.wait_ge(self.sem, self.n)
        return ins

    def restart(self):
        self.eng.sem_inc(self.token, 1)
        self.eng.sem_clear(self.sem)
        self.n = 0


def proj_jobs(l):
    q_ctx = l < L - 1
    jobs = []
    for k in range(KD):
        jobs += [("T", k, "x", "v"), ("T", k, "c", "a")]
    for g in range(2):
        jobs += [("G", g, "x", "a"), ("G", g, "c", "a")]

    def ml(c):
        out = [("M", c, "x", "a")]
        if q_ctx or c >= 2:
            out.append(("M", c, "c", "a"))
        return out
    jobs += ml(0) + ml(1) + [("X", 0, "x", "v")] + ml(2) + [("R", 0, "x", "v")] + ml(3) + [("R", 1, "x", "v")]
    for kind in "QK":
        for c in range(4):
            jobs.append((kind, c, "x", "va"[c % 2]))
            if q_ctx or kind == "K":
                jobs.append((kind, c, "c", "av"[c % 2]))
            if kind == "Q" and c < 2:
                jobs.append(("R", 2 + c, "x", "v"))
    for t in range(NT):
        jobs.append(("V", t, "x", "va"[t % 2]))
    for t in range(0 if q_ctx else NCT, NT):
        jobs.append(("O", t, "x", "a"))
    for t in list(range(NCT, NT)) + list(range(NCT)):
        jobs.append(("B", t, "x", "va"[t % 2]))
    return jobs


OFF_F = [sum(6 - m for m in range(i)) * P for i in range(6)]
OFF_B = [0, 5 * P, 11 * P, 12 * P, 14 * P, 17 * P]
N_BLK = 21 * P


def at_f(i, j):
    return OFF_F[i] + (j - i) * P


def at_b(i, j):
    if i < NCT:
        return OFF_B[i] + ((j - NCT) * P if j >= NCT else 4 * P + j * P)
    return OFF_B[i] + (j - NCT) * P


def b_sources(j):
    return list(range(j, NCT)) if j < NCT else [0, 1] + list(range(j, NT))


def tile_spans(l):
    return [(0, 1), (1, 2), (2, NT - 1), (NT - 1, NT)] if l < L - 1 else [(0, NT - NCT - 1), (NT - NCT - 1, NT - NCT)]


def attention_jobs(l):
    return [(b, h) for b in range(NBAND + (NCT if l < L - 1 else 0)) for h in range(NAH)]


SCORE_SLOTS = 3
OUT_BANK = (3, 6)
TURN_LAG, VALUES_LAG, KEEP_LAG = 2, 3, 4


def mlstm_tile_at(n, lag, tiles):
    k = (n - lag) // 2
    return k if (n - lag) % 2 == 0 and 0 <= k < tiles else None


def key_chunks(m, tiles):
    return range(m * 2 * PH // tiles, (m + 1) * 2 * PH // tiles)


BAND_DMAS = NBAND * (P // BAND)


def last_job(jobs, kind):
    return max(n for n, j in enumerate(jobs) if j[0] == kind) + 1


def chunk_end(jobs, c):
    kind, i = "MQK"[c // 4], c % 4
    return max(n for n, j in enumerate(jobs) if j[:2] == (kind, i)) + 1


def ordinals(jobs):
    count, out = {"v": 0, "a": 0}, []
    for j in jobs:
        count[j[3]] += 1
        out.append(count[j[3]])
    return out


def build(nc, xin, cT, consts, ada_w, ada_b, w_in, wg, bg, convw, ml_norm_w, bias, w_out, ln1, wqT, keysT,
          updown, ln2, mod_d, negm_d, out):
    with ExitStack() as ctx:
        def sb(name, shape, dt=F32):
            return ctx.enter_context(nc.sbuf_tensor(name, shape, dt))

        X = sb("X", [P, NT, D])
        CN = sb("CN", [P, C_KEEP])
        modcol = sb("modcol", [P, L, N_MOD * KD, 2])
        sT = sb("sT", [P, KD, 2])
        epsc = sb("epsc", [P, 1])
        ARENA_W = 45900
        arena = sb("arena", [P, ARENA_W])
        ident = CN[:, C_ID:C_ID + P]
        rot = CN[:, C_ROT:C_ROT + P]
        iota = CN[:, C_IOTA:C_IOTA + TOPK]

        class Region:

            def __init__(self, at=0):
                self.at = at

            def __call__(self, *shape):
                n = int(np.prod(shape))
                v = arena[:, self.at:self.at + n]
                self.at += n
                assert self.at <= ARENA_W, self.at
                if len(shape) == 2:
                    return v.rearrange("p (a b) -> p a b", a=shape[0])
                if len(shape) == 3:
                    return v.rearrange("p (a b c) -> p a b c", a=shape[0], b=shape[1])
                return v

        r = Region()
        adaw = r(3, KD, 512)
        adab = r(L * N_MOD * D)
        modrow = r(L * N_MOD * D)
        r = Region()
        mlqk = r(4, T)
        nq = r(4, T)
        nk = r(4, T)
        vband_at = r.at
        vband = r(2 * NBAND + NCT, 512)
        vml_at = r.at
        vml = r(NT, MLH, DV + 1)
        sigo_at = r.at
        sigo = r(NT, 512)
        gcol = r(4 * NT * 8)
        mixer_top = r.at
        r = Region(mixer_top)
        uT = r(KD, T)
        wch = r(3, KD, P)
        wtok_at = r.at
        wtok = r(2, KD, 512)
        wgs = r(KD, 16)
        convs = r(4, 5)
        bgs = r(2)
        cosr = r(SEQ)
        sinr = r(SEQ)
        proj_top = r.at
        r = Region(sigo_at)
        raw = r(2, 776)
        ysil = r(2, 512)
        assert r.at <= sigo_at + NT * 512
        r = Region(vml_at)
        cvs = r(2, 776)
        rt = r(2, 512)
        assert r.at <= vml_at + NT * MLH * (DV + 1)
        r = Region(wtok_at + KD * 512)
        li, lf, lnl, cum = [r(T)[0:8, :] for _ in range(4)]
        r = Region(vband_at)
        gF, gB, eF, eB, nMf, nMb = [r(T)[0:8, :] for _ in range(6)]
        r = Region(mixer_top)
        mixT = r(KD, T)
        mixT_end = r.at
        assert 2 * N_BLK <= mixT_end - mixer_top
        H = r(NT, 512)
        stat = r(NT * MLH, 2)
        rstd = r(NT * MLH)
        bns = r(4, 6)
        den = r(2, 2)
        rden = r(2, 2)
        nwrow = r(512)
        heads_top = r.at
        negm = r(2, 2, T)
        WD2 = [r(2, N_BLK), Region(mixer_top)(2, N_BLK)]
        wd_at = r.at - 2 * N_BLK

        def diagonal(h, i):
            at, step = (wd_at, mixer_top)[h % 2] + at_f(i, i), N_BLK + at_b(i, i) - at_f(i, i)
            return arena[:, at:at + 2 * step].rearrange("p (d n) -> p d n", d=2)[:, :, 0:P]
        biasb = r(2, 4, LOC)
        prob = r(SCORE_SLOTS, 512)
        probT = r(2, 512)
        nmax = r(SCORE_SLOTS)
        rsum = r(SCORE_SLOTS)
        rinv = r(SCORE_SLOTS)
        masks = r(NBAND, LOC)
        vlat_at = r.at - NBAND * LOC - (NT - NCT) * 512
        assert vlat_at >= proj_top
        vlat = Region(vlat_at)(NT - NCT, 512)
        r = Region()
        wk = r(KD, 2 * PH * NKEY)
        wk_flat = wk.rearrange("p k n -> p (k n)")
        sc2r, sh2r = r(D), r(D)
        keys_at = r.at
        u = r(D)
        u_next = r(D)
        uTs = r(KD, P)
        g2r = r(D)
        ln2r = r(2, D)
        junk = r(D)
        prod = junk.bitcast(BF16).rearrange("p (a d) -> p a d", a=2)
        diag = r(2, P)
        zero = r(P)
        idx16 = r(TOPK).bitcast(U32)
        sc = r(2, NKEY)
        cand2 = sc.rearrange("p a b -> p (a b)")
        tv = r(2, TOPK)
        ti = r(2, TOPK).bitcast(U32)
        cand = r(256)
        oh = cand
        tt = r(TOPK)
        pos = r(TOPK).bitcast(U32)
        hilo = r(2, TOPK).bitcast(U32)
        e1 = r(2, TOPK)
        eidx_all = r((NT + 1) * PH * TOPK).bitcast(U32)
        gate_all = r((NT + 1) * PH * TOPK)
        gsum = r(PH)
        dots = r(TOPK)
        acts = r(TOPK)
        lns2 = r(2, 6)
        mv2 = r(2)
        sd2 = r(2)
        ring = r(RING, 2 * D)
        keys = Region(keys_at)(2 * PH, NKEY)
        assert keys_at + 2 * PH * NKEY <= mixer_top
        r = Region(mixT_end)
        ln1r = r(2, D)
        wq_slots = [r(D)]
        assert r.at <= heads_top
        r = Region(heads_top)
        wo = r(KD, D)
        assert r.at <= wd_at + 2 * N_BLK
        g1r = r(2, D)
        tmp = r(2, D)
        wq_slots += [r(D), r(D)]
        lns = r(2, 6)
        mv = r(2)
        sd = r(2)

        ps = [ctx.enter_context(nc.psum_tensor(f"ps{i}", [P, 512], F32)) for i in range(8)]

        sems = {}

        def sem(name):
            if name not in sems:
                sems[name] = ctx.enter_context(nc.semaphore(name))
            return sems[name]

        barrier = sem("stage_barrier")
        bar_n = {}

        def meet(e, who):
            bar_n[who] = bar_n.get(who, 0) + 1
            e.drain()
            e.sem_inc(barrier, 1)
            e.wait_ge(barrier, 5 * bar_n[who])
            e.sem_inc(sem("stage_passed"), 1)

        def reset(e, who, scope, ch=None):
            if who == "dve":
                for name, x in sems.items():
                    if name.startswith(scope):
                        ins = e.sem_clear(x)
                ch.link(ins)
            meet(e, who)

        block = ctx.enter_context(nc.Block())
        cond_of = [0] * NCT + [1] * (NT - NCT)
        mod_v = modrow.rearrange("p (l n) -> p l n", l=L)

        @block.sync
        def _(e):
            e.dma_start(sT[:], cT).then_inc(sem("c_loaded"), 16)
            e.dma_start(adab[0:2, :], ada_b.rearrange("(o l) n -> o (l n)", o=1).to_broadcast([2, L * N_MOD * D])).then_inc(sem("adab_loaded"), 16)
            for n in range(24):
                if n >= 3:
                    e.wait_ge(sem("mod_mm"), n - 2)
                e.dma_start(adaw[:, n % 3], ada_w[n // 12].rearrange("(k p) n -> p k n", p=P)[:, :, (n % 12) * 512:(n % 12 + 1) * 512]).then_inc(sem(f"adaw_loaded{n % 3}"), 16)
                if n == 2:
                    e.dma_start(CN[:], consts[:, 0:C_KEEP]).then_inc(sem("const_loaded"), 16)
                    e.dma_start(X[:], xin.rearrange("(t p) d -> p t d", p=P)).then_inc(sem("x_loaded"), 16)
            e.wait_ge(sem("mod_row"), 24)
            for l in range(L):
                e.dma_start(mod_d[l], mod_v[0:2, l, :]).then_inc(sem("mod_stored"), 16)
            e.wait_ge(sem("mod_stored"), 16 * L)
            e.wait_ge(sem("x_loaded"), 16)
            e.wait_ge(sem("const_loaded"), 16)
            meet(e, "sp")
            for l in range(L):
                jobs = proj_jobs(l)
                e.dma_start(wgs[:], wg[l]).then_inc(sem("L.small_loaded"), 16)
                e.dma_start(bgs[0:8, :], bg[l]).then_inc(sem("L.small_loaded"), 16)
                e.dma_start(convs[:], convw[l]).then_inc(sem("L.small_loaded"), 16)
                e.dma_start(cosr, consts[:, C_COS:C_COS + SEQ]).then_inc(sem("L.rotary_loaded"), 16)
                e.dma_start(sinr, consts[:, C_SIN:C_SIN + SEQ]).then_inc(sem("L.rotary_loaded"), 16)
                wv = w_in[l].rearrange("(k p) n -> p k n", p=P)
                chunks = [COL_ML + c * P for c in range(4)] + [COL_NQ + c * P for c in range(4)] + [COL_NK + c * P for c in range(4)]

                def load_tok(n):
                    col = (COL_V, COL_O, COL_NV)[n]
                    e.dma_start(wtok[:, n % 2], wv[:, :, col:col + 512]).then_inc(sem(f"L.wtok_loaded{n % 2}"), 16)
                load_tok(0)
                for n, col in enumerate(chunks):
                    if n >= 3:
                        e.wait_ge(sem("L.proj_mm"), chunk_end(jobs, n - 3))
                    e.dma_start(wch[:, n % 3], wv[:, :, col:col + P]).then_inc(sem(f"L.wch_loaded{n % 3}"), 16)
                    if n == 3:
                        e.wait_ge(sem("L.negm_ready"), 2)
                        e.dma_start(negm_d[l, 0], nMf[0:4, :]).then_inc(sem("L.negm_stored"), 16)
                        e.dma_start(negm_d[l, 1], nMb[4:8, :]).then_inc(sem("L.negm_stored"), 16)
                e.wait_ge(sem("L.negm_stored"), 32)
                e.wait_ge(sem("L.proj_mm"), last_job(jobs, "X"))
                load_tok(1)
                e.wait_ge(sem("L.proj_mm"), last_job(jobs, "V"))
                load_tok(2)
                last = {w: max(ordinals(jobs)[n] for n, j in enumerate(jobs) if j[0] == "B" and j[1] >= NCT and j[3] == w) for w in "va"}
                e.wait_ge(sem("L.proj_evac_v"), last["v"])
                e.wait_ge(sem("L.proj_evac_a"), last["a"])
                for b in range(NBAND):
                    for q in range(P // BAND):
                        at = (q % 2) * GRID_W + BAND_LO[b]
                        e.dma_start(vband[q * BAND:(q + 1) * BAND, 2 * b:2 * b + 2, :],
                                    vlat[at:at + BAND, q // 2:NT - NCT:2, :]).then_inc(sem("L.bands_placed"), 16)
                meet(e, "sp")
                e.dma_start(nwrow, ml_norm_w[l:l + 1, :].to_broadcast([P, 512])).then_inc(sem("L.nw_loaded"), 16)
                for h in range(MLH):
                    if h >= 2:
                        e.wait_ge(sem("L.decay_ready"), (h - 1) * NT)
                    for d in range(2):
                        e.dma_start(negm[:, h % 2, d, :], negm_d[l, d, h:h + 1, :].to_broadcast([P, T])).then_inc(sem(f"L.negm_loaded{h % 2}"), 16)
                e.dma_start(masks.rearrange("p a b -> p (a b)"), consts[:, C_MASK:C_MASK + NBAND * LOC]).then_inc(sem("L.masks_loaded"), 16)
                for n in range(2 * NBAND):
                    if n == 2:
                        e.wait_ge(sem("L.num_ready"), MLH * (NT - (0 if l < L - 1 else NCT)))
                        e.dma_start(wo[:], w_out[l].rearrange("(k p) n -> p k n", p=P)).then_inc(sem("L.wo_loaded"), 16)
                    if n >= 2:
                        e.wait_ge(sem("L.bias_used"), 4 * (n - 1))
                    e.dma_start(biasb[:, n % 2], bias[l, n // 2][:, 4 * (n % 2):4 * (n % 2) + 4, :]).then_inc(sem(f"L.bias_loaded{n % 2}"), 16)
                meet(e, "sp")
                cnd = 0 if l < L - 1 else 1

                def mod_row(dst, cnd, v, name):
                    e.dma_start(dst, mod_d[l, cnd:cnd + 1, v * D:(v + 1) * D].to_broadcast([P, D])).then_inc(sem(name), 16)
                mod_row(g1r[:, cnd], cnd, G1, "L.row1_loaded")
                e.dma_start(keys[:], keysT[l]).then_inc(sem("L.keys_loaded"), 16)
                for c in range(2 * PH):
                    if c >= len(wq_slots):
                        e.wait_ge(sem("L.wk_mm"), 2 * (c - len(wq_slots) + 1))
                    e.dma_start(wq_slots[c % len(wq_slots)], wqT[l, c * P:(c + 1) * P, :]).then_inc(sem(f"L.wq_loaded{c % len(wq_slots)}"), 16)
                    if c == 0:
                        e.dma_start(ln1r[:].rearrange("p a b -> p (a b)"), ln1[l:l + 1, :].to_broadcast([P, 2 * D])).then_inc(sem("L.row1_loaded"), 16)
                    if c == 2:
                        if l < L - 1:
                            mod_row(g1r[:, 1], 1, G1, "L.row1_loaded")
                        mod_row(sc2r, cnd, SC2, "L.u_rows_loaded")
                        mod_row(sh2r, cnd, SH2, "L.u_rows_loaded")
                meet(e, "sp")
                mod_row(g2r, cnd, G2, "L.row2_loaded")
                e.dma_start(ln2r[:].rearrange("p a b -> p (a b)"), ln2[l:l + 1, :].to_broadcast([P, 2 * D])).then_inc(sem("L.row2_loaded"), 16)
                if l < L - 1:
                    e.wait_ge(sem("L.u_ready"), NCT)
                    mod_row(sc2r, 1, SC2, "L.u_rows_changed")
                    mod_row(sh2r, 1, SH2, "L.u_rows_changed")
                    e.wait_ge(sem("L.acc_free"), NCT + 1)
                    mod_row(g2r, 1, G2, "L.g_row_changed")
                if l < L - 1:
                    meet(e, "sp")
                    reset(e, "sp", "L.")
            for t in range(NT - NCT):
                e.wait_ge(sem("L.tile_done"), t + 1)
                e.dma_start(out[0, t * P:(t + 1) * P, :], X[:, NCT + t, :]).then_inc(sem("out_stored"), 16)
            e.wait_ge(sem("out_stored"), 16 * (NT - NCT))

        @block.tensor
        def _(e):
            e.wait_ge(sem("silu_c"), 1)
            for n in range(24):
                e.wait_ge(sem(f"adaw_loaded{n % 3}"), 16 * (n // 3 + 1))
                if n >= 4:
                    e.wait_ge(sem("mod_row"), n - 3)
                for k in range(KD):
                    mm = e.matmul(ps[n % 4][0:2, :], sT[:, k, :], adaw[:, n % 3, k, :], start=(k == 0), stop=(k == KD - 1))
                mm.then_inc(sem("mod_mm"), 1)
            e.wait_ge(sem("mod_row"), 24)
            e.wait_ge(sem("const_loaded"), 16)
            for l in range(L):
                for c in range(N_MOD * KD):
                    mm = e.transpose(ps[4 + l][:, 2 * c:2 * c + 2], mod_v[0:2, l, c * P:(c + 1) * P], ident[0:2, 0:2])
                mm.then_inc(sem("modcol_t"), 1)
            e.wait_ge(sem("x_loaded"), 16)
            meet(e, "pe")
            for l in range(L):
                q_ctx = l < L - 1
                t0 = 0 if q_ctx else NCT
                jobs = proj_jobs(l)
                count = {"v": 0, "a": 0}
                freed = []
                n_t = {"v": sum(j[0] == "T" and j[3] == "v" for j in jobs), "a": sum(j[0] == "T" and j[3] == "a" for j in jobs)}
                chunk_no = -1
                for n, (kind, i, part, ev) in enumerate(jobs):
                    if n >= 8:
                        w, val = freed[n - 8]
                        e.wait_ge(sem(f"L.proj_evac_{w}"), val)
                    count[ev] += 1
                    freed.append((ev, count[ev]))
                    bank = ps[n % 8]
                    cols = slice(CTX, T) if part == "x" else slice(0, CTX)
                    width = SEQ if part == "x" else CTX
                    if kind == "T":
                        tiles = range(NCT, NT) if part == "x" else range(NCT)
                        for a, t in enumerate(tiles):
                            mm = e.transpose(bank[:, a * P:(a + 1) * P], X[:, t, i * P:(i + 1) * P], ident)
                    elif kind == "G":
                        if i == 0 and part == "x":
                            e.wait_ge(sem("L.proj_evac_v"), n_t["v"])
                            e.wait_ge(sem("L.proj_evac_a"), n_t["a"])
                            e.wait_ge(sem("L.small_loaded"), 48)
                        for k in range(KD):
                            mm = e.matmul(bank[0:8, 0:width], wgs[:, k, 8 * i:8 * i + 8], uT[:, k, cols], start=(k == 0), stop=(k == KD - 1))
                    elif kind in "MQK":
                        c = i + {"M": 0, "Q": 4, "K": 8}[kind]
                        e.wait_ge(sem(f"L.wch_loaded{c % 3}"), 16 * (c // 3 + 1))
                        for k in range(KD):
                            mm = e.matmul(bank[:, 0:width], wch[:, c % 3, k, :], uT[:, k, cols], start=(k == 0), stop=(k == KD - 1))
                    elif kind == "R":
                        e.wait_ge(sem("L.silu_done"), i + 1)
                        mm = e.matmul(bank[:], rot, ysil[:, i % 2, :], start=True, stop=True)
                    elif kind == "X":
                        e.wait_ge(sem("L.gates_done"), 1)
                        for a, g in enumerate((gF, gB, eF, eB)):
                            for t in range(NT):
                                o = (a * NT + t) * 8
                                mm = e.transpose(bank[:, o:o + 8], g[:, t * P:(t + 1) * P], ident[0:8, 0:8])
                    elif kind in "VO":
                        s = "VO".index(kind)
                        if i == (0 if kind == "V" else t0):
                            e.wait_ge(sem(f"L.wtok_loaded{s}"), 16)
                        for k in range(KD):
                            mm = e.matmul(bank[:], uT[:, k, i * P:(i + 1) * P], wtok[:, s, k, :], start=(k == 0), stop=(k == KD - 1))
                    else:
                        if i == NCT:
                            e.wait_ge(sem("L.wtok_loaded0"), 32)
                        for k in range(KD):
                            mm = e.matmul(bank[:], uT[:, k, i * P:(i + 1) * P], wtok[:, 0, k, :], start=(k == 0), stop=(k == KD - 1))
                    mm.then_inc(sem("L.proj_mm"), 1)
                meet(e, "pe")
                def head_scores(h, i):
                    m, o = h * NT + i, (h % 2) * DK
                    if m >= 2:
                        e.wait_ge(sem("L.w_ready"), m - 1)
                    kk = mlqk[o:o + DK, 2 + h // 2, i * P:(i + 1) * P]
                    mm = e.matmul(ps[m % 2][:], kk, mlqk[o:o + DK, h // 2, CTX:T], start=True, stop=True)
                    if i < NCT and q_ctx:
                        mm = e.matmul(ps[2 + m % 2][:, 0:CTX], kk, mlqk[o:o + DK, h // 2, 0:CTX], start=True, stop=True)
                    mm.then_inc(sem("L.s_ready"), 1)

                def head_sums(h, j):
                    m = h * (NT - t0) + j - t0
                    if j == t0:
                        e.wait_ge(sem("L.w_ready"), (h + 1) * NT)
                    if m >= 2:
                        e.wait_ge(sem("L.h_done"), m - 1)
                    bank = ps[4 + m % 2]
                    for d, src, at in ((0, list(range(j + 1)), at_f), (1, b_sources(j), at_b)):
                        for i in src:
                            mm = e.matmul(bank[:, d * (DV + 1):(d + 1) * (DV + 1)], WD2[h % 2][:, d, at(i, j):at(i, j) + P],
                                          vml[:, i, h, :], start=(i == src[0]), stop=(i == src[-1]))
                    mm.then_inc(sem("L.num_ready"), 1)

                for h in range(MLH + 1):
                    for x in range(NT):
                        if h < MLH:
                            head_scores(h, x)
                        if h >= 1 and t0 + x < NT:
                            head_sums(h - 1, t0 + x)
                att = attention_jobs(l)

                def scores(n):
                    b, h = att[n]
                    if n >= SCORE_SLOTS:
                        e.wait_ge(sem("L.p_exp"), n - SCORE_SLOTS + 1)
                    bank = ps[n % SCORE_SLOTS]
                    o, c = (h % 2) * DH, h // 2
                    q = nq[o:o + DH, c, CTX + b * P:CTX + (b + 1) * P] if b < NBAND else nq[o:o + DH, c, (b - NBAND) * P:(b - NBAND + 1) * P]
                    if b < NBAND:
                        kb = nk[o:o + DH, c, CTX:T].rearrange("p (r w) -> p r w", w=GRID_W)[:, :, BAND_LO[b]:BAND_LO[b] + BAND]
                        e.matmul(bank[:, 0:LOC], q, kb, start=True, stop=True)
                    e.matmul(bank[:, LOC:512], q, nk[o:o + DH, c, 0:CTX], start=True, stop=True).then_inc(sem("L.s_att"), 1)

                def turn(n):
                    e.wait_ge(sem("L.p_ready"), n + 1)
                    if n == 0:
                        e.wait_ge(sem("L.bands_placed"), 16 * BAND_DMAS)
                        e.wait_ge(sem("L.h_done"), MLH * (NT - t0))
                    if n >= 2:
                        e.wait_ge(sem("L.pT_ready"), n - 1)
                    for a in range(0 if att[n][0] < NBAND else 2, 4):
                        mm = e.transpose(ps[4 + n % 2][:, a * P:(a + 1) * P], prob[:, n % SCORE_SLOTS, a * P:(a + 1) * P], ident)
                    mm.then_inc(sem("L.pT_mm"), 1)

                def values(n):
                    b, h = att[n]
                    e.wait_ge(sem("L.pT_ready"), n + 1)
                    if n >= 2:
                        e.wait_ge(sem("L.o_att"), n - 1)
                    first = 0 if b < NBAND else 2
                    for a in range(first, 4):
                        vt = 2 * b + a if a < 2 else 2 * NBAND + a - 2
                        mm = e.matmul(ps[OUT_BANK[n % 2]][:, 0:P], vband[:, vt, (h // 2) * P:(h // 2 + 1) * P],
                                      probT[:, n % 2, a * P:(a + 1) * P], start=(a == first), stop=(a == 3))
                    mm.then_inc(sem("L.o_mm"), 1)

                def turn_mlstm(k):
                    e.wait_ge(sem("L.mlout"), k + 1)
                    if k >= 1:
                        e.wait_ge(sem("L.mlT_evac"), k)
                    for h in range(MLH):
                        mm = e.transpose(ps[7][:, h * P:(h + 1) * P], H[:, t0 + k, h * P:(h + 1) * P], ident)
                    mm.then_inc(sem("L.mlT"), 1)
                for n in range(len(att) + VALUES_LAG):
                    if n < len(att):
                        scores(n)
                    if TURN_LAG <= n < len(att) + TURN_LAG:
                        turn(n - TURN_LAG)
                    if n >= VALUES_LAG:
                        values(n - VALUES_LAG)
                    k = mlstm_tile_at(n, 4, NT - t0)
                    if k is not None:
                        turn_mlstm(k)
                meet(e, "pe")
                e.wait_ge(sem("L.wo_loaded"), 16)
                for t in range(t0, NT):
                    m = t - t0
                    if m >= 2:
                        e.wait_ge(sem("L.y_read"), m - 1)
                    for hf in range(2):
                        for k in range(KD):
                            mm = e.matmul(ps[2 * (m % 2) + hf][:], mixT[:, k, t * P:(t + 1) * P], wo[:, k, hf * 512:(hf + 1) * 512],
                                          start=(k == 0), stop=(k == KD - 1))
                    mm.then_inc(sem("L.y_ready"), 1)
                    for c in key_chunks(m, NT - t0):
                        if c == 0:
                            e.wait_ge(sem("L.keys_loaded"), 16)
                        e.wait_ge(sem(f"L.wq_loaded{c % len(wq_slots)}"), 16 * (c // len(wq_slots) + 1))
                        for j in range(2):
                            n = 2 * c + j
                            if n >= 4:
                                e.wait_ge(sem("L.wk_evac"), n - 3)
                            for k in range(4):
                                mm = e.matmul(ps[4 + n % 4][:, k * P:(k + 1) * P], wq_slots[c % len(wq_slots)][:, (4 * j + k) * P:(4 * j + k + 1) * P],
                                              keys[:, c, :], start=True, stop=True)
                            mm.then_inc(sem("L.wk_mm"), 1)
                meet(e, "pe")
                nt = NT - t0

                def turn_u(t):
                    e.wait_ge(sem("L.u_ready"), t + 1)
                    for k in range(KD):
                        mm = e.transpose(ps[4 + k // 4][:, (k % 4) * P:(k % 4 + 1) * P], u_next[:, k * P:(k + 1) * P], ident)
                    mm.then_inc(sem("L.uT_mm"), 1)

                def key_scores(unit, h, lead):
                    if lead < 2 or unit >= 1:
                        e.wait_ge(sem("L.route_read"), unit + 2 - lead)
                    bank = ps[2 + (unit % 2 if lead == 2 else 0)]
                    for k in range(KD):
                        mm = e.matmul(bank[:, 0:2 * NKEY], uTs[:, k, :], wk_flat[:, bass.ds(h * (2 * NKEY) + k * (2 * PH * NKEY), 2 * NKEY)],
                                      start=(k == 0), stop=(k == KD - 1))
                    mm.then_inc(sem("L.key_mm"), 1)

                def weigh(n, k):
                    e.wait_ge(sem("L.diag_ready"), n + (k + 1))
                    for hf in range(2):
                        mm = e.matmul(ps[hf][:], diag[:, k % 2, :], ring[:, k % RING, D + hf * 512:D + (hf + 1) * 512],
                                      start=False, stop=False, skip_group_check=True)
                    mm.then_inc(sem("L.slot_done"), 1)

                def tile(t, more):
                    e.wait_ge(sem("L.acc_free"), t + 1)
                    for hf in range(2):
                        e.matmul(ps[hf][:], zero, ln2r[:, 0, 0:512], start=True, stop=False, skip_group_check=True)
                    if more:
                        turn_u(t + 1)
                    with e.Fori(0, PH - LEAD) as h:
                        key_scores(t * PH + h + LEAD, h + LEAD, 1)
                        for k in range(TOPK):
                            weigh(t * (PH * TOPK) + h * TOPK, k)
                    if more:
                        e.wait_ge(sem("L.uT_ready"), t + 2)
                        e.sem_inc(sem("pe_token"), 1)
                    with e.Fori(0, LEAD) as h:
                        if more:
                            key_scores(t * PH + h + PH, h, 1)
                        for k in range(TOPK):
                            weigh(t * (PH * TOPK) + h * TOPK + (PH - LEAD) * TOPK, k)
                    for hf in range(2):
                        mm = e.matmul(ps[hf][:], zero, ln2r[:, 0, 0:512], start=False, stop=True, skip_group_check=True)
                    mm.then_inc(sem("L.acc_ready"), 1)

                turn_u(0)
                e.wait_ge(sem("L.uT_ready"), 1)
                for h in range(LEAD):
                    key_scores(h, h, 2)
                e.wait_ge(sem("L.row2_loaded"), 32)
                e.wait_ge(sem("L.zero_set"), 2)
                for ta, tb in tile_spans(l):
                    if tb - ta > 1:
                        with e.Fori(ta, tb) as t:
                            tile(t, True)
                    else:
                        tile(ta, tb < nt)
                if l < L - 1:
                    meet(e, "pe")
                    reset(e, "pe", "L.")

        @block.scalar
        def _(e):
            ch = Chain(e, sem("act_chain"))
            e.wait_ge(sem("c_loaded"), 16)
            e.activation(sT[:], sT[:], ACT.Silu).then_inc(sem("silu_c"), 1)
            meet(e, "act")
            for l in range(L):
                q_ctx = l < L - 1
                t0 = 0 if q_ctx else NCT
                jobs = proj_jobs(l)
                n_conv = [0]

                def silu(c):
                    e.wait_ge(sem("L.conv_done"), c + 1)
                    if c >= 2:
                        e.wait_ge(sem("L.rope_done"), c - 1)
                    if q_ctx or c >= 2:
                        e.activation(mlqk[:, c, 0:CTX], cvs[:, c % 2, 0:CTX], ACT.Silu).then_inc(sem("L.silu_ctx"), 1)
                    e.activation(ysil[:, c % 2, :], cvs[:, c % 2, 260:772], ACT.Silu).then_inc(sem("L.silu_done"), 1)

                done = 0
                for n, (kind, i, part, ev) in enumerate(jobs):
                    if ev != "a":
                        continue
                    bank = ps[n % 8]
                    width = SEQ if part == "x" else CTX
                    tc = slice(CTX, T) if part == "x" else slice(0, CTX)
                    if kind == "M" and part == "x" and i >= 2:
                        e.wait_ge(sem("L.conv_done"), i - 1)
                    if kind in "VO":
                        e.wait_ge(sem("L.rope_done"), 4)
                    e.wait_ge(sem("L.proj_mm"), n + 1)
                    if kind == "T":
                        cnd = 1 if part == "x" else 0
                        ins = e.activation(uT[:, i, tc], bank[:, 0:width], ACT.Identity, scale=modcol[:, l, SC1 * KD + i, cnd:cnd + 1],
                                           bias=modcol[:, l, SH1 * KD + i, cnd:cnd + 1])
                    elif kind == "G":
                        if i == 0 and part == "x":
                            e.wait_ge(sem("L.small_loaded"), 48)
                        ins = e.activation((li, lf)[i][:, tc], bank[0:8, 0:width], ACT.Identity, bias=bgs[0:8, i:i + 1])
                    elif kind == "M":
                        at = 262 if part == "x" else 2
                        ins = e.activation(raw[:, i % 2, at:at + width], bank[:, 0:width], ACT.Copy)
                    elif kind == "Q":
                        if part == "x":
                            ins = e.activation(nq[:, i, CTX:T].rearrange("p (b r c) -> p r b c", b=NBAND, r=ROWS),
                                               bank[:, :].rearrange("p (r b c) -> p r b c", r=ROWS, b=NBAND), ACT.Copy, scale=DH ** -0.5)
                        else:
                            ins = e.activation(nq[:, i, 0:CTX], bank[:, 0:CTX], ACT.Copy, scale=DH ** -0.5)
                    elif kind == "K":
                        ins = e.activation(nk[:, i, tc], bank[:, 0:width], ACT.Copy)
                    elif kind == "V":
                        ins = e.activation(vml[:, i, :, 0:DV], bank[:, :].rearrange("p (h d) -> p h d", h=MLH), ACT.Copy)
                    elif kind == "O":
                        ins = e.activation(sigo[:, i, :], bank[:], ACT.Sigmoid)
                    elif kind == "B":
                        ins = e.activation(vlat[:, i - NCT, :] if i >= NCT else vband[:, 2 * NBAND + i, :], bank[:], ACT.Copy)
                    ins.then_inc(sem("L.proj_evac_a"), 1)
                    done += 1
                    if kind == "G" and i == 1 and part == "c":
                        e.wait_ge(sem("L.proj_evac_a"), done)
                        ch.link(e.activation(lnl, lf, ACT.Abs))
                        ch.link(e.activation(lnl, lnl, ACT.Exp, scale=-1.0))
                        e.activation(lnl, lnl, ACT.Ln, bias=1.0).then_inc(sem("L.ln_done"), 1)
                        e.wait_ge(sem("L.negm_ready"), 2)
                        ch.link(e.activation(eF, eF, ACT.Exp, scale=-1.0))
                        e.activation(eB, eB, ACT.Exp, scale=-1.0).then_inc(sem("L.gates_done"), 1)
                    if kind == "M" and i >= 1 and (part == "c" or (not q_ctx and i < 2)):
                        silu(i - 1)
                        if i == 3:
                            silu(3)
                meet(e, "act")
                gc = gcol.rearrange("p (a t r) -> p a t r", a=4, t=NT)
                for h in range(MLH):
                    for i in range(NT):
                        m = h * NT + i
                        e.wait_ge(sem("L.arg_ready"), m + 1)
                        if i == 0:
                            e.wait_ge(sem(f"L.negm_loaded{h % 2}"), 32 * (h // 2 + 1))
                        if i >= t0:
                            e.activation(diagonal(h, i), diagonal(h, i), ACT.Exp)
                        nm, WD = negm[:, h % 2], WD2[h % 2]
                        gf, gb = gc[:, 0, i, h:h + 1], gc[:, 1, i, 4 + h:5 + h]
                        fs = max(i + 1, t0)
                        if fs < NT:
                            ins = e.activation(WD[:, 0, at_f(i, fs):at_f(i, fs) + (NT - fs) * P], nm[:, 0, fs * P:T], ACT.Exp, bias=gf)
                        n = SEQ if i < NCT else (i - NCT) * P
                        if n:
                            ins = e.activation(WD[:, 1, OFF_B[i]:OFF_B[i] + n], nm[:, 1, CTX:CTX + n], ACT.Exp, bias=gb)
                        if q_ctx and 0 < i < NCT:
                            ins = e.activation(WD[:, 1, OFF_B[i] + SEQ:OFF_B[i] + SEQ + i * P], nm[:, 1, 0:i * P], ACT.Exp, bias=gb)
                        ins.then_inc(sem("L.decay_ready"), 1)
                e.wait_ge(sem("L.h_done"), MLH * (NT - t0))
                e.wait_ge(sem("eps_set"), 1)
                e.activation(rstd[:, t0 * MLH:], stat[:, t0 * MLH:, 1], ACT.Sqrt, bias=epsc[:, 0:1]).then_inc(sem("L.hsd"), 1)
                att = attention_jobs(l)
                e.wait_ge(sem("L.bands_placed"), 16 * BAND_DMAS)
                for n in range(len(att) + TURN_LAG):
                    if n < len(att):
                        b, h = att[n]
                        a0 = 0 if b < NBAND else LOC
                        e.wait_ge(sem("L.nmax_ready"), n + 1)
                        if n >= SCORE_SLOTS:
                            e.wait_ge(sem("L.pT_mm"), n - SCORE_SLOTS + 1)
                        s = n % SCORE_SLOTS
                        e.activation(prob[:, s, a0:512], ps[s][:, a0:512], ACT.Exp, bias=nmax[:, s:s + 1],
                                     accum_out=rsum[:, s:s + 1]).then_inc(sem("L.p_exp"), 1)
                    if n >= TURN_LAG:
                        m = n - TURN_LAG
                        a0 = 0 if att[m][0] < NBAND else LOC
                        e.wait_ge(sem("L.pT_mm"), m + 1)
                        if m >= 2:
                            e.wait_ge(sem("L.o_mm"), m - 1)
                        e.activation(probT[:, m % 2, a0:512], ps[4 + m % 2][:, a0:512], ACT.Copy).then_inc(sem("L.pT_ready"), 1)
                    k = mlstm_tile_at(n, 5, NT - t0)
                    if k is not None:
                        t = t0 + k
                        e.wait_ge(sem("L.mlT"), k + 1)
                        e.activation(mixT[:, 0:MLH, t * P:(t + 1) * P], ps[7][:, :].rearrange("p (h t) -> p h t", h=MLH), ACT.Copy).then_inc(sem("L.mlT_evac"), 1)
                meet(e, "act")
                for t in range(t0, NT):
                    e.wait_ge(sem("L.var1"), t - t0 + 1)
                    e.activation(sd[:, 0:1], mv[:, 1:2], ACT.Sqrt, bias=epsc[:, 0:1]).then_inc(sem("L.sd1"), 1)
                    for c in key_chunks(t - t0, NT - t0):
                        for j in range(2):
                            n = 2 * c + j
                            e.wait_ge(sem("L.wk_mm"), n + 1)
                            e.activation(wk[:, 4 * j:4 * j + 4, c * NKEY:(c + 1) * NKEY], ps[4 + n % 4][:, :].rearrange("p (k n) -> p k n", k=4), ACT.Copy).then_inc(sem("L.wk_evac"), 1)
                meet(e, "act")
                nt = NT - t0

                def keep_uT(t):
                    e.wait_ge(sem("L.uT_mm"), t + 1)
                    e.sem_inc(sem("act_token"), 1)
                    e.wait_ge(sem("L.key_mm"), t * PH)
                    e.sem_inc(sem("act_token"), 1)
                    for j in range(2):
                        ins = e.activation(uTs[:, 4 * j:4 * j + 4, :], ps[4 + j][:, :].rearrange("p (k n) -> p k n", k=4), ACT.Copy)
                    ins.then_inc(sem("L.uT_ready"), 1)

                def gate_exp(un):
                    e.wait_ge(sem("L.route_done"), un + 1)
                    e.sem_inc(sem("act_token"), 1)
                    e.activation(gate_all[:, bass.ds(un * TOPK, TOPK)], gate_all[:, bass.ds(un * TOPK, TOPK)], ACT.Exp).then_inc(sem("L.gexp"), 1)

                def unit(un, route):
                    for k in range(TOPK):
                        e.wait_ge(sem("L.dot_done"), un * TOPK + (k + 1))
                        e.activation(acts[:, k:k + 1], dots[:, k:k + 1], ACT.Gelu_apprx_tanh).then_inc(sem("L.act_done"), 1)
                        if k == EXP_AT and route:
                            gate_exp(un + LEAD)

                def tile(t, more):
                    with e.Fori(0, PH - LEAD) as h:
                        unit(t * PH + h, True)
                    if more:
                        keep_uT(t + 1)
                    with e.Fori(0, LEAD) as h:
                        unit(t * PH + h + (PH - LEAD), more)
                    e.wait_ge(sem("L.var2"), t + 1)
                    e.activation(sd2[:, 0:1], mv2[:, 1:2], ACT.Sqrt, bias=epsc[:, 0:1]).then_inc(sem("L.sd2"), 1)

                e.wait_ge(sem("L.uT_mm"), 1)
                for j in range(2):
                    ins = e.activation(uTs[:, 4 * j:4 * j + 4, :], ps[4 + j][:, :].rearrange("p (k n) -> p k n", k=4), ACT.Copy)
                ins.then_inc(sem("L.uT_ready"), 1)
                for h in range(LEAD):
                    gate_exp(h)
                for ta, tb in tile_spans(l):
                    if tb - ta > 1:
                        with e.Fori(ta, tb) as t:
                            tile(t, True)
                    else:
                        tile(ta, tb < nt)
                if l < L - 1:
                    meet(e, "act")
                    reset(e, "act", "L.")

        @block.gpsimd
        def _(e):
            e.memset(epsc[:], EPS).then_inc(sem("eps_set"), 1)
            meet(e, "pool")
            for l in range(L):
                q_ctx = l < L - 1
                meet(e, "pool")
                e.wait_ge(sem("L.masks_loaded"), 16)
                for n in range(2 * NBAND):
                    e.wait_ge(sem(f"L.bias_loaded{n % 2}"), 16 * (n // 2 + 1))
                    for q in range(4):
                        ins = e.tensor_tensor(biasb[:, n % 2, q, :], biasb[:, n % 2, q, :], masks[:, n // 2, :], ALU.add)
                    ins.then_inc(sem("L.bias_ready"), 1)
                meet(e, "pool")
                meet(e, "pool")
                nt = NT - (0 if q_ctx else NCT)
                e.sem_inc(sem("L.slot_done"), RING)
                with e.Fori(0, nt * PH) as un:
                    for k in range(TOPK):
                        if k % RING == 0:
                            e.wait_ge(sem("L.idx_ready"), un * 2 + (k // RING + 1))
                            e.sem_inc(sem("pool_token"), 1)
                        e.wait_ge(sem("L.slot_done"), un * TOPK + (k + 1))
                        e.sem_inc(sem("pool_token"), 1)
                        e.indirect_dma_start(ring[:, k % RING, :], None, updown,
                                             bass.IndirectOffsetOnAxis(ap=idx16[:, k:k + 1], axis=0)).then_inc(sem(f"rows{k % RING}"), 16)
                if l < L - 1:
                    meet(e, "pool")
                    reset(e, "pool", "L.")

        @block.vector
        def _(e):
            ch = Chain(e, sem("dve_chain"))
            lc = Chain(e, sem("dve_loop_chain"), sem("dve_restarts"))
            e.wait_ge(sem("adab_loaded"), 16)
            for n in range(24):
                e.wait_ge(sem("mod_mm"), n + 1)
                one = 1.0 if (n % 12) // 2 in (SC1, SC2) else 0.0
                e.scalar_tensor_tensor(out=modrow[0:2, n * 512:(n + 1) * 512], in0=ps[n % 4][0:2, :], scalar=one,
                                       in1=adab[0:2, n * 512:(n + 1) * 512], op0=ALU.add, op1=ALU.add).then_inc(sem("mod_row"), 1)
            e.wait_ge(sem("modcol_t"), L)
            for l in range(L):
                e.tensor_copy(modcol[:, l].rearrange("p a b -> p (a b)"), ps[4 + l][:, 0:2 * N_MOD * KD])
            meet(e, "dve")
            for l in range(L):
                q_ctx = l < L - 1
                t0 = 0 if q_ctx else NCT
                jobs = proj_jobs(l)
                for a in range(2):
                    for c0, c1 in ((0, 2), (258, 262), (774, 776)):
                        ins = e.memset(raw[:, a, c0:c1], 0.0)
                ch.link(ins)
                evac_no = ordinals(jobs)

                def conv(c):
                    lo = 0 if (q_ctx or c >= 2) else 260
                    for part in "xc":
                        if ("M", c, part, "a") in jobs:
                            e.wait_ge(sem("L.proj_evac_a"), evac_no[jobs.index(("M", c, part, "a"))])
                    if c >= 2:
                        e.wait_ge(sem("L.silu_done"), c - 1)
                    cvb = cvs[:, c % 2, lo:772]
                    ch.link(e.tensor_scalar(cvb, raw[:, c % 2, lo:772], convs[:, c, 0:1], None, ALU.mult))
                    for w in range(1, 5):
                        ins = e.scalar_tensor_tensor(out=cvb, in0=raw[:, c % 2, lo + w:772 + w], scalar=convs[:, c, w:w + 1], in1=cvb, op0=ALU.mult, op1=ALU.add)
                        if w < 4:
                            ch.link(ins)
                    ins.then_inc(sem("L.conv_done"), 1)

                def gates():
                    e.wait_ge(sem("L.ln_done"), 1)
                    ch.link(e.scalar_tensor_tensor(out=lf, in0=lf, scalar=0.0, in1=lnl, op0=ALU.min, op1=ALU.subtract))
                    ch.link(e.memset(lnl, 1.0))
                    for g, F, nM, back in ((gF, eF, nMf, False), (gB, eB, nMb, True)):
                        parts = [(0, CTX), (CTX, T)] if back else [(0, T)]
                        for what, src, dst in (("sum", lf, F), ("max", g, cum)):
                            if what == "max":
                                ch.link(e.tensor_tensor(g, li, F, ALU.subtract))
                            start = 0.0
                            for a, b in parts:
                                v = [x[:, a:b][:, ::-1] if back else x[:, a:b] for x in (lnl if what == "sum" else src, src, dst)]
                                ops = (ALU.mult, ALU.add) if what == "sum" else (ALU.max, ALU.max)
                                ch.link(e.tensor_tensor_scan(v[2], v[0], v[1], start, *ops))
                                start = dst[:, a:a + 1] if back else None
                        ch.link(e.tensor_tensor(F, F, cum, ALU.add))
                        e.tensor_scalar(nM, cum, -1.0, None, ALU.mult).then_inc(sem("L.negm_ready"), 1)
                        e.wait_ge(sem("L.negm_ready"), 2 if back else 1)

                for n, (kind, i, part, ev) in enumerate(jobs):
                    if kind == "M" and part == "x" and i >= 1:
                        conv(i - 1)
                    if kind == "M" and part == "x" and i == 0:
                        gates()
                    if kind == "Q" and i == 0 and part == "x":
                        conv(3)
                    if ev != "v":
                        continue
                    bank = ps[n % 8]
                    width = SEQ if part == "x" else CTX
                    tc = slice(CTX, T) if part == "x" else slice(0, CTX)
                    if kind in "VB":
                        e.wait_ge(sem("L.rope_done"), 4)
                    e.wait_ge(sem("L.proj_mm"), n + 1)
                    if kind == "T":
                        ins = e.tensor_scalar(uT[:, i, tc], bank[:, 0:width], modcol[:, l, SC1 * KD + i, 1:2], modcol[:, l, SH1 * KD + i, 1:2], ALU.mult, ALU.add)
                    elif kind == "X":
                        ins = e.tensor_copy(gcol, bank[:, 0:4 * NT * 8])
                    elif kind == "R":
                        e.wait_ge(sem("L.silu_done"), i + 1)
                        if i == 0:
                            e.wait_ge(sem("L.rotary_loaded"), 32)
                        e.tensor_tensor(rt[:, 0, :], ysil[:, i % 2, :], cosr, ALU.mult)
                        ch.link(e.tensor_tensor(rt[:, 1, :], bank[:], sinr, ALU.mult))
                        ch.link(e.tensor_tensor(mlqk[:, i, CTX:T], rt[:, 0, :], rt[:, 1, :], ALU.add))
                        e.sem_inc(sem("L.rope_done"), 1)
                        e.sem_inc(sem("L.proj_evac_v"), 1)
                        continue
                    elif kind == "Q":
                        if part == "x":
                            ins = e.tensor_scalar(nq[:, i, CTX:T].rearrange("p (b r c) -> p r b c", b=NBAND, r=ROWS),
                                                  bank[:, :].rearrange("p (r b c) -> p r b c", r=ROWS, b=NBAND), DH ** -0.5, None, ALU.mult)
                        else:
                            ins = e.tensor_scalar(nq[:, i, 0:CTX], bank[:, 0:CTX], DH ** -0.5, None, ALU.mult)
                    elif kind == "K":
                        ins = e.tensor_copy(nk[:, i, tc], bank[:, 0:width])
                    elif kind == "V":
                        ins = e.tensor_copy(vml[:, i, :, 0:DV], bank[:, :].rearrange("p (h d) -> p h d", h=MLH))
                    else:
                        ins = e.tensor_copy(vlat[:, i - NCT, :] if i >= NCT else vband[:, 2 * NBAND + i, :], bank[:])
                    ins.then_inc(sem("L.proj_evac_v"), 1)
                e.memset(vml[:, :, :, DV:DV + 1].rearrange("p a b c -> p (a b) c"), 1.0)
                meet(e, "dve")
                def args(h, i):
                    nm, WD = negm[:, h % 2], WD2[h % 2]
                    if i >= t0:
                        e.tensor_scalar(WD[:, 0, at_f(i, i):at_f(i, i) + P], nm[:, 0, i * P:(i + 1) * P], gc[:, 0, i, h:h + 1], 0.0, ALU.add, ALU.min)
                        e.tensor_scalar(WD[:, 1, at_b(i, i):at_b(i, i) + P], nm[:, 1, i * P:(i + 1) * P], gc[:, 1, i, 4 + h:5 + h], 0.0,
                                        ALU.add, ALU.min).then_inc(sem("L.arg_ready"), 1)
                    else:
                        e.sem_inc(sem("L.arg_ready"), 1)

                def apply(h, i):
                    m, WD = h * NT + i, WD2[h % 2]
                    e.wait_ge(sem("L.decay_ready"), m + 1)
                    e.wait_ge(sem("L.s_ready"), m + 1)
                    if i >= t0:
                        both = diagonal(h, i)
                        ch.link(e.tensor_tensor(both, both, CN[:, C_TRI:C_TRI + 2 * P].rearrange("p (d n) -> p d n", d=2), ALU.mult))
                    SX, SC = ps[m % 2], ps[2 + m % 2]
                    work = []
                    xs = max(i, NCT)
                    work.append((0, at_f(i, xs), SX, (xs - NCT) * P, (NT - xs) * P))
                    work.append((1, OFF_B[i], SX, 0, SEQ if i < NCT else (i - 1) * P))
                    if i < NCT and q_ctx:
                        work.append((0, at_f(i, i), SC, i * P, (NCT - i) * P))
                        work.append((1, OFF_B[i] + SEQ, SC, 0, (i + 1) * P))
                    for d, wa, S, sa, n in work:
                        ins = e.scalar_tensor_tensor(out=WD[:, d, wa:wa + n], in0=S[:, sa:sa + n], scalar=DK ** -0.5, in1=WD[:, d, wa:wa + n], op0=ALU.mult, op1=ALU.mult)
                    ins.then_inc(sem("L.w_ready"), 1)

                gc = gcol.rearrange("p (a t r) -> p a t r", a=4, t=NT)
                def head_rows(h, j):
                    m = h * (NT - t0) + j - t0
                    bank = ps[4 + m % 2]
                    e.wait_ge(sem("L.num_ready"), m + 1)
                    o = (2 * NT + j) * 8 + h
                    dn = bank[:, DV:2 * DV + 2:DV + 1]
                    ch.link(e.scalar_tensor_tensor(out=den[:, 1, :], in0=dn, scalar=-1.0, in1=gcol[:, o:o + NT * 8 + 5:NT * 8 + 4], op0=ALU.mult, op1=ALU.max))
                    ch.link(e.tensor_tensor(den[:, 0, :], dn, den[:, 1, :], ALU.max))
                    ch.link(e.reciprocal(rden[:, 0, :], den[:, 0, :]))
                    Hj = H[:, j, h * DV:(h + 1) * DV]
                    ch.link(e.tensor_scalar(Hj, bank[:, 0:DV], rden[:, 0, 0:1], None, ALU.mult))
                    ch.link(e.scalar_tensor_tensor(out=Hj, in0=bank[:, DV + 1:2 * DV + 1], scalar=rden[:, 0, 1:2], in1=Hj, op0=ALU.mult, op1=ALU.add))
                    ch.link(e.bn_stats(bns[:, 0, :], Hj))
                    e.bn_aggr(stat[:, j * MLH + h, :], bns[:, 0, :]).then_inc(sem("L.h_done"), 1)

                for h in range(MLH + 1):
                    if h < MLH:
                        e.wait_ge(sem(f"L.negm_loaded{h % 2}"), 32 * (h // 2 + 1))
                        if h >= 2:
                            e.wait_ge(sem("L.num_ready"), (h - 1) * (NT - t0))
                        args(h, 0)
                    for x in range(NT):
                        if h < MLH:
                            if x + 1 < NT:
                                args(h, x + 1)
                            apply(h, x)
                        if h >= 1 and t0 + x < NT:
                            head_rows(h - 1, t0 + x)

                def head_norm(t):
                    if t == t0:
                        e.wait_ge(sem("L.hsd"), 1)
                        e.wait_ge(sem("L.nw_loaded"), 16)
                        ch.link(e.reciprocal(rstd[:, t0 * MLH:], rstd[:, t0 * MLH:]))
                    for h in range(MLH):
                        n = t * MLH + h
                        ins = e.tensor_scalar(H[:, t, h * DV:(h + 1) * DV], H[:, t, h * DV:(h + 1) * DV], stat[:, n, 0:1], rstd[:, n:n + 1], ALU.subtract, ALU.mult)
                    ch.link(ins)
                    ch.link(e.tensor_tensor(H[:, t, :], H[:, t, :], nwrow, ALU.mult))
                    e.tensor_tensor(H[:, t, :], H[:, t, :], sigo[:, t, :], ALU.mult).then_inc(sem("L.mlout"), 1)
                att = attention_jobs(l)
                e.wait_ge(sem("L.bands_placed"), 16 * BAND_DMAS)
                for n in range(len(att) + KEEP_LAG):
                    s = n % SCORE_SLOTS
                    if n < len(att):
                        b, h = att[n]
                        a0 = 0 if b < NBAND else LOC
                        e.wait_ge(sem("L.s_att"), n + 1)
                        if n >= SCORE_SLOTS:
                            e.wait_ge(sem("L.p_exp"), n - SCORE_SLOTS + 1)
                        if b < NBAND:
                            half = 2 * b + h // 4
                            e.wait_ge(sem("L.bias_ready"), half + 1)
                            e.tensor_tensor(ps[s][:, 0:LOC], ps[s][:, 0:LOC], biasb[:, half % 2, h % 4, :], ALU.add).then_inc(sem("L.bias_used"), 1)
                            e.wait_ge(sem("L.bias_used"), n + 1)
                        e.tensor_reduce(nmax[:, s:s + 1], ps[s][:, a0:512], AX.X, ALU.max, negate=True).then_inc(sem("L.nmax_ready"), 1)
                    if 1 <= n <= len(att):
                        m = n - 1
                        a0 = 0 if att[m][0] < NBAND else LOC
                        e.wait_ge(sem("L.p_exp"), m + 1)
                        s = m % SCORE_SLOTS
                        ch.link(e.reciprocal(rinv[:, s:s + 1], rsum[:, s:s + 1]))
                        e.tensor_scalar(prob[:, s, a0:512], prob[:, s, a0:512], rinv[:, s:s + 1], None, ALU.mult).then_inc(sem("L.p_ready"), 1)
                    k = mlstm_tile_at(n, 2, NT - t0)
                    if k is not None:
                        head_norm(t0 + k)
                    if n >= KEEP_LAG:
                        m = n - KEEP_LAG
                        b, h = att[m]
                        o = (h % 2) * DH
                        e.wait_ge(sem("L.o_mm"), m + 1)
                        src = ps[OUT_BANK[m % 2]][o:o + DH, 0:P]
                        if b < NBAND:
                            dst = mixT[o:o + DH, 4 + h // 2, CTX:T].rearrange("p (r w) -> p r w", w=GRID_W)[:, :, b * QB:(b + 1) * QB]
                            src = src.rearrange("p (r c) -> p r c", r=ROWS)
                        else:
                            dst = mixT[o:o + DH, 4 + h // 2, (b - NBAND) * P:(b - NBAND + 1) * P]
                        e.tensor_copy(dst, src).then_inc(sem("L.o_att"), 1)
                meet(e, "dve")

                e.wait_ge(sem("L.row1_loaded"), 48 if q_ctx else 32)
                for t in range(t0, NT):
                    m = t - t0
                    w = tmp[:, m % 2, :]
                    e.wait_ge(sem("L.y_ready"), m + 1)
                    for hf in range(2):
                        c = slice(hf * 512, (hf + 1) * 512)
                        ins = e.tensor_tensor(w[:, c], ps[2 * (m % 2) + hf][:], g1r[:, cond_of[t], c], ALU.mult)
                    ins.then_inc(sem("L.y_read"), 1)
                    e.wait_ge(sem("L.y_read"), m + 1)
                    ch.link(e.scalar_tensor_tensor(out=w, in0=X[:, t, :], scalar=ALPHA, in1=w, op0=ALU.mult, op1=ALU.add))
                    e.bn_stats(lns[:, 0, :], w[:, 0:512])
                    ch.link(e.bn_stats(lns[:, 1, :], w[:, 512:D]))
                    e.bn_aggr(mv, lns.rearrange("p a b -> p (a b)")).then_inc(sem("L.var1"), 1)
                    e.wait_ge(sem("L.var1"), m + 1)
                    e.wait_ge(sem("L.sd1"), m + 1)
                    ch.link(e.reciprocal(sd[:, 1:2], sd[:, 0:1]))
                    ch.link(e.tensor_scalar(w, w, mv[:, 0:1], sd[:, 1:2], ALU.subtract, ALU.mult))
                    ch.link(e.tensor_tensor(w, w, ln1r[:, 0, :], ALU.mult))
                    ch.link(e.tensor_tensor(X[:, t, :], w, ln1r[:, 1, :], ALU.add))
                meet(e, "dve")

                if True:
                    nt = NT - t0
                    u_before = 0 if l == 0 else PH * NT
                    UN = TOPK

                    def route(un, bank=2):
                        e.wait_ge(sem("L.key_mm"), un + 1)
                        e.sem_inc(sem("L.dve_token"), 1)
                        S = [ps[bank][:, hf * NKEY:(hf + 1) * NKEY] for hf in range(2)]
                        e.max(tv[:, 0, 0:8], S[0])
                        yield
                        lc.link(e.max(tv[:, 1, 0:8], S[1]))
                        yield
                        for hf in range(2):
                            e.max_index(ti[:, hf, 0:8], tv[:, hf, 0:8], S[hf])
                            yield
                        e.match_replace(sc[:, 0, :], tv[:, 0, 0:8], S[0], LOWEST)
                        yield
                        e.match_replace(sc[:, 1, :], tv[:, 1, 0:8], S[1], LOWEST).then_inc(sem("L.route_read"), 1)
                        e.wait_ge(sem("L.route_read"), un + 2)
                        e.sem_inc(sem("L.dve_token"), 1)
                        yield
                        e.max(tv[:, 0, 8:16], sc[:, 0, :])
                        yield
                        lc.link(e.max(tv[:, 1, 8:16], sc[:, 1, :]))
                        yield
                        for hf in range(2):
                            e.max_index(ti[:, hf, 8:16], tv[:, hf, 8:16], sc[:, hf, :])
                            yield
                        lc.link(e.tensor_tensor(cand.rearrange("p (a b) -> p a b", a=TOPK), tv[:, 0, :].unsqueeze(2).to_broadcast([P, TOPK, TOPK]),
                                                tv[:, 1, :].unsqueeze(1).to_broadcast([P, TOPK, TOPK]), ALU.add))
                        yield
                        lc.link(e.max(tt[:, 0:8], cand))
                        yield
                        e.max_index(pos[:, 0:8], tt[:, 0:8], cand)
                        yield
                        lc.link(e.match_replace(cand2, tt[:, 0:8], cand, LOWEST))
                        yield
                        lc.link(e.max(tt[:, 8:16], cand2))
                        yield
                        lc.link(e.max_index(pos[:, 8:16], tt[:, 8:16], cand2))
                        yield
                        e.tensor_scalar(hilo[:, 0, :], pos, 4, None, ALU.logical_shift_right)
                        lc.link(e.tensor_scalar(hilo[:, 1, :], pos, 15, None, ALU.bitwise_and))
                        yield
                        for hf in range(2):
                            o3 = oh.rearrange("p (k a) -> p k a", k=TOPK)
                            lc.link(e.tensor_tensor(o3, hilo[:, hf, :].unsqueeze(2).to_broadcast([P, TOPK, TOPK]),
                                                    iota.unsqueeze(1).to_broadcast([P, TOPK, TOPK]), ALU.is_equal))
                            yield
                            lc.link(e.tensor_tensor(o3, o3, ti[:, hf, :].unsqueeze(1).to_broadcast([P, TOPK, TOPK]), ALU.mult))
                            yield
                            lc.link(e.tensor_reduce(e1[:, hf, :], o3, AX.X, ALU.add))
                            yield
                        lc.link(e.tensor_scalar(e1[:, 0, :], e1[:, 0, :], float(NKEY), float(l * NEXP), ALU.mult, ALU.add))
                        yield
                        e.tensor_tensor(eidx_all[:, bass.ds(un * UN, UN)], e1[:, 0, :], e1[:, 1, :], ALU.add)
                        e.tensor_scalar(gate_all[:, bass.ds(un * UN, UN)], tt, tt[:, 0:1], None, ALU.subtract).then_inc(sem("L.route_done"), 1)
                        e.wait_ge(sem("L.route_done"), un + 1)
                        yield

                    def stage_index(un, half):
                        e.tensor_copy(idx16[:, 8 * half:8 * half + 8], eidx_all[:, bass.ds(un * UN + 8 * half, 8)]).then_inc(sem("L.idx_ready"), 1)

                    def gate_norm(un):
                        e.wait_ge(sem("L.gexp"), un + 1)
                        e.sem_inc(sem("dve_token"), 1)
                        g = gate_all[:, bass.ds(un * TOPK, TOPK)]
                        lc.link(e.tensor_reduce(gsum[:, 0:1], g, AX.X, ALU.add))
                        lc.link(e.reciprocal(gsum[:, 1:2], gsum[:, 0:1]))
                        lc.link(e.tensor_scalar(g, g, gsum[:, 1:2], None, ALU.mult))

                    def make_diag(un, k):
                        e.wait_ge(sem("L.act_done"), un * UN + (k + 1))
                        e.wait_ge(sem("L.slot_done"), un * UN + (k - 1 + RING))
                        e.tensor_scalar(diag[:, k % 2, :], ident, acts[:, k:k + 1], gate_all[:, bass.ds(un * UN + k, 1)], ALU.mult, ALU.mult).then_inc(sem("L.diag_ready"), 1)

                    def unit(un, route_next):
                        lc.restart()
                        steps = route(un + LEAD) if route_next else iter(())
                        for k in range(TOPK):
                            e.wait_ge(sem(f"rows{k % RING}"), un * 32 + (32 * u_before + 16 * (k // RING + 1)))
                            e.tensor_tensor_reduce(prod[:, k % 2, :], ring[:, k % RING, 0:D], u, 1.0, 0.0, ALU.mult, ALU.add, dots[:, k:k + 1]).then_inc(sem("L.dot_done"), 1)
                            if k >= 1:
                                make_diag(un, k - 1)
                            if k % RING == RING - 1:
                                stage_index(un + 1, k // RING)
                            for _ in range(3):
                                next(steps, None)
                            if k == EXP_AT:
                                assert next(steps, None) is None
                            if k == NORM_AT and route_next:
                                gate_norm(un + LEAD)
                        make_diag(un, TOPK - 1)

                    def modulate(t):
                        e.wait_ge(sem("L.uT_mm"), t)
                        e.sem_inc(sem("dve_token"), 1)
                        lc.link(e.tensor_tensor(u_next, X[:, bass.ds(t + t0, 1), :].rearrange("p a d -> p (a d)"), sc2r, ALU.mult))
                        e.tensor_tensor(u_next, u_next, sh2r, ALU.add).then_inc(sem("L.u_ready"), 1)

                    def tile(t, more, static_first, late):
                        xt = X[:, bass.ds(t + t0, 1), :]
                        lc.restart()
                        lc.link(e.tensor_copy(u, u_next))
                        if more:
                            if l < L - 1 and not static_first:
                                e.wait_ge(sem("L.u_rows_changed"), 32)
                            modulate(t + 1)
                        with e.Fori(0, PH - LEAD) as h:
                            unit(t * PH + h, True)
                        with e.Fori(0, LEAD) as h:
                            unit(t * PH + h + (PH - LEAD), more)
                        if l < L - 1 and late:
                            e.wait_ge(sem("L.g_row_changed"), 16)
                        e.wait_ge(sem("L.acc_ready"), t + 1)
                        lc.restart()
                        for hf in range(2):
                            c = slice(hf * 512, (hf + 1) * 512)
                            ins = e.tensor_tensor(junk[:, c], ps[hf][:], g2r[:, c], ALU.mult)
                        ins.then_inc(sem("L.acc_free"), 1)
                        e.wait_ge(sem("L.acc_free"), t + 2)
                        lc.link(e.scalar_tensor_tensor(out=junk, in0=xt.rearrange("p a d -> p (a d)"), scalar=ALPHA, in1=junk, op0=ALU.mult, op1=ALU.add))
                        e.bn_stats(lns2[:, 0, :], junk[:, 0:512])
                        lc.link(e.bn_stats(lns2[:, 1, :], junk[:, 512:D]))
                        e.bn_aggr(mv2, lns2.rearrange("p a b -> p (a b)")).then_inc(sem("L.var2"), 1)
                        e.wait_ge(sem("L.sd2"), t + 1)
                        lc.link(e.reciprocal(sd2[:, 1:2], sd2[:, 0:1]))
                        lc.link(e.tensor_scalar(junk, junk, mv2[:, 0:1], sd2[:, 1:2], ALU.subtract, ALU.mult))
                        lc.link(e.tensor_tensor(junk, junk, ln2r[:, 0, :], ALU.mult))
                        lc.link(e.tensor_tensor(xt.rearrange("p a d -> p (a d)"), junk, ln2r[:, 1, :], ALU.add))
                        e.sem_inc(sem("L.tile_done"), 1)

                    e.memset(zero, 0.0).then_inc(sem("L.zero_set"), 1)
                    e.memset(eidx_all[:, nt * PH * UN:nt * PH * UN + UN], 0).then_inc(sem("L.zero_set"), 1)
                    e.sem_inc(sem("L.route_read"), 1)
                    e.sem_inc(sem("L.acc_free"), 1)
                    e.wait_ge(sem("L.u_rows_loaded"), 32)
                    lc.restart()
                    lc.link(e.tensor_tensor(u_next, X[:, t0, :], sc2r, ALU.mult))
                    e.tensor_tensor(u_next, u_next, sh2r, ALU.add).then_inc(sem("L.u_ready"), 1)
                    e.wait_ge(sem("L.u_ready"), 1)
                    for h in range(LEAD):
                        lc.restart()
                        for _ in route(h, 2 + h % 2):
                            pass
                        if h == 0:
                            stage_index(0, 0)
                            stage_index(0, 1)
                    for h in range(LEAD):
                        gate_norm(h)
                    e.wait_ge(sem("L.row2_loaded"), 32)
                    for ta, tb in tile_spans(l):
                        if tb - ta > 1:
                            with e.Fori(ta, tb) as t:
                                tile(t, True, False, ta >= NCT)
                        else:
                            tile(ta, tb < nt, ta == 0, ta >= NCT)
                    if l < L - 1:
                        meet(e, "dve")
                        reset(e, "dve", "L.", ch)


def kernel(**inputs):
    import numpy as _np
    import concourse.bacc as _bacc
    from concourse import mybir as _mybir
    from concourse.bass_utils import run_bass_kernel_spmd as _run

    nc = _bacc.Bacc("TRN2", target_bir_lowering=False, num_devices=1)
    arrays = {}

    def inp(name, a):
        a = _np.ascontiguousarray(a)
        arrays[f"in_{name}"] = a
        return nc.dram_tensor(f"in_{name}", a.shape, _mybir.dt.from_np(a.dtype), kind="ExternalInput").ap()

    i = {k: _np.asarray(v) for k, v in inputs.items()}
    li_cols = [0, 1, 2, 3, 8, 9, 10, 11]
    lf_cols = [4, 5, 6, 7, 12, 13, 14, 15]
    gates = i["w_in"][:, :, COL_G:COL_G + 16][:, :, li_cols + lf_cols]
    q = _np.arange(P)
    k = _np.arange(LOC)
    row = k[None] // BAND - q[:, None] // QB + ROWS - 1
    spread = []
    for b in range(NBAND):
        col = BAND_LO[b] + k[None] % BAND - (b * QB + q[:, None] % QB)
        col = _np.clip(col, 1 - WIN, WIN - 1) + WIN - 1
        spread.append(i["na_rpb"][:, :, row, col].transpose(0, 2, 1, 3))
    args = [
        inp("x", _np.concatenate([i["ctx"][0], i["x"][0]], 0)),
        inp("c", _np.stack([i["c_ctx"], i["c"][0]]).reshape(2, KD, P).transpose(2, 1, 0)),
        inp("consts", shape_constants()),
        inp("ada_w", i["ada_w"]), inp("ada_b", i["ada_b"]), inp("w_in", i["w_in"]),
        inp("wg", gates.reshape(L, KD, P, 16).transpose(0, 2, 1, 3)),
        inp("bg", _np.stack([i["b_gate"][:, li_cols], i["b_gate"][:, lf_cols]], -1)),
        inp("conv_w", i["conv_w"].reshape(L, 5, 4, P).transpose(0, 3, 2, 1)),
        inp("ml_norm_w", i["ml_norm_w"]),
        inp("bias", _np.stack(spread, 1)),
        inp("w_out", i["w_out"]),
        inp("ln1", _np.concatenate([i["ln1_w"], i["ln1_b"]], -1)),
        inp("wq", i["peer_wq"].transpose(0, 2, 1)),
        inp("keys", i["peer_keys"].reshape(L, 2 * PH, NKEY, P).transpose(0, 3, 1, 2)),
        inp("updown", _np.concatenate([i["peer_up"].reshape(L * NEXP, D), i["peer_down"].reshape(L * NEXP, D)], -1)),
        inp("ln2", _np.concatenate([i["ln2_w"], i["ln2_b"]], -1)),
        nc.dram_tensor("mod_rows", (L, 2, N_MOD * D), _mybir.dt.float32).ap(),
        nc.dram_tensor("negm_rows", (L, 2, MLH, T), _mybir.dt.float32).ap(),
        nc.dram_tensor("out_0", (1, SEQ, D), _mybir.dt.float32, kind="ExternalOutput").ap(),
    ]
    build(nc, *args)
    r = _run(nc, [arrays], core_ids=[0])
    return r.results[0]["out_0"]
```
